# Optimizing a Trainium2 kernel written in Bass

```python
import math
import jax, jax.numpy as jnp
from jax import lax
import numpy as np

D_MODEL = 1024
BATCH = 1
SEQ = 256
DEPTH = 2

N_META = 16
CHUNK = 64
PAD = CHUNK - N_META
GLA_HEADS = 4
GLA_DK = 128
GLA_DV = 256
GLA_RANK = 16
GLA_TAU = 16.0
RET_HEADS = 4
RET_DK = 128
RET_DV = 256
ROPE_BASE = 10000.0
D_FF = 2816
N_EXPERTS = 8
TOP_K = 2
D_FF_EXPERT = 3584
ALPHA = (2 * DEPTH) ** 0.25
BETA = (8 * DEPTH) ** -0.25
LN_EPS = 1e-5
GN_EPS = 1e-6
N_DENSE = (DEPTH + 1) // 2
N_MOE = DEPTH // 2

GLA_QK = GLA_HEADS * GLA_DK
GLA_V = GLA_HEADS * GLA_DV
RET_QK = RET_HEADS * RET_DK
RET_V = RET_HEADS * RET_DV
IN_SIZES = (GLA_QK, GLA_QK, GLA_V, GLA_V, GLA_RANK,
            RET_QK, RET_QK, RET_V, RET_V,
            D_MODEL, D_MODEL)
N_IN = sum(IN_SIZES)

kernel_name = "hybrid_gla_retention_deepnorm_moe"

def layer_norm(x, g, b):
    xf = x.astype(jnp.float32)
    mu = jnp.mean(xf, axis=-1, keepdims=True)
    var = jnp.mean(jnp.square(xf - mu), axis=-1, keepdims=True)
    y = (xf - mu) * lax.rsqrt(var + LN_EPS) * g.astype(jnp.float32) + b.astype(jnp.float32)
    return y.astype(x.dtype)

def rotary(t, pos):
    half = t.shape[-1] // 2
    inv = ROPE_BASE ** (-jnp.arange(half, dtype=jnp.float32) / half)
    ang = pos[:, None] * inv[None, :]
    cos = jnp.cos(ang)[None, :, None, :]
    sin = jnp.sin(ang)[None, :, None, :]
    t1, t2 = t[..., :half], t[..., half:]
    return jnp.concatenate([t1 * cos - t2 * sin, t1 * sin + t2 * cos], axis=-1)

def to_chunks(t, n_heads):
    bsz, length, width = t.shape
    t = jnp.pad(t.astype(jnp.float32), ((0, 0), (PAD, 0), (0, 0)))
    n = (length + PAD) // CHUNK
    return t.reshape(bsz, n, CHUNK, n_heads, width // n_heads).transpose(0, 3, 1, 2, 4)

def from_chunks(o):
    bsz, h, n, c, d = o.shape
    return o.transpose(0, 2, 3, 1, 4).reshape(bsz, n * c, h, d)[:, PAD:]

def chunk_recurrence(q_in, k_tail, v, decay):
    bsz, h, n, c, dk = q_in.shape
    dv = v.shape[-1]

    def step(s, inp):
        qc, kc, vc, dc = inp
        o = jnp.einsum('bhcd,bhdv->bhcv', qc, s)
        s = s * dc[..., None] + jnp.einsum('bhcd,bhcv->bhdv', kc, vc)
        return s, o

    xs = (jnp.moveaxis(q_in, 2, 0), jnp.moveaxis(k_tail, 2, 0),
          jnp.moveaxis(v, 2, 0), jnp.moveaxis(decay, 2, 0))
    s0 = jnp.zeros((bsz, h, dk, dv), jnp.float32)
    _, o = lax.scan(step, s0, xs)
    return jnp.moveaxis(o, 0, 2)

def gla_chunked(q, k, v, log_a):
    b = jnp.cumsum(log_a, axis=3)
    b_last = b[..., -1:, :]
    q_in = q * jnp.exp(b)
    k_in = k * jnp.exp(-b)
    causal = jnp.tril(jnp.ones((CHUNK, CHUNK), dtype=bool))
    scores = jnp.where(causal, jnp.einsum('bhnid,bhnjd->bhnij', q_in, k_in), 0.0)
    o_intra = jnp.einsum('bhnij,bhnjv->bhniv', scores, v)
    k_tail = k * jnp.exp(b_last - b)
    decay = jnp.exp(b_last[..., 0, :])
    return o_intra + chunk_recurrence(q_in, k_tail, v, decay)

def retention_chunked(q, k, v, log_gamma):
    idx = jnp.arange(CHUNK, dtype=jnp.float32)
    rel = idx[:, None] - idx[None, :]
    lg = log_gamma[:, None, None]
    dmat = jnp.where(rel >= 0, jnp.exp(lg * jnp.maximum(rel, 0.0)), 0.0)
    scores = jnp.einsum('bhnid,bhnjd->bhnij', q, k) * dmat[None, :, None]
    o_intra = jnp.einsum('bhnij,bhnjv->bhniv', scores, v)
    xi = jnp.exp(log_gamma[:, None] * (idx + 1.0))[None, :, None, :, None]
    zeta = jnp.exp(log_gamma[:, None] * (CHUNK - 1.0 - idx))[None, :, None, :, None]
    bsz, h, n, _, dk = q.shape
    decay = jnp.broadcast_to(jnp.exp(log_gamma * CHUNK)[None, :, None, None], (bsz, h, n, dk))
    return o_intra + chunk_recurrence(q * xi, k * zeta, v, decay)

def token_mixer(x, w_in, b_gate, gla_w_a2, gla_b_a, gla_norm_g, ret_norm_g, ret_norm_b,
                w_pa, w_pb, w_o):
    bsz, length, _ = x.shape
    proj = x @ w_in
    split_at = np.cumsum(np.array(IN_SIZES))[:-1].tolist()
    gq, gk, gv, gr, ga, rq, rk, rv, rg, gate_a, gate_b = jnp.split(proj, split_at, axis=-1)

    log_a = jax.nn.log_sigmoid((ga @ gla_w_a2 + gla_b_a).astype(jnp.float32)) / GLA_TAU
    o_a = gla_chunked(to_chunks(gq * GLA_DK ** -0.5, GLA_HEADS), to_chunks(gk, GLA_HEADS),
                      to_chunks(gv, GLA_HEADS), to_chunks(log_a, GLA_HEADS))
    o_a = from_chunks(o_a)
    o_a = o_a * lax.rsqrt(jnp.mean(jnp.square(o_a), axis=-1, keepdims=True) + LN_EPS) \
        * gla_norm_g.astype(jnp.float32)
    y_a = (jax.nn.silu(gr.astype(jnp.float32)) * o_a.reshape(bsz, length, GLA_V)) @ w_pa

    pos = jnp.arange(length, dtype=jnp.float32)
    rq_r = rotary(rq.astype(jnp.float32).reshape(bsz, length, RET_HEADS, RET_DK), pos)
    rk_r = rotary(rk.astype(jnp.float32).reshape(bsz, length, RET_HEADS, RET_DK), pos) * RET_DK ** -0.5
    log_gamma = jnp.log(1.0 - 2.0 ** (-5.0 - jnp.arange(RET_HEADS, dtype=jnp.float32)))
    o_b = retention_chunked(to_chunks(rq_r.reshape(bsz, length, RET_QK), RET_HEADS),
                            to_chunks(rk_r.reshape(bsz, length, RET_QK), RET_HEADS),
                            to_chunks(rv, RET_HEADS), log_gamma)
    o_b = from_chunks(o_b)
    mu = jnp.mean(o_b, axis=-1, keepdims=True)
    var = jnp.mean(jnp.square(o_b - mu), axis=-1, keepdims=True)
    o_b = ((o_b - mu) * lax.rsqrt(var + GN_EPS)).reshape(bsz, length, RET_V) \
        * ret_norm_g.astype(jnp.float32) + ret_norm_b.astype(jnp.float32)
    y_b = (jax.nn.silu(rg.astype(jnp.float32)) * o_b) @ w_pb

    merged = jax.nn.sigmoid((gate_a + b_gate[0]).astype(jnp.float32)) * y_a \
        + jax.nn.sigmoid((gate_b + b_gate[1]).astype(jnp.float32)) * y_b
    return (merged @ w_o).astype(x.dtype)

def swiglu(x, w_gate, w_up, w_down):
    return (jax.nn.silu(x @ w_gate) * (x @ w_up)) @ w_down

def moe_swiglu(x, w_router, w_gate, w_up, w_down):
    bsz, length, d = x.shape
    t = x.reshape(-1, d)
    probs = jax.nn.softmax((t @ w_router).astype(jnp.float32), axis=-1)
    top_p, top_i = lax.top_k(probs, TOP_K)
    top_p = top_p / jnp.sum(top_p, axis=-1, keepdims=True)
    combine = jnp.sum(jax.nn.one_hot(top_i, N_EXPERTS, dtype=jnp.float32) * top_p[..., None], axis=1)
    out = jnp.zeros(t.shape, jnp.float32)
    for e in range(N_EXPERTS):
        out = out + combine[:, e:e + 1] * swiglu(t, w_gate[e], w_up[e], w_down[e]).astype(jnp.float32)
    return out.reshape(bsz, length, d).astype(x.dtype)

def setup_inputs(seed: int = 0) -> dict:
    key = jax.random.key(seed)
    ks = jax.random.split(key, 24)
    f32 = jnp.float32
    nrm = lambda k, shape, scale: jax.random.normal(k, shape, f32) * scale
    d = D_MODEL
    return {
        "x": nrm(ks[0], (BATCH, SEQ, d), 1.0),
        "meta": nrm(ks[1], (N_META, d), 1.0),
        "w_in": nrm(ks[2], (DEPTH, d, N_IN), d ** -0.5),
        "b_gate": nrm(ks[3], (DEPTH, 2, d), 0.01),
        "gla_w_a2": nrm(ks[4], (DEPTH, GLA_RANK, GLA_QK), GLA_RANK ** -0.5),
        "gla_b_a": nrm(ks[5], (DEPTH, GLA_QK), 0.01),
        "gla_norm_g": 1.0 + nrm(ks[6], (DEPTH, GLA_DV), 0.02),
        "ret_norm_g": 1.0 + nrm(ks[7], (DEPTH, RET_V), 0.02),
        "ret_norm_b": nrm(ks[8], (DEPTH, RET_V), 0.01),
        "w_pa": nrm(ks[9], (DEPTH, GLA_V, d), GLA_V ** -0.5),
        "w_pb": nrm(ks[10], (DEPTH, RET_V, d), RET_V ** -0.5),
        "w_o": nrm(ks[11], (DEPTH, d, d), BETA * d ** -0.5),
        "ln1_g": 1.0 + nrm(ks[12], (DEPTH, d), 0.02),
        "ln1_b": nrm(ks[13], (DEPTH, d), 0.01),
        "ffn_w_gate": nrm(ks[14], (N_DENSE, d, D_FF), d ** -0.5),
        "ffn_w_up": nrm(ks[15], (N_DENSE, d, D_FF), d ** -0.5),
        "ffn_w_down": nrm(ks[16], (N_DENSE, D_FF, d), BETA * D_FF ** -0.5),
        "moe_w_router": nrm(ks[17], (N_MOE, d, N_EXPERTS), d ** -0.5),
        "moe_w_gate": nrm(ks[18], (N_MOE, N_EXPERTS, d, D_FF_EXPERT), d ** -0.5),
        "moe_w_up": nrm(ks[19], (N_MOE, N_EXPERTS, d, D_FF_EXPERT), d ** -0.5),
        "moe_w_down": nrm(ks[20], (N_MOE, N_EXPERTS, D_FF_EXPERT, d), BETA * D_FF_EXPERT ** -0.5),
        "ln2_g": 1.0 + nrm(ks[21], (DEPTH, d), 0.02),
        "ln2_b": nrm(ks[22], (DEPTH, d), 0.01),
    }

def reference(x, meta, w_in, b_gate, gla_w_a2, gla_b_a, gla_norm_g, ret_norm_g, ret_norm_b,
              w_pa, w_pb, w_o, ln1_g, ln1_b, ffn_w_gate, ffn_w_up, ffn_w_down,
              moe_w_router, moe_w_gate, moe_w_up, moe_w_down, ln2_g, ln2_b):
    bsz = x.shape[0]
    h = jnp.concatenate([jnp.broadcast_to(meta[None].astype(x.dtype), (bsz, N_META, x.shape[-1])), x], axis=1)
    for l in range(DEPTH):
        mix = token_mixer(h, w_in[l], b_gate[l], gla_w_a2[l], gla_b_a[l], gla_norm_g[l],
                          ret_norm_g[l], ret_norm_b[l], w_pa[l], w_pb[l], w_o[l])
        h = layer_norm(ALPHA * h + mix, ln1_g[l], ln1_b[l])
        if l % 2 == 0:
            f = swiglu(h, ffn_w_gate[l // 2], ffn_w_up[l // 2], ffn_w_down[l // 2])
        else:
            f = moe_swiglu(h, moe_w_router[l // 2], moe_w_gate[l // 2], moe_w_up[l // 2], moe_w_down[l // 2])
        h = layer_norm(ALPHA * h + f, ln2_g[l], ln2_b[l])
    return h[:, N_META:]


_drawn_inputs = setup_inputs


def setup_inputs(seed=0):
    import zlib

    import numpy as np

    out = dict(_drawn_inputs(seed))
    spreads = {}
    factors = {'b_gate': 8.0,
     'gla_w_a2': 2.84,
     'gla_b_a': 6.416,
     'gla_norm_g': 5.993,
     'ret_norm_g': 5.741,
     'ret_norm_b': 8.0,
     'ln1_b': 2.821,
     'ln2_b': 2.932}
    for name, (base, spread) in spreads.items():
        noise = np.random.default_rng([zlib.crc32(name.encode()), seed]).standard_normal(out[name].shape)
        drawn = base * np.exp(spread * noise) if base else spread * noise
        out[name] = __import__('jax').numpy.asarray(drawn.astype(out[name].dtype))
    for name, factor in factors.items():
        out[name] = (out[name] * factor).astype(out[name].dtype)
    return out
```

```python
from contextlib import ExitStack

import numpy as np

import concourse.bass as bass
from concourse import mybir

ALU = mybir.AluOpType
ACT = mybir.ActivationFunctionType
AX = mybir.AxisListType
F32 = mybir.dt.float32
F32R = mybir.dt.float32r
I32 = mybir.dt.int32
U32 = mybir.dt.uint32

P = 128
D = 1024
KT = D // P
SEQ, META = 256, 16
T = SEQ + META
CHUNK = 64
NCHUNK = 1 + SEQ // CHUNK
DEPTH = 2
HEADS, DK, DV = 4, 128, 256
RANK = 16
TAU = 16.0
DFF, DFFE = 2816, 3584
EXPERTS = 8
SPILLS = 3
ALPHA = (2 * DEPTH) ** 0.25
LN_EPS, GN_EPS = 1e-5, 1e-6
UNIT = 2048
COLS = 512
RAW, HALVES = 6, 3
JCH = DFFE // COLS
UPJ = 6
UPG = JCH * UPJ
START = 1

SIZES = dict(gq=512, gk=512, gv=1024, gr=1024, ga=RANK, rq=512, rk=512, rv=1024, rg=1024, gate_a=D, gate_b=D)
COL = {}
for _name, _size in SIZES.items():
    COL[_name] = sum(SIZES[k] for k in list(SIZES)[:len(COL)])

TILE_COL = [META, META + P, 0]
TILE_ROWS = [P, P, META]


def host_constants():
    f = np.float32
    p = np.arange(P)
    half = DK // 2
    inv = (f(10000.0) ** (-np.arange(half, dtype=f) / f(half))).astype(f)
    pos = np.stack([META + p, META + P + p, p], 1).astype(f)
    ang = (pos[:, :, None] * inv).astype(f)
    gamma = 1.0 - 2.0 ** (-5.0 - np.arange(HEADS))
    xi = gamma[None, :] ** (p[:, None] % CHUNK + 1.0)
    zeta_x = gamma[None, :] ** (CHUNK - 1.0 - p[:, None] % CHUNK)
    zeta_m = gamma[None, :] ** (META - 1.0 - p[:, None])
    zeta = np.stack([zeta_x, zeta_x, zeta_m], 1) * DK ** -0.5
    causal = (np.arange(CHUNK)[None, :] >= (p % CHUNK)[:, None])
    mask_x = causal[:, None, :] * gamma[None, :, None] ** -float(CHUNK)
    mask_m = causal[:, None, :META] * gamma[None, :, None] ** -float(META)
    restart = np.ones(T)
    restart[[0] + [META + CHUNK * c for c in range(4)]] = 0.0
    parts = dict(
        ident=np.eye(P), cos=np.cos(ang), sin=np.sin(ang), xi=xi, zeta=zeta, mask_x=mask_x, mask_m=mask_m,
        restart=np.broadcast_to(restart, (P, T)), before=(p[:, None] < p[None, :]), ones=np.ones((P, P)),
        iota=np.broadcast_to(np.arange(2 * P), (P, 2 * P)),
    )
    at, where, flat = 0, {}, []
    for name, a in parts.items():
        a = np.ascontiguousarray(a, dtype=f).reshape(P, -1)
        where[name] = (at, at + a.shape[1])
        at += a.shape[1]
        flat.append(a)
    return np.concatenate(flat, 1), where


def trunk(nc, w, consts, where, out, stop=None):
    ctx = ExitStack()
    with ctx:
        def sem(name):
            return ctx.enter_context(nc.semaphore(name))

        def sb(stack, name, shape, dt=F32):
            return stack.enter_context(nc.sbuf_tensor(name, shape, dt))

        raw = sb(ctx, "raw", [P, RAW, UNIT])
        w_hi = sb(ctx, "w_hi", [P, HALVES, UNIT], F32R)
        w_lo = sb(ctx, "w_lo", [P, HALVES, UNIT], F32R)
        h_tok = sb(ctx, "h_tok", [P, 3, D])
        hT_hi = sb(ctx, "hT_hi", [P, KT, T], F32R)
        hT_lo = sb(ctx, "hT_lo", [P, KT, T], F32R)
        rows = sb(ctx, "rows", [P, 2, D])
        tab = sb(ctx, "tab", [P, consts.shape[1]])
        a2 = sb(ctx, "a2", [RANK, DEPTH, HEADS * DK])
        b_a = sb(ctx, "b_a", [P, DEPTH, HEADS])
        b_g = sb(ctx, "b_g", [P, DEPTH, 2, KT])
        stats = sb(ctx, "stats", [P, 3, 4, 6])
        mv = sb(ctx, "mv", [P, 3, 4, 2])
        rstd = sb(ctx, "rstd", [P, 3, 4])
        shift = sb(ctx, "shift", [P, 3, 4])

        def table(name, **dims):
            lo, hi = where[name]
            return tab[:, lo:hi]

        ident = table("ident")

        mix = ExitStack()
        o_tok = sb(mix, "o_tok", [P, 3, D])
        sgA = sb(mix, "sgA", [P, KT, T])
        vlife = ExitStack()
        v_tok = sb(vlife, "v_tok", [P, 3, D])
        attn = ExitStack()
        qT = sb(attn, "qT", [P, HEADS, T])
        kT = sb(attn, "kT", [P, HEADS, T])
        eT = sb(attn, "eT", [P, HEADS, T])
        fT = sb(attn, "fT", [P, HEADS, T])
        bT = sb(attn, "bT", [P, HEADS, T])
        k_tok = sb(attn, "k_tok", [P, 3, HEADS * DK])
        state = sb(attn, "state", [P, 2, HEADS * DV])
        sT = sb(attn, "sT", [P, 3, HEADS * CHUNK])
        gaT = sb(attn, "gaT", [RANK, T])
        decay = sb(attn, "decay", [P, HEADS, NCHUNK])
        attn.close()
        zT_hi = sb(vlife, "zT_hi", [P, KT, T], F32R)
        zT_lo = sb(vlife, "zT_lo", [P, KT, T], F32R)
        vlife.close()
        gs = sb(mix, "gs", [P, 3, COLS])
        mix.close()
        mix2 = ExitStack()
        _o = sb(mix2, "pad_o", [P, 3, D])
        _s = sb(mix2, "pad_s", [P, KT, T])
        sgB = sb(mix2, "sgB", [P, KT, T])
        mix2.close()

        ffn = ExitStack()
        aT_hi = sb(ffn, "aT_hi", [P, DFF // P, T], F32R)
        aT_lo = sb(ffn, "aT_lo", [P, DFF // P, T], F32R)
        gT_s = sb(ffn, "gT_s", [P, 4, T])
        aT_f = sb(ffn, "aT_f", [P, 4, T])
        ffn.close()

        moe = ExitStack()
        x_hi = sb(moe, "x_hi", [P, 2, D], F32R)
        x_lo = sb(moe, "x_lo", [P, 2, D], F32R)
        S = sb(moe, "S", [P, 2, P], F32R)
        ST = sb(moe, "ST", [P, 2, P], F32R)
        xg_hi = sb(moe, "xg_hi", [P, KT, P], F32R)
        xg_lo = sb(moe, "xg_lo", [P, KT, P], F32R)
        g_sl = sb(moe, "g_sl", [P, COLS])
        a_sl = sb(moe, "a_sl", [P, COLS])
        ag_hi = sb(moe, "ag_hi", [P, 4, P], F32R)
        ag_lo = sb(moe, "ag_lo", [P, 4, P], F32R)
        y_hi = sb(moe, "y_hi", [P, D], F32R)
        y_lo = sb(moe, "y_lo", [P, D], F32R)
        wr = sb(moe, "wr", [P, KT, EXPERTS])
        wr_hi = sb(moe, "wr_hi", [P, KT, EXPERTS], F32R)
        wr_lo = sb(moe, "wr_lo", [P, KT, EXPERTS], F32R)
        logit = sb(moe, "logit", [P, 2, EXPERTS])
        prob = sb(moe, "prob", [P, 2, EXPERTS])
        top = sb(moe, "top", [P, 2, 8])
        top_at = sb(moe, "top_at", [P, 2, 8], U32)
        top_f = sb(moe, "top_f", [P, 2, 2])
        hit = sb(moe, "hit", [P, 2, 2, EXPERTS])
        sel = sb(moe, "sel", [P, 2, EXPERTS])
        comb = sb(moe, "comb", [P, 2, EXPERTS])
        rank = sb(moe, "rank", [P, 2, EXPERTS])
        tiny = sb(moe, "tiny", [P, 2, 4])
        slot_w = sb(moe, "slot_w", [P, 1])
        plan_f = sb(moe, "plan_f", [1, 8 * EXPERTS])
        plan = sb(moe, "plan", [1, 4], I32)
        moe.close()

        ps = [ctx.enter_context(nc.psum_tensor(f"ps{i}", [P, 4, 512], F32)) for i in range(2)]

        raw_landed = [sem(f"raw_landed{i}") for i in range(RAW)]
        hi_ready = sem("hi_ready")
        lo_ready = sem("lo_ready")
        units_used = sem("units_used")
        set_full = sem("set_full")
        act_done = sem("act_done")
        dve_done = sem("dve_done")
        act_seq = sem("act_seq")
        dve_seq = sem("dve_seq")
        zb_ready, sp_ready, b_ready, d_ready, e_ready = (sem(n) for n in ("zb_ready", "sp_ready", "b_ready", "d_ready", "e_ready"))
        gla_ready = sem("gla_ready")
        scores_out = sem("scores_out")
        masked = sem("masked")
        var_ready, std_ready = sem("var_ready"), sem("std_ready")
        rot_ready = sem("rot_ready")
        z_ready = sem("z_ready")
        merged_ready = sem("merged_ready")
        mhi_ready, mlo_ready = sem("mhi_ready"), sem("mlo_ready")
        af_ready, ahi_ready = sem("af_ready"), sem("ahi_ready")
        rows_landed, rows_used = sem("rows_landed"), sem("rows_used")
        small_landed, x_landed = sem("small_landed"), sem("x_landed")
        stored = sem("stored")
        xsplit_hi, xsplit_lo = sem("xsplit_hi"), sem("xsplit_lo")
        wrs = sem("wrs")
        prob_ready = sem("prob_ready")
        sel_ready = sem("sel_ready")
        plan_ready = sem("plan_ready")
        m_s, m_xg_full, m_xg_act, m_xg_dve = sem("m_s"), sem("m_xg_full"), sem("m_xg_act"), sem("m_xg_dve")
        m_silu, m_a = sem("m_silu"), sem("m_a")
        m_t, m_ahi, m_alo = sem("m_t"), sem("m_ahi"), sem("m_alo")
        m_yhi, m_ylo, m_sc, m_acc = sem("m_yhi"), sem("m_ylo"), sem("m_sc"), sem("m_acc")

        stream = []

        def add_cols(src, c0, cols=COLS):
            for k in range(0, KT, 4):
                stream.append(("cols", src, k, 4, c0, cols))

        for l in range(DEPTH):
            w_in = w["w_in"][l]
            add_cols(w_in, COL["gk"])
            add_cols(w_in, COL["gq"])
            add_cols(w_in, COL["ga"], P)
            for part in ("gv", "gr"):
                add_cols(w_in, COL[part])
                add_cols(w_in, COL[part] + COLS)
            for c in range(2):
                add_cols(w_in, COL["gate_a"] + c * COLS)
            for c in range(2):
                add_cols(w["w_pa"][l], c * COLS)
            add_cols(w_in, COL["rq"])
            add_cols(w_in, COL["rk"])
            for part in ("rv", "rg"):
                add_cols(w_in, COL[part])
                add_cols(w_in, COL[part] + COLS)
            for c in range(2):
                add_cols(w_in, COL["gate_b"] + c * COLS)
            for c in range(2):
                add_cols(w["w_pb"][l], c * COLS)
            for c in range(2):
                add_cols(w["w_o"][l], c * COLS)
            if l == 0:
                for c0 in range(0, DFF, COLS):
                    n = min(COLS, DFF - c0)
                    add_cols(w["ffn_w_gate"][0], c0, n)
                    add_cols(w["ffn_w_up"][0], c0, n)
                for k in range(0, DFF // P, 2):
                    stream.append(("rows", w["ffn_w_down"][0], k, 2, 0, D))
        NS = len(stream)

        def shape_of(u):
            return (stream[u][3], stream[u][5])

        def unit(buf, slot, k, n):
            return buf[:, slot, 0:k * n].rearrange("p (k n) -> p k n", k=k)

        def landed(eng, u):
            eng.wait_ge(raw_landed[u % RAW], 16 * (u // RAW + 1))

        def hi_unit(act, u):
            landed(act, u)
            if u >= HALVES:
                act.wait_ge(units_used, u - HALVES + 1)
            k, n = shape_of(u)
            nc.scalar.activation(w_hi[:, u % HALVES, 0:k * n], raw[:, u % RAW, 0:k * n], ACT.Copy).then_inc(hi_ready, 1)

        def lo_unit(dve, u):
            dve.wait_ge(hi_ready, u + 1)
            if u >= HALVES:
                dve.wait_ge(units_used, u - HALVES + 1)
            k, n = shape_of(u)
            nc.vector.tensor_tensor(w_lo[:, u % HALVES, 0:k * n], raw[:, u % RAW, 0:k * n],
                                    w_hi[:, u % HALVES, 0:k * n].bitcast(F32), ALU.subtract).then_inc(lo_ready, 1)

        class Splitter:

            def __init__(self, eng, split):
                self.eng, self.split, self.next = eng, split, 0

            def upto(self, u):
                while self.next < min(u, NS):
                    self.split(self.eng, self.next)
                    self.next += 1

        sets = []

        def plan_sets():
            u = 0
            for l in range(DEPTH):
                def weights(name, units):
                    nonlocal u
                    u += units
                    sets.append((l, name, u, True))

                def local(name):
                    sets.append((l, name, u, False))
                if l == 0:
                    local("ht0"); local("ht1")
                weights("gk", 2); weights("gq", 2); weights("ga", 2); local("z")
                weights("gv0", 2); weights("gv1", 2)
                local("g_kt"); local("g_sc")
                for c in range(NCHUNK):
                    local(f"g_o{c}")
                weights("gr0", 2); weights("gr1", 2); local("g_t0"); local("g_t1")
                weights("gta0", 2); weights("gta1", 2); weights("pa0", 2); weights("pa1", 2)
                weights("rq", 2); weights("rk", 2); local("r_qt"); local("r_kt")
                weights("rv0", 2); weights("rv1", 2); local("r_sc")
                for c in range(NCHUNK):
                    local(f"r_o{c}")
                weights("rg0", 2); weights("rg1", 2); local("r_t0"); local("r_t1")
                weights("gtb0", 2); weights("gtb1", 2); weights("pb0", 2); weights("pb1", 2)
                weights("wo0", 2); weights("wo1", 2)
                local("h1t0"); local("h1t1")
                if l == 0:
                    for j in range(6):
                        weights(f"fg{j}", 2); weights(f"fu{j}", 2)
                    weights("fd0", DFF // P // 2); weights("fd1", 0)
                    local("h2t0"); local("h2t1")
                else:
                    local("route"); local("rank")
            assert u == NS

        plan_sets()
        number = {(l, name): r for r, (l, name, _, _) in enumerate(sets)}
        ends = [u for _, _, u, _ in sets]
        NSETS = len(sets)

        def full(eng, r):
            if sets[r][3]:
                eng.wait_ge(units_used, ends[r])
            else:
                eng.wait_ge(set_full, sum(not s[3] for s in sets[:r + 1]))

        def bank(r):
            return ps[r % 2]

        def parts(l):
            return [(slice(0, P), slice(0, 2))] + ([(slice(0, META), slice(2, 3))] if l == 0 else [])

        def parts_all():
            return parts(0)

        def width(l):
            return slice(0, T) if l == 0 else slice(META, T)

        def chunk_cols(c):
            return slice(0, META) if c == 0 else slice(META + CHUNK * (c - 1), META + CHUNK * c)

        def chunk_rows(c):
            if c == 0:
                return 2, slice(0, META)
            return (c - 1) // 2, slice(CHUNK * ((c - 1) % 2), CHUNK * ((c - 1) % 2) + CHUNK)

        act_seq_router = sem("act_seq_router")
        wr_lo_ready = sem("wr_lo_ready")

        def k_tail(h):
            return o_tok[:, h // 2, (h % 2) * T:(h % 2 + 1) * T]

        def load_plan(eng):
            n = eng.value_load(plan[0:1, 0:1], min_val=0, max_val=SPILLS)
            which = [eng.value_load(plan[0:1, 1 + s:2 + s], min_val=0, max_val=EXPERTS - 1) for s in range(SPILLS)]
            return n, which

        block = ctx.enter_context(nc.Block())

        @block.sync
        def _(sp):
            def load(u):
                kind, src, k, kn, c0, n = stream[u]
                if u >= RAW:
                    sp.wait_ge(lo_ready, u - RAW + 1)
                sp.dma_start(unit(raw, u % RAW, kn, n),
                             src[k * P:(k + kn) * P, c0:c0 + n].rearrange("(k p) n -> p k n", p=P)).then_inc(raw_landed[u % RAW], 16)

            for u in range(NS):
                load(u)
            if stop is not None:
                return

            def load_expert(slot, u, src):
                sp.wait_ge(lo_ready, u - RAW + 1)
                sp.dma_start(raw[:, slot, :].rearrange("p (k n) -> p k n", k=src.shape[1]), src).then_inc(raw_landed[slot], 16)

            def gate_up(e, name, k, c0):
                a = w[name][0][bass.ds(e, 1), k * P:(k + 4) * P, bass.ds(c0, COLS)]
                return a.rearrange("e (k p) n -> p (e k) n", p=P)

            def down(e, r0):
                a = w["moe_w_down"][0][bass.ds(e, 1), bass.ds(r0, 2 * P), :]
                return a.rearrange("e (k p) n -> p (e k) n", p=P)

            def expert(g, e):
                u0 = NS + g * UPG
                at = NS % RAW
                for i, (name, k) in enumerate((("moe_w_gate", 0), ("moe_w_gate", 4), ("moe_w_up", 0), ("moe_w_up", 4))):
                    load_expert((at + i) % RAW, u0 + i, gate_up(e, name, k, 0))
                with sp.Fori(1, JCH) as j:
                    uj = u0 + (j * UPJ - 2)
                    for i, (name, k) in enumerate((("moe_w_gate", 0), ("moe_w_gate", 4), ("moe_w_up", 0), ("moe_w_up", 4))):
                        load_expert((at + 4 + i) % RAW, uj + i, gate_up(e, name, k, j * COLS))
                    for i in range(2):
                        load_expert((at + 8 + i) % RAW, uj + 4 + i, down(e, j * COLS - COLS + i * 2 * P))
                for i in range(2):
                    load_expert((at + 4 + i) % RAW, u0 + UPG - 2 + i, down(e, DFFE - COLS + i * 2 * P))

            with sp.Fori(0, EXPERTS) as g:
                expert(g, g)
            sp.wait_ge(plan_ready, 1)
            n_groups, spill = load_plan(sp)
            for s in range(SPILLS):
                with sp.If(n_groups > s):
                    expert(EXPERTS + s, spill[s])
                sp.end_ifs()
            sp.wait_ge(z_ready, 4)
            for t in range(2):
                sp.dma_start(out[0, t * P:(t + 1) * P, :], h_tok[:, t, :]).then_inc(stored, 16)
            sp.wait_ge(stored, 32)

        @block.gpsimd
        def _(pool):
            pool.dma_start(tab[:, :], consts[:, :]).then_inc(small_landed, 16)
            for l in range(DEPTH):
                pool.dma_start(a2[:, l, :], w["gla_w_a2"][l]).then_inc(small_landed, 16)
            with nc.allow_non_contiguous_dma(reason="a few parameters, one per partition"):
                for l in range(DEPTH):
                    pool.dma_start(b_a[:, l, :], w["gla_b_a"][l].rearrange("(h p) -> p h", p=P)).then_inc(small_landed, 16)
                    for s in range(2):
                        pool.dma_start(b_g[:, l, s, :], w["b_gate"][l, s].rearrange("(k p) -> p k", p=P)).then_inc(small_landed, 16)

            loads = 0

            def load_rows(srcs):
                nonlocal loads
                if loads:
                    pool.wait_ge(rows_used, loads)
                for i, a in enumerate(srcs):
                    pool.dma_start(rows[:, i, 0:a.shape[0]], a.partition_broadcast(P)).then_inc(rows_landed, 16)
                loads += 1

            for l in range(DEPTH):
                load_rows([w["gla_norm_g"][l], w["gla_norm_g"][l]])
                pool.wait_ge(scores_out, l + 1)
                for tile, lo, hi in ((0, 0, CHUNK), (0, CHUNK, P), (1, 0, CHUNK), (1, CHUNK, P), (2, 0, META)):
                    n = hi - lo
                    a = sT[lo:hi, tile, 0:HEADS * n].rearrange("p (h i) -> p h i", h=HEADS)
                    pool.affine_select(out=a, in_=a, compare_op=ALU.is_ge, fill=0.0, base=0,
                                       pattern=[[0, HEADS], [1, n]], channel_multiplier=-1).then_inc(masked, 1)
                load_rows([w["ret_norm_g"][l], w["ret_norm_b"][l]])
                load_rows([w["ln1_g"][l], w["ln1_b"][l]])
                if l == 1:
                    full(pool, number[1, "wo1"])
                    pool.dma_start(wr[:, :, :], w["moe_w_router"][0].rearrange("(k p) e -> p k e", p=P)).then_inc(wrs, 16)
                load_rows([w["ln2_g"][l], w["ln2_b"][l]])

        @block.tensor
        def _(pe):
            used = 0

            def mm3(dst, l_hi, l_lo, r_hi, r_lo, start, stop):
                nc.tensor.matmul(dst, l_lo, r_hi, start=start, stop=False)
                nc.tensor.matmul(dst, l_hi, r_lo, start=False, stop=False)
                return nc.tensor.matmul(dst, l_hi, r_hi, start=False, stop=stop)

            def begin(l, name):
                r = number[l, name]
                if r >= 2:
                    pe.wait_ge(act_done, r - 1)
                    pe.wait_ge(dve_done, r - 1)
                return bank(r)

            def after(l, name):
                pe.wait_ge(act_done, number[l, name] + 1)
                pe.wait_ge(dve_done, number[l, name] + 1)

            def next_unit():
                nonlocal used
                pe.wait_ge(lo_ready, used + 1)
                k, n = shape_of(used)
                s = used % HALVES
                used += 1
                return unit(w_hi, s, k, n), unit(w_lo, s, k, n), k, n

            def feature_major(l, name, x_hi_, x_lo_, cols):
                pt = begin(l, name)
                for k0 in (0, 4):
                    u_hi, u_lo, kn, n = next_unit()
                    for k in range(kn):
                        for m in range(n // P):
                            last = mm3(pt[:, m, cols], u_hi[:, k, m * P:(m + 1) * P], u_lo[:, k, m * P:(m + 1) * P],
                                       x_hi_[:, k0 + k, cols], x_lo_[:, k0 + k, cols],
                                       start=(k0 + k == 0), stop=(k0 + k == KT - 1))
                    last.then_inc(units_used, 1)

            def fill(last):
                last.then_inc(set_full, 1)

            def token_major(l, name, x_hi_, x_lo_, tiles):
                pt = begin(l, name)
                for k0 in (0, 4):
                    u_hi, u_lo, kn, n = next_unit()
                    for k in range(kn):
                        for t in range(tiles):
                            c = TILE_COL[t]
                            last = mm3(pt[:, t, 0:n], x_hi_[:, k0 + k, c:c + P], x_lo_[:, k0 + k, c:c + P],
                                       u_hi[:, k, :], u_lo[:, k, :], start=(k0 + k == 0), stop=(k0 + k == KT - 1))
                    last.then_inc(units_used, 1)

            def transposes(l, names, src, tiles):
                for i, name in enumerate(names):
                    pt = begin(l, name)
                    for k in range(4):
                        for t in range(tiles):
                            c, n, f = TILE_COL[t], TILE_ROWS[t], (4 * i + k) * P
                            last = nc.tensor.transpose(pt[:, k, c:c + n], src[0:n, t, f:f + P], ident[0:n, 0:n])
                    fill(last)

            def attention(l, b):
                pt = begin(l, f"{b}_sc")
                for c in range(NCHUNK):
                    tile, rws = chunk_rows(c)
                    n = rws.stop - rws.start
                    for h in range(HEADS):
                        last = nc.tensor.matmul(pt[rws, tile, h * n:(h + 1) * n], kT[:, h, chunk_cols(c)], qT[:, h, chunk_cols(c)],
                                                start=True, stop=True)
                fill(last)
                for c in range(NCHUNK):
                    tile, rws = chunk_rows(c)
                    n = rws.stop - rws.start
                    pt = begin(l, f"{b}_o{c}")
                    if c < NCHUNK - 1:
                        for h in range(HEADS):
                            last = nc.tensor.matmul(pt[:, h // 2, (h % 2) * DV:(h % 2 + 1) * DV], k_tok[rws, tile, h * DK:(h + 1) * DK],
                                                    v_tok[rws, tile, h * DV:(h + 1) * DV], start=True, stop=True)
                    if c == 0:
                        if b == "g":
                            pe.wait_ge(masked, 5 * (l + 1))
                        else:
                            after(l, "r_sc")
                    if c >= 1:
                        pe.wait_ge(dve_done, number[l, f"{b}_o{c - 1}"] + 1)
                    if c or l == 0:
                        for h in range(HEADS):
                            dst = pt[rws, 2 + h // 2, (h % 2) * DV:(h % 2 + 1) * DV]
                            last = nc.tensor.matmul(dst, sT[rws, tile, h * n:(h + 1) * n], v_tok[rws, tile, h * DV:(h + 1) * DV],
                                                    start=True, stop=(c == 0))
                            if c:
                                last = nc.tensor.matmul(dst, qT[:, h, chunk_cols(c)], state[:, c % 2, h * DV:(h + 1) * DV],
                                                        start=False, stop=True)
                    fill(last)

            pe.wait_ge(small_landed, 16 * (1 + 4 * DEPTH))
            pe.wait_ge(x_landed, 48)
            transposes(0, ("ht0", "ht1"), h_tok, 3)
            for l in range(DEPTH):
                tiles = len(parts(l)) + 1
                cols = width(l)
                after(l, "ht1") if l == 0 else after(0, "h2t1")
                feature_major(l, "gk", hT_hi, hT_lo, slice(0, T))
                feature_major(l, "gq", hT_hi, hT_lo, slice(0, T))
                feature_major(l, "ga", hT_hi, hT_lo, slice(0, T))
                after(l, "ga")
                pt = begin(l, "z")
                for h in range(HEADS):
                    last = nc.tensor.matmul(pt[:, h, 0:T], a2[:, l, h * DK:(h + 1) * DK], gaT[:, :], start=True, stop=True)
                fill(last)
                token_major(l, "gv0", hT_hi, hT_lo, 3)
                token_major(l, "gv1", hT_hi, hT_lo, 3)
                pt = begin(l, "g_kt")
                pe.wait_ge(gla_ready, l + 1)
                for t in range(3):
                    c, n = TILE_COL[t], TILE_ROWS[t]
                    for h in range(HEADS):
                        last = nc.tensor.transpose(pt[0:n, t, h * DK:(h + 1) * DK], k_tail(h)[:, c:c + n], ident)
                fill(last)
                after(l, "g_kt")
                attention(l, "g")
                token_major(l, "gr0", hT_hi, hT_lo, tiles)
                token_major(l, "gr1", hT_hi, hT_lo, tiles)
                after(l, "gr1")
                transposes(l, ("g_t0", "g_t1"), o_tok, tiles)
                for c in range(2):
                    feature_major(l, f"gta{c}", hT_hi, hT_lo, cols)
                for c in range(2):
                    feature_major(l, f"pa{c}", zT_hi, zT_lo, cols)
                token_major(l, "rq", hT_hi, hT_lo, tiles)
                token_major(l, "rk", hT_hi, hT_lo, 3)
                for name, src, n_t in (("r_qt", o_tok, tiles), ("r_kt", k_tok, 3)):
                    after(l, {"r_qt": "rq", "r_kt": "rk"}[name])
                    pt = begin(l, name)
                    for h in range(HEADS):
                        for t in range(n_t):
                            c, n = TILE_COL[t], TILE_ROWS[t]
                            last = nc.tensor.transpose(pt[:, h, c:c + n], src[0:n, t, h * DK:(h + 1) * DK], ident[0:n, 0:n])
                    fill(last)
                token_major(l, "rv0", hT_hi, hT_lo, 3)
                token_major(l, "rv1", hT_hi, hT_lo, 3)
                after(l, "rv1")
                attention(l, "r")
                token_major(l, "rg0", hT_hi, hT_lo, tiles)
                token_major(l, "rg1", hT_hi, hT_lo, tiles)
                after(l, "rg1")
                transposes(l, ("r_t0", "r_t1"), o_tok, tiles)
                for c in range(2):
                    feature_major(l, f"gtb{c}", hT_hi, hT_lo, cols)
                for c in range(2):
                    feature_major(l, f"pb{c}", zT_hi, zT_lo, cols)
                after(l, "pb1")
                token_major(l, "wo0", zT_hi, zT_lo, tiles)
                token_major(l, "wo1", zT_hi, zT_lo, tiles)
                pe.wait_ge(z_ready, 2 * l + 1)
                transposes(l, ("h1t0", "h1t1"), h_tok, tiles)
                after(l, "h1t1")
                if l == 0:
                    for j in range(6):
                        feature_major(l, f"fg{j}", hT_hi, hT_lo, slice(0, T))
                        feature_major(l, f"fu{j}", hT_hi, hT_lo, slice(0, T))
                    after(l, "fu5")
                    pt = [begin(l, "fd0"), begin(l, "fd1")]
                    for k0 in range(0, DFF // P, 2):
                        u_hi, u_lo, kn, n = next_unit()
                        for k in range(kn):
                            for t in range(3):
                                c = TILE_COL[t]
                                for q in range(2):
                                    last = mm3(pt[q][:, t, :], aT_hi[:, k0 + k, c:c + P], aT_lo[:, k0 + k, c:c + P],
                                               u_hi[:, k, q * COLS:(q + 1) * COLS], u_lo[:, k, q * COLS:(q + 1) * COLS],
                                               start=(k0 + k == 0), stop=(k0 + k == DFF // P - 1))
                        last.then_inc(units_used, 1)
                    pe.wait_ge(z_ready, 2)
                    transposes(l, ("h2t0", "h2t1"), h_tok, 3)
            if stop is not None:
                return

            pt = begin(1, "route")
            pe.wait_ge(act_seq_router, 1)
            pe.wait_ge(wr_lo_ready, 1)
            for t in range(2):
                c = TILE_COL[t]
                for k in range(KT):
                    last = mm3(pt[:, 0, t * EXPERTS:(t + 1) * EXPERTS], hT_hi[:, k, c:c + P], hT_lo[:, k, c:c + P],
                               wr_hi[:, k, :], wr_lo[:, k, :], start=(k == 0), stop=(k == KT - 1))
            fill(last)
            pt = begin(1, "rank")
            pe.wait_ge(sel_ready, 1)
            before, ones = table("before"), table("ones")
            nc.tensor.matmul(pt[:, 0, 0:EXPERTS], before, sel[:, 0, :], start=True, stop=True)
            nc.tensor.matmul(pt[:, 0, EXPERTS:2 * EXPERTS], before, sel[:, 1, :], start=True, stop=False)
            nc.tensor.matmul(pt[:, 0, EXPERTS:2 * EXPERTS], ones, sel[:, 0, :], start=False, stop=True)
            nc.tensor.matmul(pt[0:1, 1, 0:EXPERTS], ones[:, 0:1], sel[:, 0, :], start=True, stop=False)
            last = nc.tensor.matmul(pt[0:1, 1, 0:EXPERTS], ones[:, 0:1], sel[:, 1, :], start=False, stop=True)
            fill(last)
            pe.wait_ge(act_done, NSETS)
            pe.wait_ge(dve_done, NSETS)
            pe.wait_ge(xsplit_lo, 1)

            G_, U_ = ps[0][:, 0, :], ps[0][:, 1, :]
            TB, MISC = ps[0][:, 2, :], ps[0][:, 3, :]
            Y = ps[1][:, 0:2, :]
            X = ps[1][:, 2:4, :]

            def expert_unit(at, u):
                pe.wait_ge(lo_ready, u + 1)
                return w_hi[:, at % HALVES, :], w_lo[:, at % HALVES, :]

            def gate_or_up(dst, at, u):
                for i in range(2):
                    u_hi, u_lo = expert_unit(at + i, u + i)
                    for k in range(4):
                        last = mm3(dst, xg_hi[:, 4 * i + k, :], xg_lo[:, 4 * i + k, :],
                                   u_hi[:, k * COLS:(k + 1) * COLS], u_lo[:, k * COLS:(k + 1) * COLS],
                                   start=(i == 0 and k == 0), stop=(i == 1 and k == 3))
                    last.then_inc(units_used, 1)

            def turn(k):
                pe.wait_ge(m_a, START + k + 1)
                pe.wait_ge(m_alo, START + k)
                for i in range(4):
                    last = nc.tensor.transpose(TB[:, i * P:(i + 1) * P], a_sl[:, i * P:(i + 1) * P], ident)
                last.then_inc(m_t, 1)

            def down(at, u, k, first, final):
                pe.wait_ge(m_alo, START + k + 1)
                for i in range(2):
                    u_hi, u_lo = expert_unit(at + i, u + i)
                    for kk in range(2):
                        for q in range(2):
                            o = kk * D + q * COLS
                            last = nc.tensor.matmul(Y[:, q, :], ag_lo[:, 2 * i + kk, :], u_hi[:, o:o + COLS],
                                                    start=first and i == 0 and kk == 0, stop=False)
                            nc.tensor.matmul(Y[:, q, :], ag_hi[:, 2 * i + kk, :], u_lo[:, o:o + COLS], start=False, stop=False)
                            last = nc.tensor.matmul(Y[:, q, :], ag_hi[:, 2 * i + kk, :], u_hi[:, o:o + COLS],
                                                    start=False, stop=final and i == 1 and kk == 1)
                    last.then_inc(units_used, 1)

            def expert(g, e):
                u0, k0, at = NS + g * UPG, g * JCH, NS
                pe.wait_ge(m_s, START + g + 1)
                pe.wait_ge(m_acc, START + 2 * g)
                for k in range(KT):
                    for t in range(2):
                        nc.tensor.matmul(X[:, k // 4, (k % 4) * P:(k % 4 + 1) * P], x_lo[:, t, k * P:(k + 1) * P], S[:, t, :],
                                         start=(t == 0), stop=False)
                        nc.tensor.matmul(X[:, k // 4, (k % 4) * P:(k % 4 + 1) * P], x_hi[:, t, k * P:(k + 1) * P], S[:, t, :],
                                         start=False, stop=(t == 1))
                for t in range(2):
                    nc.tensor.matmul(MISC[:, 0:1], S[:, t, :].bitcast(F32), comb[:, t, bass.ds(e, 1)], start=(t == 0), stop=(t == 1))
                for t in range(2):
                    last = nc.tensor.transpose(MISC[:, (t + 1) * P:(t + 2) * P], S[:, t, :].bitcast(F32), ident)
                last.then_inc(m_xg_full, 1)
                pe.wait_ge(m_xg_act, START + g + 1)
                pe.wait_ge(m_xg_dve, START + g + 1)
                pe.wait_ge(m_silu, START + k0)
                gate_or_up(G_, at, u0)
                pe.wait_ge(m_a, START + k0)
                gate_or_up(U_, at + 2, u0 + 2)
                def chunk(j, first):
                    uj, k = u0 + (j * UPJ - 2), k0 + j
                    pe.wait_ge(m_silu, START + k)
                    gate_or_up(G_, at + 4, uj)
                    turn(k - 1)
                    gate_or_up(U_, at + 6, uj + 2)
                    if first:
                        pe.wait_ge(m_ylo, START + g)
                    down(at + 8, uj + 4, k - 1, first, False)
                chunk(1, True)
                with pe.Fori(2, JCH) as j:
                    chunk(j, False)
                turn(k0 + JCH - 1)
                down(at + 4, u0 + UPG - 2, k0 + JCH - 1, False, True)
                pe.wait_ge(m_ylo, START + g + 1)
                pe.wait_ge(m_yhi, START + g + 1)
                pe.wait_ge(m_alo, START + k0 + JCH)
                for t, dst in ((0, X), (1, ps[0][:, 2:4, :])):
                    for q in range(2):
                        nc.tensor.matmul(dst[:, q, :], ST[:, t, :], y_lo[:, q * COLS:(q + 1) * COLS], start=True, stop=False)
                        last = nc.tensor.matmul(dst[:, q, :], ST[:, t, :], y_hi[:, q * COLS:(q + 1) * COLS], start=False, stop=True)
                    last.then_inc(m_sc, 1)

            for first in (m_t, m_sc, m_xg_full):
                pe.sem_inc(first, START)
            with pe.Fori(0, EXPERTS) as g:
                expert(g, g)
            pe.wait_ge(plan_ready, 1)
            n_groups, spill = load_plan(pe)
            for s in range(SPILLS):
                with pe.If(n_groups > s):
                    expert(EXPERTS + s, spill[s])
                pe.end_ifs()

        @block.scalar
        def _(act):
            seq = 0

            def step(ins):
                nonlocal seq
                seq += 1
                ins.then_inc(act_seq, 1)

            def settle():
                act.wait_ge(act_seq, seq)

            def copy(dst, src, **kw):
                return nc.scalar.activation(dst, src, ACT.Copy, **kw)

            split = Splitter(act, hi_unit)

            def take(l, name, own=True):
                r = number[l, name]
                split.upto(ends[r] + HALVES - 1)
                full(act, r)
                return r, bank(r)

            def skip(l, name):
                take(l, name)
                act.sem_inc(act_done, 1)

            def to_transposed(l, names, dst):
                for i, name in enumerate(names):
                    r, pt = take(l, name)
                    copy(dst[:, 4 * i:4 * i + 4, width(l)], pt[:, :, width(l)]).then_inc(act_done, 1)

            def std(count):
                act.wait_ge(var_ready, count)
                for rws, ts in parts_now:
                    ins = nc.scalar.activation(rstd[rws, ts, :], rstd[rws, ts, :], ACT.Sqrt)
                ins.then_inc(std_ready, 1)

            split.upto(HALVES - 1)
            stds = 0
            for i, (tile, src) in enumerate(((0, w["x"][0, 0:P, :]), (1, w["x"][0, P:2 * P, :]), (2, w["meta"]))):
                act.dma_start(h_tok[0:TILE_ROWS[tile], tile, :], src).then_inc(x_landed, 16)
            to_transposed(0, ("ht0", "ht1"), hT_hi)
            for l in range(DEPTH):
                parts_now = parts(l)
                r, pt = take(l, "gk")
                copy(kT[:, :, :], pt[:, :, 0:T]).then_inc(act_done, 1)
                r, pt = take(l, "gq")
                copy(qT[:, :, :], pt[:, :, 0:T], scale=DK ** -0.5).then_inc(act_done, 1)
                r, pt = take(l, "ga")
                copy(gaT[:, :], pt[0:RANK, 0, 0:T]).then_inc(act_done, 1)
                take(l, "z")
                act.wait_ge(zb_ready, l + 1)
                step(nc.scalar.activation(fT[:, :, :], eT[:, :, :], ACT.Abs))
                settle()
                step(nc.scalar.activation(fT[:, :, :], fT[:, :, :], ACT.Exp, scale=-1.0))
                settle()
                nc.scalar.activation(fT[:, :, :], fT[:, :, :], ACT.Ln, bias=1.0).then_inc(sp_ready, 1)
                act.sem_inc(act_done, 1)
                for c in range(2):
                    r, pt = take(l, f"gv{c}")
                    for rws, ts in parts_all():
                        ins = copy(v_tok[rws, ts, c * COLS:(c + 1) * COLS], pt[rws, ts, :])
                    ins.then_inc(act_done, 1)
                act.wait_ge(d_ready, l + 1)
                nc.scalar.activation(fT[:, :, :], bT[:, :, :], ACT.Exp, scale=1.0 / TAU)
                nc.scalar.activation(eT[:, :, :], bT[:, :, :], ACT.Exp, scale=-1.0 / TAU)
                for h in range(0, HEADS, 2):
                    nc.scalar.activation(o_tok[:, h // 2, 0:2 * T], o_tok[:, h // 2, 0:2 * T], ACT.Exp, scale=1.0 / TAU)
                nc.scalar.activation(decay[:, :, 0:1], bT[:, :, META - 1:META], ACT.Exp, scale=1.0 / TAU)
                nc.scalar.activation(decay[:, :, 1:], bT[:, :, META + CHUNK - 1:T:CHUNK], ACT.Exp, scale=1.0 / TAU).then_inc(e_ready, 1)
                for b, q in (("g", 0), ("r", 1)):
                    if b == "g":
                        r, pt = take(l, "g_kt")
                        for rws, ts in parts_all():
                            ins = copy(k_tok[rws, ts, :], pt[rws, ts, :])
                        ins.then_inc(act_done, 1)
                    else:
                        skip(l, "rq")
                        skip(l, "rk")
                        r, pt = take(l, "r_qt")
                        copy(qT[:, :, width(l)], pt[:, :, width(l)]).then_inc(act_done, 1)
                        r, pt = take(l, "r_kt")
                        copy(kT[:, :, :], pt[:, :, 0:T]).then_inc(act_done, 1)
                        for c in range(2):
                            r, pt = take(l, f"rv{c}")
                            for rws, ts in parts_all():
                                ins = copy(v_tok[rws, ts, c * COLS:(c + 1) * COLS], pt[rws, ts, :])
                            ins.then_inc(act_done, 1)
                    skip(l, f"{b}_sc")
                    for c in range(NCHUNK):
                        if c == 0 and l == 1:
                            skip(l, f"{b}_o{c}")
                            continue
                        r, pt = take(l, f"{b}_o{c}")
                        tile, rws = chunk_rows(c)
                        copy(o_tok[rws, tile, :].rearrange("p (b n) -> p b n", b=2), pt[rws, 2:4, :]).then_inc(act_done, 1)
                    stds += 1
                    std(stds)
                    for c in range(2):
                        name = f"{b}r{c}" if b == "g" else f"rg{c}"
                        r, pt = take(l, name)
                        if c == 1:
                            act.wait_ge(dve_done, r)
                        for rws, ts in parts_now:
                            ins = nc.scalar.activation(gs[rws, ts, :], pt[rws, ts, :], ACT.Silu)
                        ins.then_inc(act_done, 1)
                    to_transposed(l, (f"{b}_t0", f"{b}_t1"), zT_hi)
                    sg = sgA if b == "g" else sgB
                    for c in range(2):
                        r, pt = take(l, f"gt{'ab'[q]}{c}")
                        for m in range(4):
                            ins = nc.scalar.activation(sg[:, 4 * c + m, width(l)], pt[:, m, width(l)], ACT.Sigmoid,
                                                       bias=b_g[:, l, q, 4 * c + m:4 * c + m + 1])
                        ins.then_inc(act_done, 1)
                    for c in range(2):
                        r, pt = take(l, f"p{'ab'[q]}{c}")
                        if b == "g":
                            act.sem_inc(act_done, 1)
                        else:
                            if c == 0:
                                act.sem_inc(act_done, 1)
                            else:
                                act.wait_ge(merged_ready, l + 1)
                                copy(zT_hi[:, :, width(l)], sgA[:, :, width(l)]).then_inc(mhi_ready, 1)
                                act.sem_inc(act_done, 1)
                skip(l, "wo0")
                skip(l, "wo1")
                stds += 1
                std(stds)
                to_transposed(l, ("h1t0", "h1t1"), hT_hi)
                if l == 0:
                    for j in range(6):
                        n = 4 if j < 5 else 2
                        r, pt = take(l, f"fg{j}")
                        if j:
                            act.wait_ge(af_ready, j)
                        nc.scalar.activation(gT_s[:, 0:n, :], pt[:, 0:n, 0:T], ACT.Silu).then_inc(act_done, 1)
                        take(l, f"fu{j}")
                        act.wait_ge(af_ready, j + 1)
                        copy(aT_hi[:, 4 * j:4 * j + n, :], aT_f[:, 0:n, :]).then_inc(ahi_ready, 1)
                        act.sem_inc(act_done, 1)
                    skip(l, "fd0")
                    skip(l, "fd1")
                    stds += 1
                    std(stds)
                    to_transposed(0, ("h2t0", "h2t1"), hT_hi)
            if stop is not None:
                return

            act.wait_ge(wrs, 16)
            copy(wr_hi[:, :, :], wr[:, :, :]).then_inc(act_seq_router, 1)
            copy(x_hi[:, :, :], h_tok[:, 0:2, :]).then_inc(xsplit_hi, 1)
            r, pt = take(1, "route")
            copy(logit[:, :, :], pt[:, 0, 0:2 * EXPERTS].rearrange("p (t e) -> p t e", t=2)).then_inc(act_done, 1)
            act.wait_ge(prob_ready, 1)
            for t in range(2):
                ins = nc.scalar.activation(prob[:, t, :], logit[:, t, :], ACT.Exp, bias=tiny[:, t, 0:1], accum_out=tiny[:, t, 1:2])
            ins.then_inc(act_seq_router, 1)
            skip(1, "rank")

            def hi_at(at, u, uses):
                act.wait_ge(raw_landed[at % RAW], uses * 16 + 16)
                act.wait_ge(units_used, u - HALVES + 1)
                copy(w_hi[:, at % HALVES, :], raw[:, at % RAW, :]).then_inc(hi_ready, 1)

            def expert(g, e):
                u0, k0 = NS + g * UPG, g * JCH
                base = g * (UPG // RAW)

                def hi(i, turns, u):
                    hi_at(NS + i, u, base + turns + (NS + i) // RAW)

                def turned(k, u):
                    act.wait_ge(m_t, START + k + 1)
                    act.wait_ge(units_used, u)
                    copy(ag_hi[:, :, :], TB4).then_inc(m_ahi, 1)

                def silu(k, u):
                    act.wait_ge(units_used, u)
                    act.wait_ge(m_a, START + k)
                    nc.scalar.activation(g_sl[:, :], ps[0][:, 0, :], ACT.Silu).then_inc(m_silu, 1)

                for i in range(3):
                    hi(i, 0, u0 + i)
                act.wait_ge(m_xg_full, START + g + 1)
                copy(xg_hi[:, :, :], ps[1][:, 2:4, :].rearrange("p b (k s) -> p (b k) s", s=P))
                copy(slot_w[:, :], ps[0][:, 3, 0:1])
                copy(ST[:, :, :], ps[0][:, 3, P:3 * P].rearrange("p (t s) -> p t s", t=2)).then_inc(m_xg_act, 1)
                hi(3, 0, u0 + 3)
                silu(k0, u0 + 2)
                with act.Fori(1, JCH) as j:
                    uj, k, turns = u0 + (j * UPJ - 2), k0 + j, j - 1
                    for i in range(4):
                        hi(4 + i, turns, uj + i)
                    turned(k - 1, uj)
                    silu(k, uj + 2)
                    for i in range(4, 6):
                        hi(4 + i, turns, uj + i)
                for i in range(2):
                    hi(4 + i, JCH - 1, u0 + UPG - 2 + i)
                turned(k0 + JCH - 1, u0 + UPG - 2)
                act.wait_ge(units_used, u0 + UPG)
                nc.scalar.activation(y_hi[:, :].rearrange("p (b n) -> p b n", b=2), ps[1][:, 0:2, :], ACT.Copy,
                                     scale=slot_w[:, 0:1]).then_inc(m_yhi, 1)

            TB4 = ps[0][:, 2, :].rearrange("p (k s) -> p k s", s=P)
            for first in (m_silu, m_xg_act, m_ahi, m_yhi):
                act.sem_inc(first, START)
            with act.Fori(0, EXPERTS) as g:
                expert(g, g)
            act.wait_ge(plan_ready, 1)
            n_groups, spill = load_plan(act)
            for s in range(SPILLS):
                with act.If(n_groups > s):
                    expert(EXPERTS + s, spill[s])
                act.end_ifs()
            act.wait_ge(var_ready, stds + 1)
            nc.scalar.activation(rstd[:, 0:2, :], rstd[:, 0:2, :], ACT.Sqrt).then_inc(std_ready, 1)

        @block.vector
        def _(dve):
            seq = 0

            def step(ins):
                nonlocal seq
                seq += 1
                ins.then_inc(dve_seq, 1)

            def settle():
                dve.wait_ge(dve_seq, seq)

            split = Splitter(dve, lo_unit)

            def take(l, name):
                r = number[l, name]
                split.upto(ends[r] + HALVES - 1)
                full(dve, r)
                return r, bank(r)

            def skip(l, name):
                take(l, name)
                dve.sem_inc(dve_done, 1)

            tt, ts_, stt = nc.vector.tensor_tensor, nc.vector.tensor_scalar, nc.vector.scalar_tensor_tensor

            def to_transposed(l, names, hi, lo):
                for i, name in enumerate(names):
                    r, pt = take(l, name)
                    dve.wait_ge(act_done, r + 1)
                    s = (slice(None), slice(4 * i, 4 * i + 4), width(l))
                    tt(lo[s], pt[:, :, width(l)], hi[s].bitcast(F32), ALU.subtract).then_inc(dve_done, 1)

            stds = 0

            def normalise(src, groups, size, eps, centred, where_parts):
                nonlocal stds
                pieces = max(1, size // 512)
                for rws, ts in where_parts:
                    for t in range(ts.start, ts.stop):
                        for g in range(groups):
                            for q in range(pieces):
                                n = size // pieces
                                step(nc.vector.bn_stats(stats[rws, t, g + q, :], src[rws, t, g * size + q * n:g * size + (q + 1) * n]))
                settle()
                for rws, ts in where_parts:
                    for t in range(ts.start, ts.stop):
                        for g in range(groups):
                            step(nc.vector.bn_aggr(mv[rws, t, g, :], stats[rws, t, g:g + pieces, :].rearrange("p a b -> p (a b)")))
                settle()
                for rws, ts in where_parts:
                    mean, var, r_ = mv[rws, ts, 0:groups, 0], mv[rws, ts, 0:groups, 1], rstd[rws, ts, 0:groups]
                    if not centred:
                        step(tt(r_, mean, mean, ALU.mult))
                        settle()
                        step(tt(r_, r_, var, ALU.add))
                        settle()
                        var = r_
                    step(ts_(r_, var, float(eps), None, ALU.add))
                settle()
                stds += 1
                for i, (rws, ts) in enumerate(where_parts):
                    ins = nc.vector.reciprocal(rstd[rws, ts, 0:groups], rstd[rws, ts, 0:groups])
                ins.then_inc(var_ready, 1)
                dve.wait_ge(std_ready, stds)
                if centred:
                    for rws, ts in where_parts:
                        step(stt(shift[rws, ts, 0:groups], mv[rws, ts, 0:groups, 0], -1.0, rstd[rws, ts, 0:groups], ALU.mult, ALU.mult))
                    settle()

            rows_n = 0

            def rows_ready():
                nonlocal rows_n
                rows_n += 1
                dve.wait_ge(rows_landed, 32 * rows_n)

            def layer_norm(where_parts):
                normalise(h_tok, 1, D, LN_EPS, True, where_parts)
                for rws, ts in where_parts:
                    for t in range(ts.start, ts.stop):
                        step(ts_(h_tok[rws, t, :], h_tok[rws, t, :], rstd[rws, t, 0:1], shift[rws, t, 0:1], ALU.mult, ALU.add))
                settle()
                rows_ready()
                for rws, ts in where_parts:
                    for t in range(ts.start, ts.stop):
                        step(tt(h_tok[rws, t, :], h_tok[rws, t, :], rows[rws, 0, :], ALU.mult))
                settle()
                for rws, ts in where_parts:
                    for t in range(ts.start, ts.stop):
                        step(tt(h_tok[rws, t, :], h_tok[rws, t, :], rows[rws, 1, :], ALU.add))
                settle()
                dve.sem_inc(rows_used, 1)

            def heads(a, n):
                return a.rearrange("p (h n) -> p h n", n=n)

            step(nc.vector.memset(rstd[:, :, :], 1.0))
            settle()
            dve.wait_ge(small_landed, 16 * (1 + 4 * DEPTH))
            to_transposed(0, ("ht0", "ht1"), hT_hi, hT_lo)
            for l in range(DEPTH):
                now = parts(l)
                skip(l, "gk")
                skip(l, "gq")
                skip(l, "ga")
                r, pt = take(l, "z")
                for h in range(HEADS):
                    ins = ts_(eT[:, h, :], pt[:, h, 0:T], b_a[:, l, h:h + 1], None, ALU.add)
                ins.then_inc(zb_ready, 1)
                dve.sem_inc(dve_done, 1)
                dve.wait_ge(zb_ready, l + 1)
                dve.wait_ge(sp_ready, l + 1)
                step(stt(eT[:, :, :], eT[:, :, :], 0.0, fT[:, :, :], ALU.min, ALU.subtract))
                settle()
                for h in range(HEADS):
                    step(nc.vector.tensor_tensor_scan(bT[:, h, :], table("restart"), eT[:, h, :], 0.0, ALU.mult, ALU.add))
                settle()
                for h in range(0, HEADS, 2):
                    dst = o_tok[:, h // 2, 0:2 * T].rearrange("p (h t) -> p h t", h=2)
                    b2 = bT[:, h:h + 2, :]
                    step(tt(dst[:, :, 0:META], b2[:, :, META - 1:META].broadcast_to([P, 2, META]), b2[:, :, 0:META], ALU.subtract))
                    for hh in range(2):
                        d4 = dst[:, hh, META:].rearrange("p (c i) -> p c i", i=CHUNK)
                        s4 = b2[:, hh, META:].rearrange("p (c i) -> p c i", i=CHUNK)
                        ins = tt(d4, s4[:, :, CHUNK - 1:CHUNK].broadcast_to([P, NCHUNK - 1, CHUNK]), s4, ALU.subtract)
                        if h + hh < HEADS - 1:
                            step(ins)
                ins.then_inc(d_ready, 1)
                skip(l, "gv0")
                skip(l, "gv1")
                dve.wait_ge(e_ready, l + 1)
                step(tt(qT[:, :, :], qT[:, :, :], fT[:, :, :], ALU.mult))
                for h in range(HEADS):
                    step(tt(k_tail(h), kT[:, h, :], k_tail(h), ALU.mult))
                settle()
                tt(kT[:, :, :], kT[:, :, :], eT[:, :, :], ALU.mult).then_inc(gla_ready, 1)
                skip(l, "g_kt")
                for b, q in (("g", 0), ("r", 1)):
                    if b == "r":
                        for name, dst, n_parts, scale in (("rq", o_tok, now, "xi"), ("rk", k_tok, parts_all(), "zeta")):
                            r, pt = take(l, name)
                            half = DK // 2
                            for rws, ts in n_parts:
                                for t in range(ts.start, ts.stop):
                                    src = heads(pt[rws, t, :], DK)
                                    d = heads(dst[rws, t, 0:HEADS * DK], DK)
                                    tmp = heads(o_tok[rws, t, HEADS * DK:D], half)
                                    cs = table("cos")[rws, t * half:(t + 1) * half].unsqueeze(1).broadcast_to([rws.stop, HEADS, half])
                                    sn = table("sin")[rws, t * half:(t + 1) * half].unsqueeze(1).broadcast_to([rws.stop, HEADS, half])
                                    t1, t2 = src[:, :, 0:half], src[:, :, half:DK]
                                    step(tt(d[:, :, 0:half], t1, cs, ALU.mult))
                                    step(tt(tmp[:, 0:HEADS, :], t2, sn, ALU.mult))
                                    step(tt(d[:, :, half:DK], t2, cs, ALU.mult))
                                    step(tt(tmp[:, HEADS:2 * HEADS, :], t1, sn, ALU.mult))
                                    settle()
                                    step(tt(d[:, :, 0:half], d[:, :, 0:half], tmp[:, 0:HEADS, :], ALU.subtract))
                                    step(tt(d[:, :, half:DK], d[:, :, half:DK], tmp[:, HEADS:2 * HEADS, :], ALU.add))
                                    settle()
                                    at = 0 if scale == "xi" else t * HEADS
                                    f = table(scale)[rws, at:at + HEADS].unsqueeze(2).broadcast_to([rws.stop, HEADS, DK])
                                    step(tt(d, d, f, ALU.mult))
                                    settle()
                            dve.sem_inc(dve_done, 1)
                        skip(l, "r_qt")
                        skip(l, "r_kt")
                        skip(l, "rv0")
                        skip(l, "rv1")
                    r, pt = take(l, f"{b}_sc")
                    for tile, n in ((0, CHUNK), (1, CHUNK), (2, META)):
                        rws = slice(0, TILE_ROWS[tile])
                        dst, src = sT[rws, tile, 0:HEADS * n], pt[rws, tile, 0:HEADS * n]
                        if b == "g":
                            ins = nc.vector.tensor_copy(dst, src)
                        else:
                            ins = tt(dst, src, table("mask_x" if n == CHUNK else "mask_m")[rws, :], ALU.mult)
                    if b == "g":
                        ins.then_inc(scores_out, 1)
                        dve.wait_ge(scores_out, l + 1)
                        dve.sem_inc(dve_done, 1)
                    else:
                        ins.then_inc(dve_done, 1)
                    for c in range(NCHUNK):
                        r, pt = take(l, f"{b}_o{c}")
                        if c == NCHUNK - 1:
                            dve.sem_inc(dve_done, 1)
                            continue
                        if c:
                            dve.wait_ge(dve_done, r)
                        for h in range(HEADS):
                            new = state[:, (c + 1) % 2, h * DV:(h + 1) * DV]
                            add = pt[:, h // 2, (h % 2) * DV:(h % 2 + 1) * DV]
                            if c == 0:
                                ins = nc.vector.tensor_copy(new, add)
                            else:
                                by = decay[:, h, c:c + 1] if b == "g" else float((1.0 - 2.0 ** (-5.0 - h)) ** CHUNK)
                                ins = stt(new, state[:, c % 2, h * DV:(h + 1) * DV], by, add, ALU.mult, ALU.add)
                        ins.then_inc(dve_done, 1)
                    dve.wait_ge(act_done, number[l, f"{b}_o{NCHUNK - 1}"] + 1)
                    normalise(o_tok, HEADS, DV, LN_EPS if b == "g" else GN_EPS, b == "r", now)
                    rows_ready()
                    for rws, ts in now:
                        for t in range(ts.start, ts.stop):
                            for h in range(HEADS):
                                o = o_tok[rws, t, h * DV:(h + 1) * DV]
                                if b == "g":
                                    step(stt(o, o, rstd[rws, t, h:h + 1], rows[rws, 0, 0:DV], ALU.mult, ALU.mult))
                                else:
                                    step(ts_(o, o, rstd[rws, t, h:h + 1], shift[rws, t, h:h + 1], ALU.mult, ALU.add))
                    settle()
                    if b == "r":
                        for op, i in ((ALU.mult, 0), (ALU.add, 1)):
                            for rws, ts in now:
                                for t in range(ts.start, ts.stop):
                                    step(tt(o_tok[rws, t, :], o_tok[rws, t, :], rows[rws, i, :], op))
                            settle()
                    dve.sem_inc(rows_used, 1)
                    for c in range(2):
                        r, pt = take(l, f"gr{c}" if b == "g" else f"rg{c}")
                        dve.wait_ge(act_done, r + 1)
                        for rws, ts in now:
                            o = o_tok[rws, ts, c * COLS:(c + 1) * COLS]
                            ins = tt(o, o, gs[rws, ts, :], ALU.mult)
                        ins.then_inc(dve_done, 1)
                    to_transposed(l, (f"{b}_t0", f"{b}_t1"), zT_hi, zT_lo)
                    skip(l, f"gt{'ab'[q]}0")
                    skip(l, f"gt{'ab'[q]}1")
                    sg = sgA if b == "g" else sgB
                    for c in range(2):
                        r, pt = take(l, f"p{'ab'[q]}{c}")
                        s = (slice(None), slice(4 * c, 4 * c + 4), width(l))
                        dve.wait_ge(act_done, number[l, f"gt{'ab'[q]}{c}"] + 1)
                        if b == "g":
                            tt(sg[s], pt[:, :, width(l)], sg[s], ALU.mult).then_inc(dve_done, 1)
                        else:
                            step(tt(sg[s], pt[:, :, width(l)], sg[s], ALU.mult))
                            settle()
                            ins = tt(sgA[s], sgA[s], sg[s], ALU.add)
                            if c == 0:
                                ins.then_inc(dve_done, 1)
                            else:
                                ins.then_inc(merged_ready, 1)
                                dve.wait_ge(merged_ready, l + 1)
                                dve.wait_ge(mhi_ready, l + 1)
                                a = (slice(None), slice(None), width(l))
                                tt(zT_lo[a], sgA[a], zT_hi[a].bitcast(F32), ALU.subtract).then_inc(dve_done, 1)

                def residual(names, count):
                    for c, name in enumerate(names):
                        r, pt = take(l, name)
                        for rws, ts in now:
                            x_ = h_tok[rws, ts, c * COLS:(c + 1) * COLS]
                            ins = stt(x_, x_, float(ALPHA), pt[rws, ts, :], ALU.mult, ALU.add)
                        ins.then_inc(dve_done, 1)
                        dve.wait_ge(dve_done, r + 1)
                    layer_norm(now)
                    dve.sem_inc(z_ready, 1)

                residual(("wo0", "wo1"), 2 * l + 1)
                to_transposed(l, ("h1t0", "h1t1"), hT_hi, hT_lo)
                if l == 0:
                    for j in range(6):
                        n = 4 if j < 5 else 2
                        skip(l, f"fg{j}")
                        r, pt = take(l, f"fu{j}")
                        dve.wait_ge(act_done, r)
                        if j:
                            dve.wait_ge(ahi_ready, j)
                        tt(aT_f[:, 0:n, :], pt[:, 0:n, 0:T], gT_s[:, 0:n, :], ALU.mult).then_inc(af_ready, 1)
                        dve.wait_ge(ahi_ready, j + 1)
                        dve.wait_ge(af_ready, j + 1)
                        tt(aT_lo[:, 4 * j:4 * j + n, :], aT_f[:, 0:n, :], aT_hi[:, 4 * j:4 * j + n, :].bitcast(F32),
                           ALU.subtract).then_inc(dve_done, 1)
                    residual(("fd0", "fd1"), 2)
                    to_transposed(0, ("h2t0", "h2t1"), hT_hi, hT_lo)
            if stop is not None:
                for t in range(2):
                    pass
                dve.sem_inc(m_acc, 1)
                return

            dve.wait_ge(act_seq_router, 1)
            tt(wr_lo[:, :, :], wr[:, :, :], wr_hi[:, :, :].bitcast(F32), ALU.subtract).then_inc(wr_lo_ready, 1)
            dve.wait_ge(xsplit_hi, 1)
            tt(x_lo[:, :, :], h_tok[:, 0:2, :], x_hi[:, :, :].bitcast(F32), ALU.subtract).then_inc(xsplit_lo, 1)
            dve.wait_ge(xsplit_lo, 1)
            step(ts_(h_tok[:, 0:2, :], h_tok[:, 0:2, :], float(ALPHA), None, ALU.mult))
            r, pt = take(1, "route")
            dve.wait_ge(act_done, r + 1)
            for t in range(2):
                step(nc.vector.tensor_reduce(tiny[:, t, 0:1], logit[:, t, :], AX.X, ALU.max))
            settle()
            ts_(tiny[:, :, 0:1], tiny[:, :, 0:1], -1.0, None, ALU.mult).then_inc(prob_ready, 1)
            dve.wait_ge(act_seq_router, 2)
            step(nc.vector.reciprocal(tiny[:, :, 1:2], tiny[:, :, 1:2]))
            settle()
            for t in range(2):
                step(ts_(prob[:, t, :], prob[:, t, :], tiny[:, t, 1:2], None, ALU.mult))
            settle()
            for t in range(2):
                step(nc.vector.max(top[:, t, :], prob[:, t, :]))
            settle()
            for t in range(2):
                step(nc.vector.max_index(top_at[:, t, :], top[:, t, :], prob[:, t, :]))
            step(tt(tiny[:, :, 2:3], top[:, :, 0:1], top[:, :, 1:2], ALU.add))
            settle()
            step(nc.vector.tensor_copy(top_f[:, :, :], top_at[:, :, 0:2]))
            step(nc.vector.reciprocal(tiny[:, :, 2:3], tiny[:, :, 2:3]))
            settle()
            for t in range(2):
                for i in range(2):
                    step(ts_(hit[:, t, i, :], table("iota")[:, 0:EXPERTS], top_f[:, t, i:i + 1], None, ALU.is_equal))
                step(ts_(top[:, t, 0:2], top[:, t, 0:2], tiny[:, t, 2:3], None, ALU.mult))
            settle()
            step(tt(sel[:, :, :], hit[:, :, 0, :], hit[:, :, 1, :], ALU.add))
            for t in range(2):
                step(ts_(comb[:, t, :], hit[:, t, 0, :], top[:, t, 0:1], None, ALU.mult))
            settle()
            for t in range(2):
                step(stt(comb[:, t, :], hit[:, t, 1, :], top[:, t, 1:2], comb[:, t, :], ALU.mult, ALU.add))
            settle()
            dve.sem_inc(sel_ready, 1)
            dve.sem_inc(dve_done, 1)
            r, pt = take(1, "rank")
            big = float(4 * P)
            step(ts_(rank[:, :, :], sel[:, :, :], -big, big, ALU.mult, ALU.add))
            settle()
            step(tt(rank[:, :, :], rank[:, :, :], pt[:, 0, 0:2 * EXPERTS].rearrange("p (t e) -> p t e", t=2), ALU.add))
            E = EXPERTS
            over, excl, num, hits = (plan_f[0:1, i * E:(i + 1) * E] for i in range(4))
            iota, ones = table("iota"), table("ones")
            step(ts_(over, pt[0:1, 1, 0:E], float(P), None, ALU.is_gt))
            settle()
            step(nc.vector.tensor_tensor_scan(excl, ones[0:1, 0:E], over, 0.0, ALU.mult, ALU.add))
            step(tt(num, over, iota[0:1, 0:E], ALU.mult))
            settle()
            for s in range(SPILLS):
                step(stt(hits, excl, float(s + 1), num, ALU.is_equal, ALU.mult))
                settle()
                step(nc.vector.tensor_reduce(plan_f[0:1, 4 * E + 1 + s:4 * E + 2 + s], hits, AX.X, ALU.add))
                settle()
            step(nc.vector.tensor_reduce(plan_f[0:1, 4 * E:4 * E + 1], over, AX.X, ALU.add))
            settle()
            nc.vector.tensor_copy(plan[:, :], plan_f[0:1, 4 * E:4 * E + 4]).then_inc(plan_ready, 1)
            dve.wait_ge(plan_ready, 1)
            dve.sem_inc(dve_done, 1)

            def expert(g, e, first_slot):
                u0, k0 = NS + g * UPG, g * JCH

                def lo(i, u):
                    at = NS + i
                    dve.wait_ge(hi_ready, u + 1)
                    dve.wait_ge(units_used, u - HALVES + 1)
                    tt(w_lo[:, at % HALVES, :], raw[:, at % RAW, :], w_hi[:, at % HALVES, :].bitcast(F32),
                       ALU.subtract).then_inc(lo_ready, 1)

                def turned(k):
                    dve.wait_ge(m_ahi, START + k + 1)
                    tt(ag_lo[:, :, :], ps[0][:, 2, :].rearrange("p (k s) -> p k s", s=P), ag_hi[:, :, :].bitcast(F32),
                       ALU.subtract).then_inc(m_alo, 1)

                def gated(k, u):
                    dve.wait_ge(units_used, u)
                    dve.wait_ge(m_silu, START + k + 1)
                    dve.wait_ge(m_t, START + k)
                    tt(a_sl[:, :], ps[0][:, 1, :], g_sl[:, :], ALU.mult).then_inc(m_a, 1)

                dve.wait_ge(m_sc, START + 2 * g)
                dve.wait_ge(m_acc, START + 2 * g)
                for t in range(2):
                    ins = ts_(S[:, t, :], iota[:, first_slot:first_slot + P], rank[:, t, bass.ds(e, 1)], None, ALU.is_equal)
                ins.then_inc(m_s, 1)
                for i in range(3):
                    lo(i, u0 + i)
                dve.wait_ge(m_xg_act, START + g + 1)
                tt(xg_lo[:, :, :], ps[1][:, 2:4, :].rearrange("p b (k s) -> p (b k) s", s=P), xg_hi[:, :, :].bitcast(F32),
                   ALU.subtract).then_inc(m_xg_dve, 1)
                lo(3, u0 + 3)
                gated(k0, u0 + 4)
                with dve.Fori(1, JCH) as j:
                    uj, k = u0 + (j * UPJ - 2), k0 + j
                    for i in range(4):
                        lo(4 + i, uj + i)
                    turned(k - 1)
                    for i in range(4, 6):
                        lo(4 + i, uj + i)
                    gated(k, uj + 4)
                for i in range(2):
                    lo(4 + i, u0 + UPG - 2 + i)
                turned(k0 + JCH - 1)
                dve.wait_ge(m_yhi, START + g + 1)
                stt(y_lo[:, :].rearrange("p (b n) -> p b n", b=2), ps[1][:, 0:2, :], slot_w[:, 0:1],
                    y_hi[:, :].bitcast(F32).rearrange("p (b n) -> p b n", b=2), ALU.mult, ALU.subtract).then_inc(m_ylo, 1)
                for t, src in ((0, ps[1][:, 2:4, :]), (1, ps[0][:, 2:4, :])):
                    dve.wait_ge(m_sc, START + 2 * g + t + 1)
                    h = h_tok[:, t, :].rearrange("p (b n) -> p b n", b=2)
                    tt(h, h, src, ALU.add).then_inc(m_acc, 1)

            for first in (m_s, m_xg_dve, m_a, m_alo, m_ylo, m_acc):
                dve.sem_inc(first, START)
            with dve.Fori(0, EXPERTS) as g:
                expert(g, g, 0)
            n_groups, spill = load_plan(dve)
            for s in range(SPILLS):
                with dve.If(n_groups > s):
                    expert(EXPERTS + s, spill[s], P)
                dve.end_ifs()
            dve.wait_ge(m_acc, START + n_groups * 2 + 2 * EXPERTS)
            layer_norm(parts(1))
            dve.sem_inc(z_ready, 1)


NAMES = ["x", "meta", "w_in", "b_gate", "gla_w_a2", "gla_b_a", "gla_norm_g", "ret_norm_g", "ret_norm_b", "w_pa", "w_pb",
         "w_o", "ln1_g", "ln1_b", "ffn_w_gate", "ffn_w_up", "ffn_w_down", "moe_w_router", "moe_w_gate", "moe_w_up",
         "moe_w_down", "ln2_g", "ln2_b"]


def kernel(**inputs):
    import numpy as _np
    import concourse.bacc as _bacc
    from concourse import mybir as _mybir
    from concourse.bass_utils import run_bass_kernel_spmd as _run

    nc = _bacc.Bacc("TRN2", target_bir_lowering=False, num_devices=1, dynamic_dma_scratch_size=4096)
    arrays, w = {}, {}
    for name in NAMES:
        a = _np.ascontiguousarray(inputs[name])
        arrays[f"in_{name}"] = a
        w[name] = nc.dram_tensor(f"in_{name}", a.shape, _mybir.dt.from_np(a.dtype), kind="ExternalInput").ap()
    tables, where = host_constants()
    arrays["in_tables"] = tables
    consts = nc.dram_tensor("in_tables", tables.shape, _mybir.dt.float32, kind="ExternalInput").ap()
    out = nc.dram_tensor("out", (1, SEQ, D), _mybir.dt.float32, kind="ExternalOutput").ap()
    trunk(nc, w, consts, where, out, STOP)
    r = _run(nc, [arrays], core_ids=[0])
    return r.results[0]["out"]


STOP = None
```

```python
from contextlib import ExitStack

import numpy as np

import concourse.bass as bass
from concourse import mybir

ALU = mybir.AluOpType
ACT = mybir.ActivationFunctionType
AX = mybir.AxisListType
F32 = mybir.dt.float32
F32R = mybir.dt.float32r
I32 = mybir.dt.int32
U32 = mybir.dt.uint32

P = 128
D = 1024
KT = D // P
SEQ, META = 256, 16
T = SEQ + META
CHUNK = 64
NCHUNK = 1 + SEQ // CHUNK
DEPTH = 2
HEADS, DK, DV = 4, 128, 256
RANK = 16
TAU = 16.0
DFF, DFFE = 2816, 3584
EXPERTS = 8
SPILLS = 3
ALPHA = (2 * DEPTH) ** 0.25
LN_EPS, GN_EPS = 1e-5, 1e-6
UNIT = 2048
COLS = 512
RAW, HALVES = 6, 3
JCH = DFFE // COLS
UPJ = 6
UPG = JCH * UPJ
START = 1

SIZES = dict(gq=512, gk=512, gv=1024, gr=1024, ga=RANK, rq=512, rk=512, rv=1024, rg=1024, gate_a=D, gate_b=D)
COL = {}
for _name, _size in SIZES.items():
    COL[_name] = sum(SIZES[k] for k in list(SIZES)[:len(COL)])

TILE_COL = [META, META + P, 0]
TILE_ROWS = [P, P, META]


def host_constants():
    f = np.float32
    p = np.arange(P)
    half = DK // 2
    inv = (f(10000.0) ** (-np.arange(half, dtype=f) / f(half))).astype(f)
    pos = np.stack([META + p, META + P + p, p], 1).astype(f)
    ang = (pos[:, :, None] * inv).astype(f)
    gamma = 1.0 - 2.0 ** (-5.0 - np.arange(HEADS))
    xi = gamma[None, :] ** (p[:, None] % CHUNK + 1.0)
    zeta_x = gamma[None, :] ** (CHUNK - 1.0 - p[:, None] % CHUNK)
    zeta_m = gamma[None, :] ** (META - 1.0 - p[:, None])
    zeta = np.stack([zeta_x, zeta_x, zeta_m], 1) * DK ** -0.5
    causal = (np.arange(CHUNK)[None, :] >= (p % CHUNK)[:, None])
    mask_x = causal[:, None, :] * gamma[None, :, None] ** -float(CHUNK)
    mask_m = causal[:, None, :META] * gamma[None, :, None] ** -float(META)
    restart = np.ones(T)
    restart[[0] + [META + CHUNK * c for c in range(4)]] = 0.0
    parts = dict(
        ident=np.eye(P), cos=np.cos(ang), sin=np.sin(ang), xi=xi, zeta=zeta, mask_x=mask_x, mask_m=mask_m,
        restart=np.broadcast_to(restart, (P, T)), before=(p[:, None] < p[None, :]), ones=np.ones((P, P)),
        iota=np.broadcast_to(np.arange(2 * P), (P, 2 * P)),
    )
    at, where, flat = 0, {}, []
    for name, a in parts.items():
        a = np.ascontiguousarray(a, dtype=f).reshape(P, -1)
        where[name] = (at, at + a.shape[1])
        at += a.shape[1]
        flat.append(a)
    return np.concatenate(flat, 1), where


def trunk(nc, w, consts, where, out, stop=None):
    ctx = ExitStack()
    with ctx:
        def sem(name):
            return ctx.enter_context(nc.semaphore(name))

        def sb(stack, name, shape, dt=F32):
            return stack.enter_context(nc.sbuf_tensor(name, shape, dt))

        raw = sb(ctx, "raw", [P, RAW, UNIT])
        w_hi = sb(ctx, "w_hi", [P, HALVES, UNIT], F32R)
        w_lo = sb(ctx, "w_lo", [P, HALVES, UNIT], F32R)
        h_tok = sb(ctx, "h_tok", [P, 3, D])
        hT_hi = sb(ctx, "hT_hi", [P, KT, T], F32R)
        hT_lo = sb(ctx, "hT_lo", [P, KT, T], F32R)
        rows = sb(ctx, "rows", [P, 2, D])
        tab = sb(ctx, "tab", [P, consts.shape[1]])
        a2 = sb(ctx, "a2", [RANK, DEPTH, HEADS * DK])
        b_a = sb(ctx, "b_a", [P, DEPTH, HEADS])
        b_g = sb(ctx, "b_g", [P, DEPTH, 2, KT])
        gla_g = sb(ctx, "gla_g", [P, DEPTH, DV // P])
        ret_gb = sb(ctx, "ret_gb", [P, DEPTH, 2, KT])
        stats = sb(ctx, "stats", [P, 3, 4, 6])
        mv = sb(ctx, "mv", [P, 3, 4, 2])
        rstd = sb(ctx, "rstd", [P, 3, 4])
        shift = sb(ctx, "shift", [P, 3, 4])

        def table(name, **dims):
            lo, hi = where[name]
            return tab[:, lo:hi]

        ident = table("ident")

        mix = ExitStack()
        o_tok = sb(mix, "o_tok", [P, 3, D])
        sgA = sb(mix, "sgA", [P, KT, T])
        gated = ExitStack()
        srT = sb(gated, "srT", [P, KT, T])
        gated.close()
        mT_hi = sb(mix, "mT_hi", [P, 4, T], F32R)
        mT_lo = sb(mix, "mT_lo", [P, 4, T], F32R)
        vlife = ExitStack()
        v_tok = sb(vlife, "v_tok", [P, 3, D])
        attn = ExitStack()
        qT = sb(attn, "qT", [P, HEADS, T])
        kT = sb(attn, "kT", [P, HEADS, T])
        eT = sb(attn, "eT", [P, HEADS, T])
        fT = sb(attn, "fT", [P, HEADS, T])
        bT = sb(attn, "bT", [P, HEADS, T])
        k_tok = sb(attn, "k_tok", [P, 3, HEADS * DK])
        state = srT[:, :, :].rearrange("p k t -> p (k t)")[:, 0:2 * HEADS * DV].rearrange("p (a n) -> p a n", a=2)
        sT = sb(attn, "sT", [P, 3, HEADS * CHUNK])
        gaT = sgA[0:RANK, 0, :]
        decay = sb(attn, "decay", [P, HEADS, NCHUNK])
        attn.close()
        zT_hi = sb(vlife, "zT_hi", [P, KT, T], F32R)
        zT_lo = sb(vlife, "zT_lo", [P, KT, T], F32R)
        vlife.close()
        m_hi = (mT_hi[:, :, :], zT_hi[:, 4:8, :])
        m_lo = (mT_lo[:, :, :], zT_lo[:, 4:8, :])
        sgB = sb(mix, "sgB", [P, KT, T])
        mix.close()

        ffn = ExitStack()
        aT_hi = sb(ffn, "aT_hi", [P, DFF // P, T], F32R)
        aT_lo = sb(ffn, "aT_lo", [P, DFF // P, T], F32R)
        gT_s = sb(ffn, "gT_s", [P, 4, T])
        aT_f = sb(ffn, "aT_f", [P, 4, T])
        ffn.close()

        moe = ExitStack()
        x_hi = sb(moe, "x_hi", [P, 2, D], F32R)
        x_lo = sb(moe, "x_lo", [P, 2, D], F32R)
        S = sb(moe, "S", [P, 2, P], F32R)
        ST = sb(moe, "ST", [P, 2, P], F32R)
        xg_hi = sb(moe, "xg_hi", [P, KT, P], F32R)
        xg_lo = sb(moe, "xg_lo", [P, KT, P], F32R)
        g_sl = sb(moe, "g_sl", [P, COLS])
        a_sl = sb(moe, "a_sl", [P, COLS])
        ag_hi = sb(moe, "ag_hi", [P, 4, P], F32R)
        ag_lo = sb(moe, "ag_lo", [P, 4, P], F32R)
        y_hi = sb(moe, "y_hi", [P, D], F32R)
        y_lo = sb(moe, "y_lo", [P, D], F32R)
        wr = sb(moe, "wr", [P, KT, EXPERTS])
        wr_hi = sb(moe, "wr_hi", [P, KT, EXPERTS], F32R)
        wr_lo = sb(moe, "wr_lo", [P, KT, EXPERTS], F32R)
        logit = sb(moe, "logit", [P, 2, EXPERTS])
        prob = sb(moe, "prob", [P, 2, EXPERTS])
        top = sb(moe, "top", [P, 2, 8])
        top_at = sb(moe, "top_at", [P, 2, 8], U32)
        top_f = sb(moe, "top_f", [P, 2, 2])
        hit = sb(moe, "hit", [P, 2, 2, EXPERTS])
        sel = sb(moe, "sel", [P, 2, EXPERTS])
        comb = sb(moe, "comb", [P, 2, EXPERTS])
        rank = sb(moe, "rank", [P, 2, EXPERTS + 1])
        tiny = sb(moe, "tiny", [P, 2, 4])
        slot_w = sb(moe, "slot_w", [P, 1])
        plan_f = sb(moe, "plan_f", [1, 8 * EXPERTS])
        plan = sb(moe, "plan", [1, 4], I32)
        moe.close()

        ps = [ctx.enter_context(nc.psum_tensor(f"ps{i}", [P, 4, 512], F32)) for i in range(2)]

        raw_landed = [sem(f"raw_landed{i}") for i in range(RAW)]
        hi_ready = sem("hi_ready")
        lo_ready = sem("lo_ready")
        units_used = sem("units_used")
        set_full = sem("set_full")
        act_done = sem("act_done")
        dve_done = sem("dve_done")
        act_seq = sem("act_seq")
        dve_seq = sem("dve_seq")
        zb_ready, sp_ready, b_ready, d_ready, e_ready = (sem(n) for n in ("zb_ready", "sp_ready", "b_ready", "d_ready", "e_ready"))
        gla_ready = sem("gla_ready")
        scores_out = sem("scores_out")
        masked = sem("masked")
        var_ready, std_ready = sem("var_ready"), sem("std_ready")
        rot_ready = sem("rot_ready")
        z_ready = sem("z_ready")
        merged_ready = sem("merged_ready")
        af_ready, ahi_ready = sem("af_ready"), sem("ahi_ready")
        o_ready = sem("o_ready")
        zf_ready = sem("zf_ready")
        rows_landed, rows_used = sem("rows_landed"), sem("rows_used")
        small_landed, x_landed = sem("small_landed"), sem("x_landed")
        stored = sem("stored")
        xsplit_hi, xsplit_lo = sem("xsplit_hi"), sem("xsplit_lo")
        wrs = sem("wrs")
        prob_ready = sem("prob_ready")
        sel_ready = sem("sel_ready")
        plan_ready = sem("plan_ready")
        m_s, m_st_full, m_st, m_xg_full, m_xg_act, m_xg_dve = sem("m_s"), sem("m_st_full"), sem("m_st"), sem("m_xg_full"), sem("m_xg_act"), sem("m_xg_dve")
        m_zero = sem("m_zero")
        m_silu, m_a = sem("m_silu"), sem("m_a")
        m_t, m_ahi, m_alo = sem("m_t"), sem("m_ahi"), sem("m_alo")
        m_yhi, m_ylo, m_sc, m_acc = sem("m_yhi"), sem("m_ylo"), sem("m_sc"), sem("m_acc")

        stream = []

        def add_cols(src, c0, cols=COLS):
            for k in range(0, KT, 4):
                stream.append(("cols", src, k, 4, c0, cols))

        for l in range(DEPTH):
            w_in = w["w_in"][l]
            def pair(src, c0):
                add_cols(src, c0)
                add_cols(src, c0 + COLS)

            add_cols(w_in, COL["gk"])
            add_cols(w_in, COL["gq"])
            add_cols(w_in, COL["ga"], P)
            pair(w_in, COL["gv"])
            add_cols(w_in, COL["gate_a"])
            pair(w_in, COL["gr"])
            add_cols(w_in, COL["gate_a"] + COLS)
            add_cols(w_in, COL["rq"])
            add_cols(w_in, COL["rk"])
            pair(w["w_pa"][l], 0)
            pair(w_in, COL["rv"])
            pair(w_in, COL["rg"])
            pair(w_in, COL["gate_b"])
            pair(w["w_pb"][l], 0)
            pair(w["w_o"][l], 0)
            if l == 0:
                for c0 in range(0, DFF, COLS):
                    n = min(COLS, DFF - c0)
                    add_cols(w["ffn_w_gate"][0], c0, n)
                    add_cols(w["ffn_w_up"][0], c0, n)
                for c in range(2):
                    for k in range(0, DFF // P, 4):
                        stream.append(("cols", w["ffn_w_down"][0], k, min(4, DFF // P - k), c * COLS, COLS))
        NS = len(stream)

        def shape_of(u):
            return (stream[u][3], stream[u][5])

        def unit(buf, slot, k, n):
            return buf[:, slot, 0:k * n].rearrange("p (k n) -> p k n", k=k)

        def landed(eng, u):
            eng.wait_ge(raw_landed[u % RAW], 16 * (u // RAW + 1))

        def hi_unit(act, u):
            landed(act, u)
            if u >= HALVES:
                act.wait_ge(units_used, u - HALVES + 1)
            k, n = shape_of(u)
            nc.scalar.activation(w_hi[:, u % HALVES, 0:k * n], raw[:, u % RAW, 0:k * n], ACT.Copy).then_inc(hi_ready, 1)

        def lo_unit(dve, u):
            dve.wait_ge(hi_ready, u + 1)
            if u >= HALVES:
                dve.wait_ge(units_used, u - HALVES + 1)
            k, n = shape_of(u)
            nc.vector.tensor_tensor(w_lo[:, u % HALVES, 0:k * n], raw[:, u % RAW, 0:k * n],
                                    w_hi[:, u % HALVES, 0:k * n].bitcast(F32), ALU.subtract).then_inc(lo_ready, 1)

        class Splitter:

            def __init__(self, eng, split):
                self.eng, self.split, self.next = eng, split, 0

            def upto(self, u):
                while self.next < min(u, NS):
                    self.split(self.eng, self.next)
                    self.next += 1

        sets = []

        def plan_sets():
            u = 0
            for l in range(DEPTH):
                def weights(name, units):
                    nonlocal u
                    u += units
                    sets.append((l, name, u, True))

                def local(name):
                    sets.append((l, name, u, False))
                if l == 0:
                    local("ht0"); local("ht1")
                weights("gk", 2); weights("gq", 2); weights("ga", 2); local("z")
                weights("gv0", 2); weights("gv1", 2); weights("gta0", 2)
                local("g_kt"); local("g_sc")
                for c in range(NCHUNK):
                    local(f"g_o{c}")
                weights("gr0", 2); weights("gr1", 2); weights("gta1", 2)
                local("g_t0"); local("g_t1")
                weights("rq", 2); weights("rk", 2)
                weights("pa0", 2); weights("pa1", 2); local("r_qt"); local("r_kt")
                weights("rv0", 2); weights("rv1", 2); local("r_sc")
                for c in range(NCHUNK):
                    local(f"r_o{c}")
                weights("rg0", 2); weights("rg1", 2); weights("gtb0", 2)
                local("r_t0"); local("r_t1")
                weights("gtb1", 2)
                weights("pb0", 2); weights("pb1", 2)
                weights("wo0", 2); weights("wo1", 2); local("wot0"); local("wot1")
                local("h1t0"); local("h1t1")
                if l == 0:
                    for j in range(6):
                        weights(f"fg{j}", 2); weights(f"fu{j}", 2)
                    weights("fd0", 6); weights("fd1", 6); local("fdt0"); local("fdt1")
                    local("h2t0"); local("h2t1")
                else:
                    local("route"); local("rank")
            assert u == NS

        plan_sets()
        number = {(l, name): r for r, (l, name, _, _) in enumerate(sets)}
        ends = [u for _, _, u, _ in sets]
        NSETS = len(sets)

        def full(eng, r):
            if sets[r][3]:
                eng.wait_ge(units_used, ends[r])
            else:
                eng.wait_ge(set_full, sum(not s[3] for s in sets[:r + 1]))

        def bank(r):
            return ps[r % 2]

        def parts(l):
            return [(slice(0, P), slice(0, 2))] + ([(slice(0, META), slice(2, 3))] if l == 0 else [])

        def parts_all():
            return parts(0)

        def width(l):
            return slice(0, T) if l == 0 else slice(META, T)

        def chunk_cols(c):
            return slice(0, META) if c == 0 else slice(META + CHUNK * (c - 1), META + CHUNK * c)

        def chunk_rows(c):
            if c == 0:
                return 2, slice(0, META)
            return (c - 1) // 2, slice(CHUNK * ((c - 1) % 2), CHUNK * ((c - 1) % 2) + CHUNK)

        act_seq_router = sem("act_seq_router")
        wr_lo_ready = sem("wr_lo_ready")

        def k_tail(h):
            return o_tok[:, h // 2, (h % 2) * T:(h % 2 + 1) * T]

        def load_plan(eng):
            n = eng.value_load(plan[0:1, 0:1], min_val=0, max_val=SPILLS)
            which = [eng.value_load(plan[0:1, 1 + s:2 + s], min_val=0, max_val=EXPERTS - 1) for s in range(SPILLS)]
            return n, which

        block = ctx.enter_context(nc.Block())

        @block.sync
        def _(sp):
            def load(u):
                kind, src, k, kn, c0, n = stream[u]
                if u >= RAW:
                    sp.wait_ge(lo_ready, u - RAW + 1)
                sp.dma_start(unit(raw, u % RAW, kn, n),
                             src[k * P:(k + kn) * P, c0:c0 + n].rearrange("(k p) n -> p k n", p=P)).then_inc(raw_landed[u % RAW], 16)

            for u in range(NS):
                load(u)
            if stop is not None:
                return

            def load_expert(slot, u, src):
                sp.wait_ge(lo_ready, u - RAW + 1)
                sp.dma_start(raw[:, slot, :].rearrange("p (k n) -> p k n", k=src.shape[1]), src).then_inc(raw_landed[slot], 16)

            def gate_up(e, name, k, c0):
                a = w[name][0][bass.ds(e, 1), k * P:(k + 4) * P, bass.ds(c0, COLS)]
                return a.rearrange("e (k p) n -> p (e k) n", p=P)

            def down(e, r0):
                a = w["moe_w_down"][0][bass.ds(e, 1), bass.ds(r0, 2 * P), :]
                return a.rearrange("e (k p) n -> p (e k) n", p=P)

            def expert(g, e):
                u0 = NS + g * UPG
                at = NS % RAW
                for i, (name, k) in enumerate((("moe_w_gate", 0), ("moe_w_gate", 4), ("moe_w_up", 0), ("moe_w_up", 4))):
                    load_expert((at + i) % RAW, u0 + i, gate_up(e, name, k, 0))
                with sp.Fori(1, JCH) as j:
                    uj = u0 + (j * UPJ - 2)
                    for i, (name, k) in enumerate((("moe_w_gate", 0), ("moe_w_gate", 4), ("moe_w_up", 0), ("moe_w_up", 4))):
                        load_expert((at + 4 + i) % RAW, uj + i, gate_up(e, name, k, j * COLS))
                    for i in range(2):
                        load_expert((at + 8 + i) % RAW, uj + 4 + i, down(e, j * COLS - COLS + i * 2 * P))
                for i in range(2):
                    load_expert((at + 4 + i) % RAW, u0 + UPG - 2 + i, down(e, DFFE - COLS + i * 2 * P))

            with sp.Fori(0, EXPERTS) as g:
                expert(g, g)
            sp.wait_ge(plan_ready, 1)
            n_groups, spill = load_plan(sp)
            for s in range(SPILLS):
                with sp.If(n_groups > s):
                    expert(EXPERTS + s, spill[s])
                sp.end_ifs()
            sp.wait_ge(z_ready, 4)
            for t in range(2):
                sp.dma_start(out[0, t * P:(t + 1) * P, :], h_tok[:, t, :]).then_inc(stored, 16)
            sp.wait_ge(stored, 32)

        @block.gpsimd
        def _(pool):
            pool.dma_start(tab[:, :], consts[:, :]).then_inc(small_landed, 16)
            for l in range(DEPTH):
                pool.dma_start(a2[:, l, :], w["gla_w_a2"][l]).then_inc(small_landed, 16)
            with nc.allow_non_contiguous_dma(reason="a few parameters, one per partition"):
                for l in range(DEPTH):
                    pool.dma_start(b_a[:, l, :], w["gla_b_a"][l].rearrange("(h p) -> p h", p=P)).then_inc(small_landed, 16)
                    pool.dma_start(gla_g[:, l, :], w["gla_norm_g"][l].rearrange("(k p) -> p k", p=P)).then_inc(small_landed, 16)
                    for s in range(2):
                        pool.dma_start(b_g[:, l, s, :], w["b_gate"][l, s].rearrange("(k p) -> p k", p=P)).then_inc(small_landed, 16)
                        pool.dma_start(ret_gb[:, l, s, :], w[("ret_norm_g", "ret_norm_b")[s]][l].rearrange("(k p) -> p k", p=P)).then_inc(small_landed, 16)

            loads = 0

            def load_rows(srcs):
                nonlocal loads
                if loads:
                    pool.wait_ge(rows_used, loads)
                for i, a in enumerate(srcs):
                    pool.dma_start(rows[:, i, 0:a.shape[0]], a.partition_broadcast(P)).then_inc(rows_landed, 16)
                loads += 1

            for l in range(DEPTH):
                pool.wait_ge(scores_out, l + 1)
                for tile, lo, hi in ((0, 0, CHUNK), (0, CHUNK, P), (1, 0, CHUNK), (1, CHUNK, P), (2, 0, META)):
                    n = hi - lo
                    a = sT[lo:hi, tile, 0:HEADS * n].rearrange("p (h i) -> p h i", h=HEADS)
                    pool.affine_select(out=a, in_=a, compare_op=ALU.is_ge, fill=0.0, base=0,
                                       pattern=[[0, HEADS], [1, n]], channel_multiplier=-1).then_inc(masked, 1)
                load_rows([w["ln1_g"][l], w["ln1_b"][l]])
                if l == 1:
                    full(pool, number[1, "wo1"])
                    pool.dma_start(wr[:, :, :], w["moe_w_router"][0].rearrange("(k p) e -> p k e", p=P)).then_inc(wrs, 16)
                load_rows([w["ln2_g"][l], w["ln2_b"][l]])

        @block.tensor
        def _(pe):
            used = 0

            def mm3(dst, l_hi, l_lo, r_hi, r_lo, start, stop):
                nc.tensor.matmul(dst, l_lo, r_hi, start=start, stop=False)
                nc.tensor.matmul(dst, l_hi, r_lo, start=False, stop=False)
                return nc.tensor.matmul(dst, l_hi, r_hi, start=False, stop=stop)

            def begin(l, name):
                r = number[l, name]
                if r >= 2:
                    pe.wait_ge(act_done, r - 1)
                    pe.wait_ge(dve_done, r - 1)
                return bank(r)

            def after(l, name):
                pe.wait_ge(act_done, number[l, name] + 1)
                pe.wait_ge(dve_done, number[l, name] + 1)

            def rowtile(x, k):
                return x[k // 4][:, k % 4, :] if type(x) is tuple else x[:, k, :]

            def next_unit():
                nonlocal used
                pe.wait_ge(lo_ready, used + 1)
                k, n = shape_of(used)
                s = used % HALVES
                used += 1
                return unit(w_hi, s, k, n), unit(w_lo, s, k, n), k, n

            def feature_major(l, name, x_hi_, x_lo_, cols, depth=KT, made_by=None):
                pt = begin(l, name)
                for k0 in range(0, depth, 4):
                    u_hi, u_lo, kn, n = next_unit()
                    if made_by:
                        after(l, made_by[k0 // 4])
                    for k in range(kn):
                        for m in range(n // P):
                            last = mm3(pt[:, m, cols], u_hi[:, k, m * P:(m + 1) * P], u_lo[:, k, m * P:(m + 1) * P],
                                       rowtile(x_hi_, k0 + k)[:, cols], rowtile(x_lo_, k0 + k)[:, cols],
                                       start=(k0 + k == 0), stop=(k0 + k == depth - 1))
                    last.then_inc(units_used, 1)

            def fill(last):
                last.then_inc(set_full, 1)

            def token_major(l, name, x_hi_, x_lo_, tiles):
                pt = begin(l, name)
                for k0 in (0, 4):
                    u_hi, u_lo, kn, n = next_unit()
                    for k in range(kn):
                        for t in range(tiles):
                            c = TILE_COL[t]
                            last = mm3(pt[:, t, 0:n], x_hi_[:, k0 + k, c:c + P], x_lo_[:, k0 + k, c:c + P],
                                       u_hi[:, k, :], u_lo[:, k, :], start=(k0 + k == 0), stop=(k0 + k == KT - 1))
                    last.then_inc(units_used, 1)

            def transposes(l, names, src, tiles):
                for i, name in enumerate(names):
                    pt = begin(l, name)
                    for k in range(4):
                        for t in range(tiles):
                            c, n, f = TILE_COL[t], TILE_ROWS[t], (4 * i + k) * P
                            last = nc.tensor.transpose(pt[:, k, c:c + n], src[0:n, t, f:f + P], ident[0:n, 0:n])
                    fill(last)

            def back(l, names, sources, cols, tiles):
                for (name, made_by), src in zip(names, sources):
                    after(l, made_by)
                    pt = begin(l, name)
                    for k in range(4):
                        for t in range(tiles):
                            c, n = TILE_COL[t], TILE_ROWS[t]
                            last = nc.tensor.transpose(pt[0:n, t, k * P:(k + 1) * P], src[:, k, c:c + n], ident)
                    fill(last)

            def attention(l, b):
                pt = begin(l, f"{b}_sc")
                for c in range(NCHUNK):
                    tile, rws = chunk_rows(c)
                    n = rws.stop - rws.start
                    for h in range(HEADS):
                        last = nc.tensor.matmul(pt[rws, tile, h * n:(h + 1) * n], kT[:, h, chunk_cols(c)], qT[:, h, chunk_cols(c)],
                                                start=True, stop=True)
                fill(last)
                for c in range(NCHUNK):
                    tile, rws = chunk_rows(c)
                    n = rws.stop - rws.start
                    pt = begin(l, f"{b}_o{c}")
                    if c < NCHUNK - 1:
                        for h in range(HEADS):
                            last = nc.tensor.matmul(pt[:, h // 2, (h % 2) * DV:(h % 2 + 1) * DV], k_tok[rws, tile, h * DK:(h + 1) * DK],
                                                    v_tok[rws, tile, h * DV:(h + 1) * DV], start=True, stop=True)
                    if c == 0:
                        if b == "g":
                            pe.wait_ge(masked, 5 * (l + 1))
                        else:
                            after(l, "r_sc")
                    if c >= 1:
                        pe.wait_ge(dve_done, number[l, f"{b}_o{c - 1}"] + 1)
                    if c or l == 0:
                        for h in range(HEADS):
                            dst = pt[rws, 2 + h // 2, (h % 2) * DV:(h % 2 + 1) * DV]
                            last = nc.tensor.matmul(dst, sT[rws, tile, h * n:(h + 1) * n], v_tok[rws, tile, h * DV:(h + 1) * DV],
                                                    start=True, stop=(c == 0))
                            if c:
                                last = nc.tensor.matmul(dst, qT[:, h, chunk_cols(c)], state[:, c % 2, h * DV:(h + 1) * DV],
                                                        start=False, stop=True)
                    fill(last)

            pe.wait_ge(small_landed, 16 * (1 + 7 * DEPTH))
            pe.wait_ge(x_landed, 48)
            transposes(0, ("ht0", "ht1"), h_tok, 3)
            for l in range(DEPTH):
                tiles = len(parts(l)) + 1
                cols = width(l)
                after(l, "ht1") if l == 0 else after(0, "h2t1")
                feature_major(l, "gk", hT_hi, hT_lo, slice(0, T))
                feature_major(l, "gq", hT_hi, hT_lo, slice(0, T))
                feature_major(l, "ga", hT_hi, hT_lo, slice(0, T))
                after(l, "ga")
                pt = begin(l, "z")
                for h in range(HEADS):
                    last = nc.tensor.matmul(pt[:, h, 0:T], a2[:, l, h * DK:(h + 1) * DK], gaT, start=True, stop=True)
                fill(last)
                token_major(l, "gv0", hT_hi, hT_lo, 3)
                token_major(l, "gv1", hT_hi, hT_lo, 3)
                feature_major(l, "gta0", hT_hi, hT_lo, cols)
                pt = begin(l, "g_kt")
                pe.wait_ge(gla_ready, l + 1)
                for t in range(3):
                    c, n = TILE_COL[t], TILE_ROWS[t]
                    for h in range(HEADS):
                        last = nc.tensor.transpose(pt[0:n, t, h * DK:(h + 1) * DK], k_tail(h)[:, c:c + n], ident)
                fill(last)
                after(l, "g_kt")
                attention(l, "g")
                for c in range(2):
                    feature_major(l, f"gr{c}", hT_hi, hT_lo, cols)
                feature_major(l, "gta1", hT_hi, hT_lo, cols)
                pe.wait_ge(o_ready, 2 * l + 1)
                transposes(l, ("g_t0", "g_t1"), o_tok, tiles)
                token_major(l, "rq", hT_hi, hT_lo, tiles)
                token_major(l, "rk", hT_hi, hT_lo, 3)
                for c in range(2):
                    feature_major(l, f"pa{c}", zT_hi, zT_lo, cols, made_by=("g_t0", "g_t1"))
                for name, src, n_t in (("r_qt", o_tok, tiles), ("r_kt", k_tok, 3)):
                    after(l, {"r_qt": "rq", "r_kt": "rk"}[name])
                    pt = begin(l, name)
                    for h in range(HEADS):
                        for t in range(n_t):
                            c, n = TILE_COL[t], TILE_ROWS[t]
                            last = nc.tensor.transpose(pt[:, h, c:c + n], src[0:n, t, h * DK:(h + 1) * DK], ident[0:n, 0:n])
                    fill(last)
                token_major(l, "rv0", hT_hi, hT_lo, 3)
                token_major(l, "rv1", hT_hi, hT_lo, 3)
                after(l, "rv1")
                attention(l, "r")
                for c in range(2):
                    feature_major(l, f"rg{c}", hT_hi, hT_lo, cols)
                feature_major(l, "gtb0", hT_hi, hT_lo, cols)
                pe.wait_ge(o_ready, 2 * l + 2)
                transposes(l, ("r_t0", "r_t1"), o_tok, tiles)
                feature_major(l, "gtb1", hT_hi, hT_lo, cols)
                for c in range(2):
                    feature_major(l, f"pb{c}", zT_hi, zT_lo, cols, made_by=("r_t0", "r_t1"))
                for c in range(2):
                    feature_major(l, f"wo{c}", m_hi, m_lo, cols, made_by=("pb0", "pb1"))
                back(l, (("wot0", "wo0"), ("wot1", "wo1")), (sgA[:, 0:4, :], sgA[:, 4:8, :]), cols, tiles)
                pe.wait_ge(z_ready, 2 * l + 1)
                transposes(l, ("h1t0", "h1t1"), h_tok, tiles)
                after(l, "h1t1")
                if l == 0:
                    for j in range(6):
                        feature_major(l, f"fg{j}", hT_hi, hT_lo, slice(0, T))
                        feature_major(l, f"fu{j}", hT_hi, hT_lo, slice(0, T))
                    for c in range(2):
                        feature_major(l, f"fd{c}", aT_hi, aT_lo, slice(0, T), DFF // P, [f"fu{j}" for j in range(6)])
                    back(l, (("fdt0", "fd0"), ("fdt1", "fd1")), (gT_s, aT_f), slice(0, T), 3)
                    pe.wait_ge(z_ready, 2)
                    transposes(l, ("h2t0", "h2t1"), h_tok, 3)
            if stop is not None:
                return

            pt = begin(1, "route")
            pe.wait_ge(act_seq_router, 1)
            pe.wait_ge(wr_lo_ready, 1)
            for t in range(2):
                c = TILE_COL[t]
                for k in range(KT):
                    last = mm3(pt[:, 0, t * EXPERTS:(t + 1) * EXPERTS], hT_hi[:, k, c:c + P], hT_lo[:, k, c:c + P],
                               wr_hi[:, k, :], wr_lo[:, k, :], start=(k == 0), stop=(k == KT - 1))
            fill(last)
            pt = begin(1, "rank")
            pe.wait_ge(sel_ready, 1)
            before, ones = table("before"), table("ones")
            nc.tensor.matmul(pt[:, 0, 0:EXPERTS], before, sel[:, 0, :], start=True, stop=True)
            nc.tensor.matmul(pt[:, 0, EXPERTS:2 * EXPERTS], before, sel[:, 1, :], start=True, stop=False)
            nc.tensor.matmul(pt[:, 0, EXPERTS:2 * EXPERTS], ones, sel[:, 0, :], start=False, stop=True)
            nc.tensor.matmul(pt[0:1, 1, 0:EXPERTS], ones[:, 0:1], sel[:, 0, :], start=True, stop=False)
            last = nc.tensor.matmul(pt[0:1, 1, 0:EXPERTS], ones[:, 0:1], sel[:, 1, :], start=False, stop=True)
            fill(last)
            pe.wait_ge(act_done, NSETS)
            pe.wait_ge(dve_done, NSETS)
            pe.wait_ge(xsplit_lo, 1)

            G_, U_ = ps[0][:, 0, :], ps[0][:, 1, :]
            TB, MISC = ps[0][:, 2, :], ps[0][:, 3, :]
            Y = ps[1][:, 0:2, :]
            X = ps[1][:, 2:4, :]

            def expert_unit(at, u):
                pe.wait_ge(lo_ready, u + 1)
                return w_hi[:, at % HALVES, :], w_lo[:, at % HALVES, :]

            def gate_or_up(dst, at, u):
                for i in range(2):
                    u_hi, u_lo = expert_unit(at + i, u + i)
                    for k in range(4):
                        last = mm3(dst, xg_hi[:, 4 * i + k, :], xg_lo[:, 4 * i + k, :],
                                   u_hi[:, k * COLS:(k + 1) * COLS], u_lo[:, k * COLS:(k + 1) * COLS],
                                   start=(i == 0 and k == 0), stop=(i == 1 and k == 3))
                    last.then_inc(units_used, 1)

            def turn(k):
                pe.wait_ge(m_a, START + k + 1)
                pe.wait_ge(m_alo, START + k)
                for i in range(4):
                    last = nc.tensor.transpose(TB[:, i * P:(i + 1) * P], a_sl[:, i * P:(i + 1) * P], ident)
                last.then_inc(m_t, 1)

            def down(at, u, k, first, final):
                pe.wait_ge(m_alo, START + k + 1)
                for i in range(2):
                    u_hi, u_lo = expert_unit(at + i, u + i)
                    for kk in range(2):
                        for q in range(2):
                            o = kk * D + q * COLS
                            last = nc.tensor.matmul(Y[:, q, :], ag_lo[:, 2 * i + kk, :], u_hi[:, o:o + COLS],
                                                    start=first and i == 0 and kk == 0, stop=False)
                            nc.tensor.matmul(Y[:, q, :], ag_hi[:, 2 * i + kk, :], u_lo[:, o:o + COLS], start=False, stop=False)
                            last = nc.tensor.matmul(Y[:, q, :], ag_hi[:, 2 * i + kk, :], u_hi[:, o:o + COLS],
                                                    start=False, stop=final and i == 1 and kk == 1)
                    last.then_inc(units_used, 1)

            def gather(n):
                pe.wait_ge(m_s, START + n + 1)
                pe.wait_ge(m_acc, START + 2 * n)
                for k in range(KT):
                    dst = X[:, k // 4, (k % 4) * P:(k % 4 + 1) * P]
                    for t in range(2):
                        nc.tensor.matmul(dst, x_lo[:, t, k * P:(k + 1) * P], S[:, t, :], start=(t == 0), stop=False)
                        last = nc.tensor.matmul(dst, x_hi[:, t, k * P:(k + 1) * P], S[:, t, :], start=False, stop=(t == 1))
                last.then_inc(m_xg_full, 1)

            def slots(g, e):
                pe.wait_ge(m_acc, START + 2 * g + 2)
                for t in range(2):
                    nc.tensor.matmul(MISC[:, 0:1], S[:, t, :].bitcast(F32), comb[:, t, bass.ds(e, 1)], start=(t == 0), stop=(t == 1))
                for t in range(2):
                    last = nc.tensor.transpose(MISC[:, (t + 1) * P:(t + 2) * P], S[:, t, :].bitcast(F32), ident)
                last.then_inc(m_st_full, 1)

            def scatter(n):
                pe.wait_ge(m_ylo, START + n + 1)
                pe.wait_ge(m_yhi, START + n + 1)
                pe.wait_ge(m_st, START + n)
                for t, dst in ((0, X), (1, ps[0][:, 2:4, :])):
                    for q in range(2):
                        nc.tensor.matmul(dst[:, q, :], ST[:, t, :], y_lo[:, q * COLS:(q + 1) * COLS], start=True, stop=False)
                        last = nc.tensor.matmul(dst[:, q, :], ST[:, t, :], y_hi[:, q * COLS:(q + 1) * COLS], start=False, stop=True)
                    last.then_inc(m_sc, 1)

            def expert(g, e, overlapped):
                u0, k0, at = NS + g * UPG, g * JCH, NS
                n = g if overlapped else g + 1
                pe.wait_ge(m_xg_act, START + n + 1)
                pe.wait_ge(m_xg_dve, START + n + 1)
                pe.wait_ge(m_silu, START + k0)
                gate_or_up(G_, at, u0)
                if overlapped:
                    scatter(g)
                pe.wait_ge(m_a, START + k0)
                gate_or_up(U_, at + 2, u0 + 2)
                slots(g, e)

                def chunk(j, first):
                    uj, k = u0 + (j * UPJ - 2), k0 + j
                    pe.wait_ge(m_silu, START + k)
                    gate_or_up(G_, at + 4, uj)
                    turn(k - 1)
                    gate_or_up(U_, at + 6, uj + 2)
                    if first:
                        pe.wait_ge(m_ylo, START + g + 1)
                    down(at + 8, uj + 4, k - 1, first, False)

                chunk(1, True)
                with pe.Fori(2, JCH) as j:
                    chunk(j, False)
                if overlapped:
                    gather(g + 1)
                turn(k0 + JCH - 1)
                down(at + 4, u0 + UPG - 2, k0 + JCH - 1, False, True)

            for first in (m_t, m_sc, m_xg_full, m_st_full):
                pe.sem_inc(first, START)
            gather(0)
            with pe.Fori(0, EXPERTS) as g:
                expert(g, g, True)
            scatter(EXPERTS)
            pe.wait_ge(plan_ready, 1)
            n_groups, spill = load_plan(pe)
            for s in range(SPILLS):
                with pe.If(n_groups > s):
                    gather(EXPERTS + s + 1)
                    expert(EXPERTS + s, spill[s], False)
                    scatter(EXPERTS + s + 1)
                pe.end_ifs()

        @block.scalar
        def _(act):
            seq = 0

            def step(ins):
                nonlocal seq
                seq += 1
                ins.then_inc(act_seq, 1)

            def settle():
                act.wait_ge(act_seq, seq)

            def copy(dst, src, **kw):
                return nc.scalar.activation(dst, src, ACT.Copy, **kw)

            split = Splitter(act, hi_unit)

            def take(l, name, own=True):
                r = number[l, name]
                split.upto(ends[r] + HALVES - 1)
                full(act, r)
                return r, bank(r)

            def signed_off(r):
                if r:
                    act.wait_ge(act_done, r)
                act.sem_inc(act_done, 1)

            def skip(l, name):
                r, _ = take(l, name)
                signed_off(r)

            def to_transposed(l, names, dst):
                for i, name in enumerate(names):
                    r, pt = take(l, name)
                    copy(dst[:, 4 * i:4 * i + 4, width(l)], pt[:, :, width(l)]).then_inc(act_done, 1)

            def std(count):
                act.wait_ge(var_ready, count)
                for rws, ts in parts_now:
                    ins = nc.scalar.activation(rstd[rws, ts, :], rstd[rws, ts, :], ACT.Sqrt)
                ins.then_inc(std_ready, 1)

            split.upto(HALVES - 1)
            stds = 0
            for i, (tile, src) in enumerate(((0, w["x"][0, 0:P, :]), (1, w["x"][0, P:2 * P, :]), (2, w["meta"]))):
                act.dma_start(h_tok[0:TILE_ROWS[tile], tile, :], src).then_inc(x_landed, 16)
            to_transposed(0, ("ht0", "ht1"), hT_hi)
            for l in range(DEPTH):
                parts_now = parts(l)
                r, pt = take(l, "gk")
                copy(kT[:, :, :], pt[:, :, 0:T]).then_inc(act_done, 1)
                r, pt = take(l, "gq")
                copy(qT[:, :, :], pt[:, :, 0:T], scale=DK ** -0.5).then_inc(act_done, 1)
                r, pt = take(l, "ga")
                copy(gaT, pt[0:RANK, 0, 0:T]).then_inc(act_done, 1)
                r, _ = take(l, "z")
                act.wait_ge(zb_ready, l + 1)
                step(nc.scalar.activation(fT[:, :, :], eT[:, :, :], ACT.Abs))
                settle()
                step(nc.scalar.activation(fT[:, :, :], fT[:, :, :], ACT.Exp, scale=-1.0))
                settle()
                nc.scalar.activation(fT[:, :, :], fT[:, :, :], ACT.Ln, bias=1.0).then_inc(sp_ready, 1)
                signed_off(r)
                for c in range(2):
                    r, pt = take(l, f"gv{c}")
                    for rws, ts in parts_all():
                        ins = copy(v_tok[rws, ts, c * COLS:(c + 1) * COLS], pt[rws, ts, :])
                    ins.then_inc(act_done, 1)
                act.wait_ge(d_ready, l + 1)
                nc.scalar.activation(fT[:, :, :], bT[:, :, :], ACT.Exp, scale=1.0 / TAU)
                nc.scalar.activation(eT[:, :, :], bT[:, :, :], ACT.Exp, scale=-1.0 / TAU)
                for h in range(0, HEADS, 2):
                    nc.scalar.activation(o_tok[:, h // 2, 0:2 * T], o_tok[:, h // 2, 0:2 * T], ACT.Exp, scale=1.0 / TAU)
                nc.scalar.activation(decay[:, :, 0:1], bT[:, :, META - 1:META], ACT.Exp, scale=1.0 / TAU)
                nc.scalar.activation(decay[:, :, 1:], bT[:, :, META + CHUNK - 1:T:CHUNK], ACT.Exp, scale=1.0 / TAU).then_inc(e_ready, 1)

                def merge_gate(q, c):
                    sg = (sgA, sgB)[q]
                    r, pt = take(l, f"gt{'ab'[q]}{c}")
                    for m in range(4):
                        ins = nc.scalar.activation(sg[:, 4 * c + m, width(l)], pt[:, m, width(l)], ACT.Sigmoid,
                                                   bias=b_g[:, l, q, 4 * c + m:4 * c + m + 1])
                    ins.then_inc(act_done, 1)

                merge_gate(0, 0)
                for b, q in (("g", 0), ("r", 1)):
                    if b == "g":
                        r, pt = take(l, "g_kt")
                        for rws, ts in parts_all():
                            ins = copy(k_tok[rws, ts, :], pt[rws, ts, :])
                        ins.then_inc(act_done, 1)
                    else:
                        r, pt = take(l, "r_qt")
                        copy(qT[:, :, width(l)], pt[:, :, width(l)]).then_inc(act_done, 1)
                        r, pt = take(l, "r_kt")
                        copy(kT[:, :, :], pt[:, :, 0:T]).then_inc(act_done, 1)
                        for c in range(2):
                            r, pt = take(l, f"rv{c}")
                            for rws, ts in parts_all():
                                ins = copy(v_tok[rws, ts, c * COLS:(c + 1) * COLS], pt[rws, ts, :])
                            ins.then_inc(act_done, 1)
                    skip(l, f"{b}_sc")
                    for c in range(NCHUNK):
                        if c == 0 and l == 1:
                            skip(l, f"{b}_o{c}")
                            continue
                        r, pt = take(l, f"{b}_o{c}")
                        tile, rws = chunk_rows(c)
                        copy(o_tok[rws, tile, :].rearrange("p (b n) -> p b n", b=2), pt[rws, 2:4, :]).then_inc(act_done, 1)
                    stds += 1
                    split.upto(ends[number[l, f"{b}_o0"]] + HALVES)
                    std(stds)
                    for c in range(2):
                        r, pt = take(l, f"gr{c}" if b == "g" else f"rg{c}")
                        nc.scalar.activation(srT[:, 4 * c:4 * c + 4, width(l)], pt[:, :, width(l)], ACT.Silu).then_inc(act_done, 1)
                    merge_gate(q, 1 if b == "g" else 0)
                    for c in range(2):
                        r, pt = take(l, f"{b}_t{c}")
                        act.wait_ge(zf_ready, 4 * l + 2 * q + c + 1)
                        copy(zT_hi[:, 4 * c:4 * c + 4, width(l)], srT[:, 4 * c:4 * c + 4, width(l)]).then_inc(act_done, 1)
                    if b == "g":
                        for name in ("rq", "rk", "pa0", "pa1"):
                            skip(l, name)
                    else:
                        merge_gate(1, 1)
                        for c in range(2):
                            r, _ = take(l, f"pb{c}")
                            act.wait_ge(merged_ready, 2 * l + c + 1)
                            copy(m_hi[c][:, :, width(l)], sgA[:, 4 * c:4 * c + 4, width(l)]).then_inc(act_done, 1)
                for c in range(2):
                    r, pt = take(l, f"wo{c}")
                    copy(sgA[:, 4 * c:4 * c + 4, width(l)], pt[:, :, width(l)]).then_inc(act_done, 1)
                skip(l, "wot0")
                skip(l, "wot1")
                stds += 1
                std(stds)
                to_transposed(l, ("h1t0", "h1t1"), hT_hi)
                if l == 0:
                    for j in range(6):
                        n = 4 if j < 5 else 2
                        r, pt = take(l, f"fg{j}")
                        if j:
                            act.wait_ge(af_ready, j)
                        nc.scalar.activation(gT_s[:, 0:n, :], pt[:, 0:n, 0:T], ACT.Silu).then_inc(act_done, 1)
                        r, _ = take(l, f"fu{j}")
                        act.wait_ge(af_ready, j + 1)
                        copy(aT_hi[:, 4 * j:4 * j + n, :], aT_f[:, 0:n, :]).then_inc(ahi_ready, 1)
                        signed_off(r)
                    for c, dst in enumerate((gT_s, aT_f)):
                        r, pt = take(l, f"fd{c}")
                        copy(dst[:, :, :], pt[:, :, 0:T]).then_inc(act_done, 1)
                    skip(l, "fdt0")
                    skip(l, "fdt1")
                    stds += 1
                    std(stds)
                    to_transposed(0, ("h2t0", "h2t1"), hT_hi)
            if stop is not None:
                return

            act.wait_ge(wrs, 16)
            copy(wr_hi[:, :, :], wr[:, :, :]).then_inc(act_seq_router, 1)
            copy(x_hi[:, :, :], h_tok[:, 0:2, :]).then_inc(xsplit_hi, 1)
            r, pt = take(1, "route")
            copy(logit[:, :, :], pt[:, 0, 0:2 * EXPERTS].rearrange("p (t e) -> p t e", t=2)).then_inc(act_done, 1)
            act.wait_ge(prob_ready, 1)
            for t in range(2):
                ins = nc.scalar.activation(prob[:, t, :], logit[:, t, :], ACT.Exp, bias=tiny[:, t, 0:1], accum_out=tiny[:, t, 1:2])
            ins.then_inc(act_seq_router, 1)
            skip(1, "rank")

            def hi_at(at, u, uses):
                act.wait_ge(raw_landed[at % RAW], uses * 16 + 16)
                act.wait_ge(units_used, u - HALVES + 1)
                copy(w_hi[:, at % HALVES, :], raw[:, at % RAW, :]).then_inc(hi_ready, 1)

            def expert(g, e, overlapped):
                u0, k0 = NS + g * UPG, g * JCH
                base = g * (UPG // RAW)

                def hi(i, turns, u):
                    hi_at(NS + i, u, base + turns + (NS + i) // RAW)

                def turned(k, u):
                    act.wait_ge(m_t, START + k + 1)
                    act.wait_ge(units_used, u)
                    copy(ag_hi[:, :, :], TB4).then_inc(m_ahi, 1)

                def silu(k, u):
                    act.wait_ge(units_used, u)
                    act.wait_ge(m_a, START + k)
                    nc.scalar.activation(g_sl[:, :], ps[0][:, 0, :], ACT.Silu).then_inc(m_silu, 1)

                def chunk(j, first):
                    uj, k, turns = u0 + (j * UPJ - 2), k0 + j, j - 1
                    for i in range(3):
                        hi(4 + i, turns, uj + i)
                    if first:
                        act.wait_ge(m_st_full, START + g + 1)
                        act.wait_ge(m_ylo, START + g + 1)
                        copy(slot_w[:, :], ps[0][:, 3, 0:1])
                        copy(ST[:, :, :], ps[0][:, 3, P:3 * P].rearrange("p (t s) -> p t s", t=2)).then_inc(m_st, 1)
                    hi(7, turns, uj + 3)
                    turned(k - 1, uj)
                    silu(k, uj + 2)
                    for i in range(4, 6):
                        hi(4 + i, turns, uj + i)

                if not overlapped:
                    gathered(g + 1)
                for i in range(2):
                    hi(i, 0, u0 + i)
                if overlapped:
                    result(g, u0)
                for i in range(2, 4):
                    hi(i, 0, u0 + i)
                silu(k0, u0 + 2)
                chunk(1, True)
                with act.Fori(2, JCH) as j:
                    chunk(j, False)
                for i in range(2):
                    hi(4 + i, JCH - 1, u0 + UPG - 2 + i)
                turned(k0 + JCH - 1, u0 + UPG - 2)
                if overlapped:
                    gathered(g + 1)
                else:
                    result(g + 1, u0 + UPG)

            def gathered(n):
                act.wait_ge(m_xg_full, START + n + 1)
                copy(xg_hi[:, :, :], ps[1][:, 2:4, :].rearrange("p b (k s) -> p (b k) s", s=P)).then_inc(m_xg_act, 1)

            def result(n, u):
                act.wait_ge(units_used, u)
                act.wait_ge(m_st, START + n)
                act.wait_ge(m_sc, START + 2 * n)
                nc.scalar.activation(y_hi[:, :].rearrange("p (b n) -> p b n", b=2), ps[1][:, 0:2, :], ACT.Copy,
                                     scale=slot_w[:, 0:1]).then_inc(m_yhi, 1)

            TB4 = ps[0][:, 2, :].rearrange("p (k s) -> p k s", s=P)
            for first in (m_silu, m_xg_act, m_ahi, m_yhi, m_st):
                act.sem_inc(first, START)
            gathered(0)
            act.wait_ge(m_zero, 1)
            with act.Fori(0, EXPERTS) as g:
                expert(g, g, True)
            result(EXPERTS, NS + EXPERTS * UPG)
            act.wait_ge(plan_ready, 1)
            n_groups, spill = load_plan(act)
            for s in range(SPILLS):
                with act.If(n_groups > s):
                    expert(EXPERTS + s, spill[s], False)
                act.end_ifs()
            act.wait_ge(var_ready, stds + 1)
            nc.scalar.activation(rstd[:, 0:2, :], rstd[:, 0:2, :], ACT.Sqrt).then_inc(std_ready, 1)

        @block.vector
        def _(dve):
            seq = 0

            def step(ins):
                nonlocal seq
                seq += 1
                ins.then_inc(dve_seq, 1)

            def settle():
                dve.wait_ge(dve_seq, seq)

            split = Splitter(dve, lo_unit)

            def take(l, name):
                r = number[l, name]
                split.upto(ends[r] + HALVES - 1)
                full(dve, r)
                return r, bank(r)

            def signed_off(r):
                if r:
                    dve.wait_ge(dve_done, r)
                dve.sem_inc(dve_done, 1)

            def skip(l, name):
                r, _ = take(l, name)
                signed_off(r)

            tt, ts_, stt = nc.vector.tensor_tensor, nc.vector.tensor_scalar, nc.vector.scalar_tensor_tensor

            def to_transposed(l, names, hi, lo):
                for i, name in enumerate(names):
                    r, pt = take(l, name)
                    dve.wait_ge(act_done, r + 1)
                    s = (slice(None), slice(4 * i, 4 * i + 4), width(l))
                    tt(lo[s], pt[:, :, width(l)], hi[s].bitcast(F32), ALU.subtract).then_inc(dve_done, 1)

            stds = 0

            def normalise(src, groups, size, eps, centred, where_parts, ahead=0):
                nonlocal stds
                pieces = max(1, size // 512)
                for rws, ts in where_parts:
                    for t in range(ts.start, ts.stop):
                        for g in range(groups):
                            for q in range(pieces):
                                n = size // pieces
                                step(nc.vector.bn_stats(stats[rws, t, g + q, :], src[rws, t, g * size + q * n:g * size + (q + 1) * n]))
                settle()
                for rws, ts in where_parts:
                    for t in range(ts.start, ts.stop):
                        for g in range(groups):
                            step(nc.vector.bn_aggr(mv[rws, t, g, :], stats[rws, t, g:g + pieces, :].rearrange("p a b -> p (a b)")))
                settle()
                for rws, ts in where_parts:
                    mean, var, r_ = mv[rws, ts, 0:groups, 0], mv[rws, ts, 0:groups, 1], rstd[rws, ts, 0:groups]
                    if not centred:
                        step(tt(r_, mean, mean, ALU.mult))
                        settle()
                        step(tt(r_, r_, var, ALU.add))
                        settle()
                        var = r_
                    step(ts_(r_, var, float(eps), None, ALU.add))
                settle()
                stds += 1
                for i, (rws, ts) in enumerate(where_parts):
                    ins = nc.vector.reciprocal(rstd[rws, ts, 0:groups], rstd[rws, ts, 0:groups])
                ins.then_inc(var_ready, 1)
                if ahead:
                    split.upto(ahead)
                dve.wait_ge(std_ready, stds)
                if centred:
                    for rws, ts in where_parts:
                        step(stt(shift[rws, ts, 0:groups], mv[rws, ts, 0:groups, 0], -1.0, rstd[rws, ts, 0:groups], ALU.mult, ALU.mult))
                    settle()

            rows_n = 0

            def rows_ready():
                nonlocal rows_n
                rows_n += 1
                dve.wait_ge(rows_landed, 32 * rows_n)

            def layer_norm(where_parts):
                normalise(h_tok, 1, D, LN_EPS, True, where_parts)
                for rws, ts in where_parts:
                    for t in range(ts.start, ts.stop):
                        step(ts_(h_tok[rws, t, :], h_tok[rws, t, :], rstd[rws, t, 0:1], shift[rws, t, 0:1], ALU.mult, ALU.add))
                settle()
                rows_ready()
                for rws, ts in where_parts:
                    for t in range(ts.start, ts.stop):
                        step(tt(h_tok[rws, t, :], h_tok[rws, t, :], rows[rws, 0, :], ALU.mult))
                settle()
                for rws, ts in where_parts:
                    for t in range(ts.start, ts.stop):
                        step(tt(h_tok[rws, t, :], h_tok[rws, t, :], rows[rws, 1, :], ALU.add))
                settle()
                dve.sem_inc(rows_used, 1)

            def heads(a, n):
                return a.rearrange("p (h n) -> p h n", n=n)

            step(nc.vector.memset(rstd[:, :, :], 1.0))
            settle()
            dve.wait_ge(small_landed, 16 * (1 + 7 * DEPTH))
            to_transposed(0, ("ht0", "ht1"), hT_hi, hT_lo)
            for l in range(DEPTH):
                now = parts(l)
                skip(l, "gk")
                skip(l, "gq")
                skip(l, "ga")
                r, pt = take(l, "z")
                for h in range(HEADS):
                    ins = ts_(eT[:, h, :], pt[:, h, 0:T], b_a[:, l, h:h + 1], None, ALU.add)
                ins.then_inc(zb_ready, 1)
                signed_off(r)
                dve.wait_ge(zb_ready, l + 1)
                dve.wait_ge(sp_ready, l + 1)
                step(stt(eT[:, :, :], eT[:, :, :], 0.0, fT[:, :, :], ALU.min, ALU.subtract))
                settle()
                for h in range(HEADS):
                    step(nc.vector.tensor_tensor_scan(bT[:, h, :], table("restart"), eT[:, h, :], 0.0, ALU.mult, ALU.add))
                settle()
                for h in range(0, HEADS, 2):
                    dst = o_tok[:, h // 2, 0:2 * T].rearrange("p (h t) -> p h t", h=2)
                    b2 = bT[:, h:h + 2, :]
                    step(tt(dst[:, :, 0:META], b2[:, :, META - 1:META].broadcast_to([P, 2, META]), b2[:, :, 0:META], ALU.subtract))
                    for hh in range(2):
                        d4 = dst[:, hh, META:].rearrange("p (c i) -> p c i", i=CHUNK)
                        s4 = b2[:, hh, META:].rearrange("p (c i) -> p c i", i=CHUNK)
                        ins = tt(d4, s4[:, :, CHUNK - 1:CHUNK].broadcast_to([P, NCHUNK - 1, CHUNK]), s4, ALU.subtract)
                        if h + hh < HEADS - 1:
                            step(ins)
                ins.then_inc(d_ready, 1)
                skip(l, "gv0")
                skip(l, "gv1")
                dve.wait_ge(e_ready, l + 1)
                step(tt(qT[:, :, :], qT[:, :, :], fT[:, :, :], ALU.mult))
                for h in range(HEADS):
                    step(tt(k_tail(h), kT[:, h, :], k_tail(h), ALU.mult))
                settle()
                tt(kT[:, :, :], kT[:, :, :], eT[:, :, :], ALU.mult).then_inc(gla_ready, 1)
                skip(l, "gta0")
                skip(l, "g_kt")
                for b, q in (("g", 0), ("r", 1)):
                    if b == "r":
                        skip(l, "r_qt")
                        skip(l, "r_kt")
                        skip(l, "rv0")
                        skip(l, "rv1")
                    r, pt = take(l, f"{b}_sc")
                    for tile, n in ((0, CHUNK), (1, CHUNK), (2, META)):
                        rws = slice(0, TILE_ROWS[tile])
                        dst, src = sT[rws, tile, 0:HEADS * n], pt[rws, tile, 0:HEADS * n]
                        if b == "g":
                            ins = nc.vector.tensor_copy(dst, src)
                        else:
                            ins = tt(dst, src, table("mask_x" if n == CHUNK else "mask_m")[rws, :], ALU.mult)
                    if b == "g":
                        ins.then_inc(scores_out, 1)
                        dve.wait_ge(scores_out, l + 1)
                        signed_off(r)
                    else:
                        ins.then_inc(dve_done, 1)
                    for c in range(NCHUNK):
                        r, pt = take(l, f"{b}_o{c}")
                        if c == NCHUNK - 1:
                            signed_off(r)
                            continue
                        if c:
                            dve.wait_ge(dve_done, r)
                        for h in range(HEADS):
                            new = state[:, (c + 1) % 2, h * DV:(h + 1) * DV]
                            add = pt[:, h // 2, (h % 2) * DV:(h % 2 + 1) * DV]
                            if c == 0:
                                ins = nc.vector.tensor_copy(new, add)
                            else:
                                by = decay[:, h, c:c + 1] if b == "g" else float((1.0 - 2.0 ** (-5.0 - h)) ** CHUNK)
                                ins = stt(new, state[:, c % 2, h * DV:(h + 1) * DV], by, add, ALU.mult, ALU.add)
                        ins.then_inc(dve_done, 1)
                    dve.wait_ge(act_done, number[l, f"{b}_o{NCHUNK - 1}"] + 1)
                    normalise(o_tok, HEADS, DV, LN_EPS if b == "g" else GN_EPS, b == "r", now,
                              ends[number[l, f"{b}_o0"]] + HALVES + 1)
                    for rws, ts in now:
                        for t in range(ts.start, ts.stop):
                            for h in range(HEADS):
                                o = o_tok[rws, t, h * DV:(h + 1) * DV]
                                if b == "g":
                                    step(ts_(o, o, rstd[rws, t, h:h + 1], None, ALU.mult))
                                else:
                                    step(ts_(o, o, rstd[rws, t, h:h + 1], shift[rws, t, h:h + 1], ALU.mult, ALU.add))
                    settle()
                    dve.sem_inc(o_ready, 1)
                    skip(l, f"{b[0]}r0" if b == "g" else "rg0")
                    skip(l, f"{b[0]}r1" if b == "g" else "rg1")
                    skip(l, "gta1" if b == "g" else "gtb0")
                    for c in range(2):
                        r, pt = take(l, f"{b}_t{c}")
                        dve.wait_ge(act_done, number[l, f"gr{c}" if b == "g" else f"rg{c}"] + 1)
                        z = srT[:, 4 * c:4 * c + 4, width(l)]
                        if b == "g":
                            for m in range(4):
                                ins = stt(z[:, m, :], pt[:, m, width(l)], gla_g[:, l, m % 2:m % 2 + 1], z[:, m, :], ALU.mult, ALU.mult)
                        else:
                            for m in range(4):
                                k = 4 * c + m
                                step(ts_(pt[:, m, width(l)], pt[:, m, width(l)], ret_gb[:, l, 0, k:k + 1], ret_gb[:, l, 1, k:k + 1],
                                         ALU.mult, ALU.add))
                            settle()
                            ins = tt(z, pt[:, :, width(l)], z, ALU.mult)
                        ins.then_inc(zf_ready, 1)
                        dve.wait_ge(zf_ready, 4 * l + 2 * q + c + 1)
                        dve.wait_ge(act_done, r + 1)
                        lo_s = (slice(None), slice(4 * c, 4 * c + 4), width(l))
                        tt(zT_lo[lo_s], z, zT_hi[lo_s].bitcast(F32), ALU.subtract).then_inc(dve_done, 1)
                    if b == "g":
                        for name, dst, n_parts, scale in (("rq", o_tok, now, "xi"), ("rk", k_tok, parts_all(), "zeta")):
                            r, pt = take(l, name)
                            half = DK // 2
                            for rws, ts in n_parts:
                                for t in range(ts.start, ts.stop):
                                    src = heads(pt[rws, t, :], DK)
                                    d = heads(dst[rws, t, 0:HEADS * DK], DK)
                                    tmp = heads(o_tok[rws, t, HEADS * DK:D], half)
                                    cs = table("cos")[rws, t * half:(t + 1) * half].unsqueeze(1).broadcast_to([rws.stop, HEADS, half])
                                    sn = table("sin")[rws, t * half:(t + 1) * half].unsqueeze(1).broadcast_to([rws.stop, HEADS, half])
                                    t1, t2 = src[:, :, 0:half], src[:, :, half:DK]
                                    step(tt(d[:, :, 0:half], t1, cs, ALU.mult))
                                    step(tt(tmp[:, 0:HEADS, :], t2, sn, ALU.mult))
                                    step(tt(d[:, :, half:DK], t2, cs, ALU.mult))
                                    step(tt(tmp[:, HEADS:2 * HEADS, :], t1, sn, ALU.mult))
                                    settle()
                                    step(tt(d[:, :, 0:half], d[:, :, 0:half], tmp[:, 0:HEADS, :], ALU.subtract))
                                    step(tt(d[:, :, half:DK], d[:, :, half:DK], tmp[:, HEADS:2 * HEADS, :], ALU.add))
                                    settle()
                                    at = 0 if scale == "xi" else t * HEADS
                                    f = table(scale)[rws, at:at + HEADS].unsqueeze(2).broadcast_to([rws.stop, HEADS, DK])
                                    step(tt(d, d, f, ALU.mult))
                                    settle()
                            signed_off(r)
                        for c in range(2):
                            r, pt = take(l, f"pa{c}")
                            s = (slice(None), slice(4 * c, 4 * c + 4), width(l))
                            tt(sgA[s], pt[:, :, width(l)], sgA[s], ALU.mult).then_inc(dve_done, 1)
                    else:
                        skip(l, "gtb1")
                        for c in range(2):
                            r, pt = take(l, f"pb{c}")
                            s = (slice(None), slice(4 * c, 4 * c + 4), width(l))
                            dve.wait_ge(act_done, number[l, f"gtb{c}"] + 1)
                            step(tt(sgB[s], pt[:, :, width(l)], sgB[s], ALU.mult))
                            settle()
                            tt(sgA[s], sgA[s], sgB[s], ALU.add).then_inc(merged_ready, 1)
                            dve.wait_ge(merged_ready, 2 * l + c + 1)
                            dve.wait_ge(act_done, r + 1)
                            tt(m_lo[c][:, :, width(l)], sgA[s], m_hi[c][:, :, width(l)].bitcast(F32), ALU.subtract).then_inc(dve_done, 1)

                def residual(names, count):
                    for c, name in enumerate(names):
                        r, pt = take(l, name)
                        for rws, ts in now:
                            x_ = h_tok[rws, ts, c * COLS:(c + 1) * COLS]
                            ins = stt(x_, x_, float(ALPHA), pt[rws, ts, :], ALU.mult, ALU.add)
                        ins.then_inc(dve_done, 1)
                        dve.wait_ge(dve_done, r + 1)
                    layer_norm(now)
                    dve.sem_inc(z_ready, 1)

                skip(l, "wo0")
                skip(l, "wo1")
                residual(("wot0", "wot1"), 2 * l + 1)
                to_transposed(l, ("h1t0", "h1t1"), hT_hi, hT_lo)
                if l == 0:
                    for j in range(6):
                        n = 4 if j < 5 else 2
                        skip(l, f"fg{j}")
                        r, pt = take(l, f"fu{j}")
                        dve.wait_ge(act_done, r)
                        if j:
                            dve.wait_ge(ahi_ready, j)
                        tt(aT_f[:, 0:n, :], pt[:, 0:n, 0:T], gT_s[:, 0:n, :], ALU.mult).then_inc(af_ready, 1)
                        dve.wait_ge(ahi_ready, j + 1)
                        dve.wait_ge(af_ready, j + 1)
                        tt(aT_lo[:, 4 * j:4 * j + n, :], aT_f[:, 0:n, :], aT_hi[:, 4 * j:4 * j + n, :].bitcast(F32),
                           ALU.subtract).then_inc(dve_done, 1)
                    skip(l, "fd0")
                    skip(l, "fd1")
                    residual(("fdt0", "fdt1"), 2)
                    to_transposed(0, ("h2t0", "h2t1"), hT_hi, hT_lo)
            if stop is not None:
                for t in range(2):
                    pass
                dve.sem_inc(m_acc, 1)
                return

            dve.wait_ge(act_seq_router, 1)
            tt(wr_lo[:, :, :], wr[:, :, :], wr_hi[:, :, :].bitcast(F32), ALU.subtract).then_inc(wr_lo_ready, 1)
            dve.wait_ge(xsplit_hi, 1)
            tt(x_lo[:, :, :], h_tok[:, 0:2, :], x_hi[:, :, :].bitcast(F32), ALU.subtract).then_inc(xsplit_lo, 1)
            dve.wait_ge(xsplit_lo, 1)
            step(ts_(h_tok[:, 0:2, :], h_tok[:, 0:2, :], float(ALPHA), None, ALU.mult))
            r, pt = take(1, "route")
            dve.wait_ge(act_done, r + 1)
            for t in range(2):
                step(nc.vector.tensor_reduce(tiny[:, t, 0:1], logit[:, t, :], AX.X, ALU.max))
            settle()
            ts_(tiny[:, :, 0:1], tiny[:, :, 0:1], -1.0, None, ALU.mult).then_inc(prob_ready, 1)
            dve.wait_ge(act_seq_router, 2)
            step(nc.vector.reciprocal(tiny[:, :, 1:2], tiny[:, :, 1:2]))
            settle()
            for t in range(2):
                step(ts_(prob[:, t, :], prob[:, t, :], tiny[:, t, 1:2], None, ALU.mult))
            settle()
            for t in range(2):
                step(nc.vector.max(top[:, t, :], prob[:, t, :]))
            settle()
            for t in range(2):
                step(nc.vector.max_index(top_at[:, t, :], top[:, t, :], prob[:, t, :]))
            step(tt(tiny[:, :, 2:3], top[:, :, 0:1], top[:, :, 1:2], ALU.add))
            settle()
            step(nc.vector.tensor_copy(top_f[:, :, :], top_at[:, :, 0:2]))
            step(nc.vector.reciprocal(tiny[:, :, 2:3], tiny[:, :, 2:3]))
            settle()
            for t in range(2):
                for i in range(2):
                    step(ts_(hit[:, t, i, :], table("iota")[:, 0:EXPERTS], top_f[:, t, i:i + 1], None, ALU.is_equal))
                step(ts_(top[:, t, 0:2], top[:, t, 0:2], tiny[:, t, 2:3], None, ALU.mult))
            settle()
            step(tt(sel[:, :, :], hit[:, :, 0, :], hit[:, :, 1, :], ALU.add))
            for t in range(2):
                step(ts_(comb[:, t, :], hit[:, t, 0, :], top[:, t, 0:1], None, ALU.mult))
            settle()
            for t in range(2):
                step(stt(comb[:, t, :], hit[:, t, 1, :], top[:, t, 1:2], comb[:, t, :], ALU.mult, ALU.add))
            settle()
            dve.sem_inc(sel_ready, 1)
            dve.sem_inc(dve_done, 1)
            r, pt = take(1, "rank")
            big = float(4 * P)
            step(nc.vector.memset(rank[:, :, EXPERTS:], big))
            step(ts_(rank[:, :, 0:EXPERTS], sel[:, :, :], -big, big, ALU.mult, ALU.add))
            settle()
            step(tt(rank[:, :, 0:EXPERTS], rank[:, :, 0:EXPERTS], pt[:, 0, 0:2 * EXPERTS].rearrange("p (t e) -> p t e", t=2), ALU.add))
            E = EXPERTS
            over, excl, num, hits = (plan_f[0:1, i * E:(i + 1) * E] for i in range(4))
            iota, ones = table("iota"), table("ones")
            step(ts_(over, pt[0:1, 1, 0:E], float(P), None, ALU.is_gt))
            settle()
            step(nc.vector.tensor_tensor_scan(excl, ones[0:1, 0:E], over, 0.0, ALU.mult, ALU.add))
            step(tt(num, over, iota[0:1, 0:E], ALU.mult))
            settle()
            for s in range(SPILLS):
                step(stt(hits, excl, float(s + 1), num, ALU.is_equal, ALU.mult))
                settle()
                step(nc.vector.tensor_reduce(plan_f[0:1, 4 * E + 1 + s:4 * E + 2 + s], hits, AX.X, ALU.add))
                settle()
            step(nc.vector.tensor_reduce(plan_f[0:1, 4 * E:4 * E + 1], over, AX.X, ALU.add))
            settle()
            nc.vector.tensor_copy(plan[:, :], plan_f[0:1, 4 * E:4 * E + 4]).then_inc(plan_ready, 1)
            dve.wait_ge(plan_ready, 1)
            dve.sem_inc(dve_done, 1)

            def expert(g, e, overlapped):
                u0, k0 = NS + g * UPG, g * JCH

                def lo(i, u):
                    at = NS + i
                    dve.wait_ge(hi_ready, u + 1)
                    dve.wait_ge(units_used, u - HALVES + 1)
                    tt(w_lo[:, at % HALVES, :], raw[:, at % RAW, :], w_hi[:, at % HALVES, :].bitcast(F32),
                       ALU.subtract).then_inc(lo_ready, 1)

                def turned(k):
                    dve.wait_ge(m_ahi, START + k + 1)
                    tt(ag_lo[:, :, :], ps[0][:, 2, :].rearrange("p (k s) -> p k s", s=P), ag_hi[:, :, :].bitcast(F32),
                       ALU.subtract).then_inc(m_alo, 1)

                def gated(k, u):
                    dve.wait_ge(units_used, u)
                    dve.wait_ge(m_silu, START + k + 1)
                    dve.wait_ge(m_t, START + k)
                    tt(a_sl[:, :], ps[0][:, 1, :], g_sl[:, :], ALU.mult).then_inc(m_a, 1)

                def chunk(j, start):
                    uj, k = u0 + (j * UPJ - 2), k0 + j
                    for i in range(start, 4):
                        lo(4 + i, uj + i)
                    turned(k - 1)
                    for i in range(4, 6):
                        lo(4 + i, uj + i)
                    gated(k, uj + 4)

                if not overlapped:
                    places(g + 1, g, e, P)
                    gathered(g + 1)
                for i in range(2):
                    lo(i, u0 + i)
                if overlapped:
                    result(g)
                for i in range(2, 4):
                    lo(i, u0 + i)
                if overlapped:
                    add(g, 0)
                lo(4, u0 + 4)
                if overlapped:
                    add(g, 1)
                lo(5, u0 + 5)
                gated(k0, u0 + 4)
                chunk(1, 2)
                with dve.Fori(2, JCH) as j:
                    chunk(j, 0)
                if overlapped:
                    places(g + 1, g + 1, e + 1, 0)
                for i in range(2):
                    lo(4 + i, u0 + UPG - 2 + i)
                turned(k0 + JCH - 1)
                if overlapped:
                    gathered(g + 1)
                else:
                    result(g + 1)
                    add(g + 1, 0)
                    add(g + 1, 1)

            def places(n, slots_read, e, first_slot):
                dve.wait_ge(m_xg_full, START + n)
                dve.wait_ge(m_st_full, START + slots_read)
                for t in range(2):
                    ins = ts_(S[:, t, :], iota[:, first_slot:first_slot + P], rank[:, t, bass.ds(e, 1)], None, ALU.is_equal)
                ins.then_inc(m_s, 1)

            def gathered(n):
                dve.wait_ge(m_xg_act, START + n + 1)
                tt(xg_lo[:, :, :], ps[1][:, 2:4, :].rearrange("p b (k s) -> p (b k) s", s=P), xg_hi[:, :, :].bitcast(F32),
                   ALU.subtract).then_inc(m_xg_dve, 1)

            def result(n):
                dve.wait_ge(m_yhi, START + n + 1)
                stt(y_lo[:, :].rearrange("p (b n) -> p b n", b=2), ps[1][:, 0:2, :], slot_w[:, 0:1],
                    y_hi[:, :].bitcast(F32).rearrange("p (b n) -> p b n", b=2), ALU.mult, ALU.subtract).then_inc(m_ylo, 1)

            def add(n, t):
                dve.wait_ge(m_sc, START + 2 * n + t + 1)
                dve.wait_ge(m_acc, START + 2 * n + t)
                h = h_tok[:, t, :].rearrange("p (b n) -> p b n", b=2)
                src = (ps[1][:, 2:4, :], ps[0][:, 2:4, :])[t]
                tt(h, h, src, ALU.add).then_inc(m_acc, 1)

            for first in (m_s, m_xg_dve, m_a, m_alo, m_ylo, m_acc):
                dve.sem_inc(first, START)
            step(nc.vector.memset(ps[1][:, 0:2, :], 0.0))
            step(nc.vector.memset(ST[:, :, :].bitcast(F32), 0.0))
            nc.vector.memset(slot_w[:, :], 0.0).then_inc(m_zero, 1)
            settle()
            places(0, 0, 0, 0)
            gathered(0)
            with dve.Fori(0, EXPERTS) as g:
                expert(g, g, True)
            result(EXPERTS)
            add(EXPERTS, 0)
            add(EXPERTS, 1)
            n_groups, spill = load_plan(dve)
            for s in range(SPILLS):
                with dve.If(n_groups > s):
                    expert(EXPERTS + s, spill[s], False)
                dve.end_ifs()
            dve.wait_ge(m_acc, START + n_groups * 2 + 2 * EXPERTS + 2)
            layer_norm(parts(1))
            dve.sem_inc(z_ready, 1)


NAMES = ["x", "meta", "w_in", "b_gate", "gla_w_a2", "gla_b_a", "gla_norm_g", "ret_norm_g", "ret_norm_b", "w_pa", "w_pb",
         "w_o", "ln1_g", "ln1_b", "ffn_w_gate", "ffn_w_up", "ffn_w_down", "moe_w_router", "moe_w_gate", "moe_w_up",
         "moe_w_down", "ln2_g", "ln2_b"]


def kernel(**inputs):
    import numpy as _np
    import concourse.bacc as _bacc
    from concourse import mybir as _mybir
    from concourse.bass_utils import run_bass_kernel_spmd as _run

    nc = _bacc.Bacc("TRN2", target_bir_lowering=False, num_devices=1, dynamic_dma_scratch_size=4096)
    arrays, w = {}, {}
    for name in NAMES:
        a = _np.ascontiguousarray(inputs[name])
        arrays[f"in_{name}"] = a
        w[name] = nc.dram_tensor(f"in_{name}", a.shape, _mybir.dt.from_np(a.dtype), kind="ExternalInput").ap()
    tables, where = host_constants()
    arrays["in_tables"] = tables
    consts = nc.dram_tensor("in_tables", tables.shape, _mybir.dt.float32, kind="ExternalInput").ap()
    out = nc.dram_tensor("out", (1, SEQ, D), _mybir.dt.float32, kind="ExternalOutput").ap()
    trunk(nc, w, consts, where, out, STOP)
    r = _run(nc, [arrays], core_ids=[0])
    return r.results[0]["out"]


STOP = None
```

```python
from contextlib import ExitStack

import numpy as np

import concourse.bass as bass
from concourse import mybir

ALU = mybir.AluOpType
ACT = mybir.ActivationFunctionType
AX = mybir.AxisListType
F32 = mybir.dt.float32
F32R = mybir.dt.float32r
I32 = mybir.dt.int32
U32 = mybir.dt.uint32

P = 128
D = 1024
KT = D // P
SEQ, META = 256, 16
T = SEQ + META
CHUNK = 64
NCHUNK = 1 + SEQ // CHUNK
DEPTH = 2
HEADS, DK, DV = 4, 128, 256
RANK = 16
TAU = 16.0
DFF, DFFE = 2816, 3584
EXPERTS = 8
SPILLS = 3
ALPHA = (2 * DEPTH) ** 0.25
LN_EPS, GN_EPS = 1e-5, 1e-6
UNIT = 2048
COLS = 512
RAW, HALVES = 6, 3
JCH = DFFE // COLS
UPJ = 6
UPG = JCH * UPJ
START = 1

SIZES = dict(gq=512, gk=512, gv=1024, gr=1024, ga=RANK, rq=512, rk=512, rv=1024, rg=1024, gate_a=D, gate_b=D)
COL = {}
for _name, _size in SIZES.items():
    COL[_name] = sum(SIZES[k] for k in list(SIZES)[:len(COL)])

TILE_COL = [META, META + P, 0]
TILE_ROWS = [P, P, META]


def host_constants():
    f = np.float32
    p = np.arange(P)
    half = DK // 2
    inv = (f(10000.0) ** (-np.arange(half, dtype=f) / f(half))).astype(f)
    ang = (np.arange(T, dtype=f) * inv[p % half, None]).astype(f)
    sign = np.where(p < half, -1.0, 1.0)[:, None]
    gamma = 1.0 - 2.0 ** (-5.0 - np.arange(HEADS))
    xi = gamma[None, :] ** (p[:, None] + 1.0)
    zeta_x = gamma[None, :] ** (P - 1.0 - p[:, None])
    zeta_m = gamma[None, :] ** (META - 1.0 - p[:, None])
    zeta = np.stack([zeta_x, zeta_x, zeta_m], 1) * DK ** -0.5
    causal = (p[None, :] >= p[:, None])
    mask = causal[:, None, :] * (gamma[None, :] ** -(p[:, None] + 1.0))[:, :, None] * DK ** -0.5
    restart = np.ones(T)
    restart[[0] + [META + CHUNK * c for c in range(4)]] = 0.0
    parts = dict(
        ident=np.eye(P), cos=np.cos(ang), sin=sign * np.sin(ang), xi=xi, xi_squared=xi ** 2, zeta=zeta, mask=mask,
        restart=np.broadcast_to(restart, (P, T)), before=(p[:, None] < p[None, :]), ones=np.ones((P, P)),
        iota=np.broadcast_to(np.arange(2 * P), (P, 2 * P)),
    )
    at, where, flat = 0, {}, []
    for name, a in parts.items():
        a = np.ascontiguousarray(a, dtype=f).reshape(P, -1)
        where[name] = (at, at + a.shape[1])
        at += a.shape[1]
        flat.append(a)
    return np.concatenate(flat, 1), where


def trunk(nc, w, consts, where, out):
    ctx = ExitStack()
    with ctx:
        def sem(name):
            return ctx.enter_context(nc.semaphore(name))

        def sb(stack, name, shape, dt=F32):
            return stack.enter_context(nc.sbuf_tensor(name, shape, dt))

        raw = sb(ctx, "raw", [P, RAW, UNIT])
        w_hi = sb(ctx, "w_hi", [P, HALVES, UNIT], F32R)
        w_lo = sb(ctx, "w_lo", [P, HALVES, UNIT], F32R)
        h_tok = sb(ctx, "h_tok", [P, 3, D])
        hT_hi = sb(ctx, "hT_hi", [P, KT, T], F32R)
        hT_lo = sb(ctx, "hT_lo", [P, KT, T], F32R)
        rows = sb(ctx, "rows", [P, 2, D])
        tab = sb(ctx, "tab", [P, consts.shape[1]])
        a2 = sb(ctx, "a2", [RANK, DEPTH, HEADS * DK])
        b_a = sb(ctx, "b_a", [P, DEPTH, HEADS])
        b_g = sb(ctx, "b_g", [P, DEPTH, 2, KT])
        gla_g = sb(ctx, "gla_g", [P, DEPTH, DV // P])
        ret_gb = sb(ctx, "ret_gb", [P, DEPTH, 2, KT])
        ln_gb = sb(ctx, "ln_gb", [P, 3, 2, KT])
        stats = sb(ctx, "stats", [P, 3, 4, 6])
        mv = sb(ctx, "mv", [P, 3, 4, 2])
        rstd = sb(ctx, "rstd", [P, 3, 4])
        shift = sb(ctx, "shift", [P, 3, 4])

        def table(name, **dims):
            lo, hi = where[name]
            return tab[:, lo:hi]

        ident = table("ident")

        mix = ExitStack()
        o_tok = sb(mix, "o_tok", [P, 3, D])
        sgA = sb(mix, "sgA", [P, KT, T])
        gated = ExitStack()
        ln_T = o_tok[:, :, :].rearrange("p a n -> p (a n)")[:, 0:KT * T].rearrange("p (k t) -> p k t", k=KT)
        raw_qk = ln_T
        srT = sb(gated, "srT", [P, KT, T])
        gated.close()
        mT_hi = sb(mix, "mT_hi", [P, 4, T], F32R)
        mT_lo = sb(mix, "mT_lo", [P, 4, T], F32R)
        vlife = ExitStack()
        v_tok = sb(vlife, "v_tok", [P, 3, D])
        attn = ExitStack()
        qT = sb(attn, "qT", [P, HEADS, T])
        kT = sb(attn, "kT", [P, HEADS, T])
        eT = sb(attn, "eT", [P, HEADS, T])
        fT = sb(attn, "fT", [P, HEADS, T])
        bT = sb(attn, "bT", [P, HEADS, T])
        k_tok = sb(attn, "k_tok", [P, 3, HEADS * DK])
        state = srT[:, :, :].rearrange("p k t -> p (k t)")[:, 0:2 * HEADS * DV].rearrange("p (a n) -> p a n", a=2)
        sR = eT[:, :, :].rearrange("p h t -> p (h t)")
        sT = sb(attn, "sT", [P, 3, HEADS * CHUNK])
        gaT = sgA[0:RANK, 0, :]
        decay = sb(attn, "decay", [P, HEADS, NCHUNK])
        attn.close()
        zT_hi = sb(vlife, "zT_hi", [P, KT, T], F32R)
        zT_lo = sb(vlife, "zT_lo", [P, KT, T], F32R)
        vlife.close()
        m_hi = (mT_hi[:, :, :], zT_hi[:, 4:8, :])
        m_lo = (mT_lo[:, :, :], zT_lo[:, 4:8, :])
        sgB = sb(mix, "sgB", [P, KT, T])
        mix.close()

        ffn = ExitStack()
        aT_hi = sb(ffn, "aT_hi", [P, DFF // P, T], F32R)
        aT_lo = sb(ffn, "aT_lo", [P, DFF // P, T], F32R)
        gT_s = sb(ffn, "gT_s", [P, 4, T])
        aT_f = sb(ffn, "aT_f", [P, 4, T])
        ffn.close()

        moe = ExitStack()
        x_hi = sb(moe, "x_hi", [P, 2, D], F32R)
        x_lo = sb(moe, "x_lo", [P, 2, D], F32R)
        S = sb(moe, "S", [P, 2, P], F32R)
        ST = sb(moe, "ST", [P, 2, P], F32R)
        xg_hi = sb(moe, "xg_hi", [P, KT, P], F32R)
        xg_lo = sb(moe, "xg_lo", [P, KT, P], F32R)
        g_sl = sb(moe, "g_sl", [P, COLS])
        a_sl = sb(moe, "a_sl", [P, COLS])
        ag_hi = sb(moe, "ag_hi", [P, 4, P], F32R)
        ag_lo = sb(moe, "ag_lo", [P, 4, P], F32R)
        y_hi = sb(moe, "y_hi", [P, D], F32R)
        y_lo = sb(moe, "y_lo", [P, D], F32R)
        wr = sb(moe, "wr", [P, KT, EXPERTS])
        prob = sb(moe, "prob", [P, 2, EXPERTS])
        top = sb(moe, "top", [P, 2, 8])
        top_at = sb(moe, "top_at", [P, 2, 8], U32)
        top_f = sb(moe, "top_f", [P, 2, 2])
        hit = sb(moe, "hit", [P, 2, 2, EXPERTS])
        sel = sb(moe, "sel", [P, 2, EXPERTS])
        comb = sb(moe, "comb", [P, 2, EXPERTS])
        rank = sb(moe, "rank", [P, 2, EXPERTS + 1])
        tiny = sb(moe, "tiny", [P, 2, 4])
        slot_w = sb(moe, "slot_w", [P, 1])
        plan_f = sb(moe, "plan_f", [1, 8 * EXPERTS])
        plan = sb(moe, "plan", [1, 4], I32)
        moe.close()

        ps = [ctx.enter_context(nc.psum_tensor(f"ps{i}", [P, 4, 512], F32)) for i in range(2)]

        raw_landed = [sem(f"raw_landed{i}") for i in range(RAW)]
        hi_ready = sem("hi_ready")
        lo_ready = sem("lo_ready")
        units_used = sem("units_used")
        set_full = sem("set_full")
        act_done = sem("act_done")
        dve_done = sem("dve_done")
        act_seq = sem("act_seq")
        dve_seq = sem("dve_seq")
        decay_input_ready = sem("decay_input_ready")
        softplus_ready = sem("softplus_ready")
        log_decays_ready = sem("log_decays_ready")
        decays_ready = sem("decays_ready")
        gla_ready = sem("gla_ready")
        state_full = sem("state_full")
        scores_out = sem("scores_out")
        masked = sem("masked")
        var_ready = sem("var_ready")
        std_ready = sem("std_ready")
        rotated = sem("rotated")
        swap_landed = [sem("q_swap_landed"), sem("k_swap_landed")]
        normed_ready = sem("normed_ready")
        merged_ready = sem("merged_ready")
        ffn_hidden_ready = sem("ffn_hidden_ready")
        ffn_hidden_hi_ready = sem("ffn_hidden_hi_ready")
        o_ready = sem("o_ready")
        gated_ready = sem("gated_ready")
        gated_hi_ready = sem("gated_hi_ready")
        rows_landed, rows_used = sem("rows_landed"), sem("rows_used")
        small_landed, x_landed, ident_landed = sem("small_landed"), sem("x_landed"), sem("ident_landed")
        norm_T = sem("norm_T")
        norm_hi = sem("norm_hi")
        x_scaled = sem("x_scaled")
        stored = sem("stored")
        x_hi_ready, x_lo_ready = sem("x_hi_ready"), sem("x_lo_ready")
        router_landed = sem("router_landed")
        prob_ready = sem("prob_ready")
        sel_ready = sem("sel_ready")
        plan_ready = sem("plan_ready")
        places_ready = sem("places_ready")
        slots_full = sem("slots_full")
        slots_ready = sem("slots_ready")
        gather_full = sem("gather_full")
        gather_hi_ready, gather_lo_ready = sem("gather_hi_ready"), sem("gather_lo_ready")
        silu_ready = sem("silu_ready")
        hidden_ready = sem("hidden_ready")
        hidden_turned = sem("hidden_turned")
        hidden_hi_ready, hidden_lo_ready = sem("hidden_hi_ready"), sem("hidden_lo_ready")
        result_hi_ready, result_lo_ready = sem("result_hi_ready"), sem("result_lo_ready")
        scatter_full = sem("scatter_full")
        scatter_added = sem("scatter_added")

        stream = []

        def add_cols(src, c0, cols=COLS):
            for k in range(0, KT, 4):
                stream.append(("cols", src, k, 4, c0, cols))

        for l in range(DEPTH):
            w_in = w["w_in"][l]
            def pair(src, c0):
                add_cols(src, c0)
                add_cols(src, c0 + COLS)

            add_cols(w_in, COL["gk"])
            add_cols(w_in, COL["gq"])
            add_cols(w_in, COL["ga"], P)
            pair(w_in, COL["gv"])
            add_cols(w_in, COL["gate_a"])
            pair(w_in, COL["gr"])
            add_cols(w_in, COL["gate_a"] + COLS)
            add_cols(w_in, COL["rq"])
            add_cols(w_in, COL["rk"])
            pair(w["w_pa"][l], 0)
            pair(w_in, COL["rv"])
            pair(w_in, COL["rg"])
            pair(w_in, COL["gate_b"])
            pair(w["w_pb"][l], 0)
            pair(w["w_o"][l], 0)
            if l == 0:
                for c0 in range(0, DFF, COLS):
                    n = min(COLS, DFF - c0)
                    add_cols(w["ffn_w_gate"][0], c0, n)
                    add_cols(w["ffn_w_up"][0], c0, n)
                for c in range(2):
                    for k in range(0, DFF // P, 4):
                        stream.append(("cols", w["ffn_w_down"][0], k, min(4, DFF // P - k), c * COLS, COLS))
        NS = len(stream)

        def shape_of(u):
            return (stream[u][3], stream[u][5])

        def unit(buf, slot, k, n):
            return buf[:, slot, 0:k * n].rearrange("p (k n) -> p k n", k=k)

        def landed(eng, u):
            eng.wait_ge(raw_landed[u % RAW], 16 * (u // RAW + 1))

        def hi_unit(act, u):
            landed(act, u)
            if u >= HALVES:
                act.wait_ge(units_used, u - HALVES + 1)
            k, n = shape_of(u)
            nc.scalar.activation(w_hi[:, u % HALVES, 0:k * n], raw[:, u % RAW, 0:k * n], ACT.Copy).then_inc(hi_ready, 1)

        def lo_unit(dve, u):
            dve.wait_ge(hi_ready, u + 1)
            if u >= HALVES:
                dve.wait_ge(units_used, u - HALVES + 1)
            k, n = shape_of(u)
            nc.vector.tensor_tensor(w_lo[:, u % HALVES, 0:k * n], raw[:, u % RAW, 0:k * n],
                                    w_hi[:, u % HALVES, 0:k * n].bitcast(F32), ALU.subtract).then_inc(lo_ready, 1)

        class Splitter:

            def __init__(self, eng, split):
                self.eng, self.split, self.next = eng, split, 0

            def upto(self, u):
                while self.next < min(u, NS):
                    self.split(self.eng, self.next)
                    self.next += 1

        sets = []

        def plan_sets():
            u = 0
            for l in range(DEPTH):
                def weights(name, units):
                    nonlocal u
                    u += units
                    sets.append((l, name, u, True))

                def local(name):
                    sets.append((l, name, u, False))
                if l == 0:
                    local("ht0"); local("ht1")
                weights("gk", 2); weights("gq", 2); weights("ga", 2); local("z")
                weights("gv0", 2); weights("gv1", 2); local("gvt0"); weights("gta0", 2)
                local("gvt1"); local("g_kt"); local("g_sc")
                for c in range(NCHUNK):
                    local(f"g_o{c}")
                weights("gr0", 2); weights("gr1", 2); weights("gta1", 2)
                local("g_t0"); local("g_t1")
                weights("rq", 2); weights("rk", 2)
                weights("pa0", 2); weights("pa1", 2)
                weights("rv0", 2); local("r_kt"); weights("rv1", 2); local("rvt0"); local("rvt1"); local("r_sc")
                for c in range(3):
                    local(f"r_o{c}")
                weights("rg0", 2); weights("rg1", 2); weights("gtb0", 2)
                local("r_t0"); local("r_t1")
                weights("gtb1", 2)
                weights("pb0", 2); weights("pb1", 2)
                weights("wo0", 2); weights("wo1", 2); local("wot0"); local("wot1")
                local("h1t0"); local("h1t1")
                if l == 0:
                    for j in range(6):
                        weights(f"fg{j}", 2); weights(f"fu{j}", 2)
                    weights("fd0", 6); weights("fd1", 6); local("fdt0"); local("fdt1")
                    local("h2t0"); local("h2t1")
                else:
                    local("route"); local("rank")
            assert u == NS

        plan_sets()
        number = {(l, name): r for r, (l, name, _, _) in enumerate(sets)}
        ends = [u for _, _, u, _ in sets]
        NSETS = len(sets)

        def full(eng, r):
            if sets[r][3]:
                eng.wait_ge(units_used, ends[r])
            else:
                eng.wait_ge(set_full, sum(not s[3] for s in sets[:r + 1]))

        def bank(r):
            return ps[r % 2]

        def parts(l):
            return [(slice(0, P), slice(0, 2))] + ([(slice(0, META), slice(2, 3))] if l == 0 else [])

        def parts_all():
            return parts(0)

        def width(l):
            return slice(0, T) if l == 0 else slice(META, T)

        TILE_CHUNKS = [(t, slice(0, TILE_ROWS[t]), slice(TILE_COL[t], TILE_COL[t] + TILE_ROWS[t])) for t in (2, 0, 1)]
        CHUNKS = dict(g=TILE_CHUNKS[0:1] + [(c // 2, slice(CHUNK * (c % 2), CHUNK * (c % 2) + CHUNK),
                                             slice(META + CHUNK * c, META + CHUNK * c + CHUNK)) for c in range(NCHUNK - 1)],
                      r=TILE_CHUNKS)

        def scores(b, tile, rws, h=None):
            n = rws.stop - rws.start
            row, at = (sT[rws, tile, :], 0) if b == "g" else (sR[rws, :], tile * HEADS * P)
            return row[:, at:at + HEADS * n] if h is None else row[:, at + h * n:at + (h + 1) * n]

        def state_n(l, b, c):
            n = {k: len(v) - 1 for k, v in CHUNKS.items()}
            return l * (n["g"] + n["r"]) + (n["g"] if b == "r" else 0) + c + 1

        def k_tail(h):
            return o_tok[:, h // 2, (h % 2) * T:(h % 2 + 1) * T]

        def load_plan(eng):
            n = eng.value_load(plan[0:1, 0:1], min_val=0, max_val=SPILLS)
            which = [eng.value_load(plan[0:1, 1 + s:2 + s], min_val=0, max_val=EXPERTS - 1) for s in range(SPILLS)]
            return n, which

        SMALL = 16 * (1 + 7 * DEPTH + 6)

        block = ctx.enter_context(nc.Block())

        @block.sync
        def _(sp):
            def load(u):
                kind, src, k, kn, c0, n = stream[u]
                if u >= RAW:
                    sp.wait_ge(lo_ready, u - RAW + 1)
                sp.dma_start(unit(raw, u % RAW, kn, n),
                             src[k * P:(k + kn) * P, c0:c0 + n].rearrange("(k p) n -> p k n", p=P)).then_inc(raw_landed[u % RAW], 16)

            for tile, src in ((0, w["x"][0, 0:P, :]), (1, w["x"][0, P:2 * P, :]), (2, w["meta"])):
                sp.dma_start(h_tok[0:TILE_ROWS[tile], tile, :], src).then_inc(x_landed, 16)
            for u in range(NS):
                load(u)

            def load_expert(slot, u, src):
                sp.wait_ge(lo_ready, u - RAW + 1)
                sp.dma_start(raw[:, slot, :].rearrange("p (k n) -> p k n", k=src.shape[1]), src).then_inc(raw_landed[slot], 16)

            def gate_up(e, name, k, c0):
                a = w[name][0][bass.ds(e, 1), k * P:(k + 4) * P, bass.ds(c0, COLS)]
                return a.rearrange("e (k p) n -> p (e k) n", p=P)

            def down(e, r0):
                a = w["moe_w_down"][0][bass.ds(e, 1), bass.ds(r0, 2 * P), :]
                return a.rearrange("e (k p) n -> p (e k) n", p=P)

            def expert(g, e):
                u0 = NS + g * UPG
                at = NS % RAW
                for i, (name, k) in enumerate((("moe_w_gate", 0), ("moe_w_gate", 4), ("moe_w_up", 0), ("moe_w_up", 4))):
                    load_expert((at + i) % RAW, u0 + i, gate_up(e, name, k, 0))
                with sp.Fori(1, JCH) as j:
                    uj = u0 + (j * UPJ - 2)
                    for i, (name, k) in enumerate((("moe_w_gate", 0), ("moe_w_gate", 4), ("moe_w_up", 0), ("moe_w_up", 4))):
                        load_expert((at + 4 + i) % RAW, uj + i, gate_up(e, name, k, j * COLS))
                    for i in range(2):
                        load_expert((at + 8 + i) % RAW, uj + 4 + i, down(e, j * COLS - COLS + i * 2 * P))
                for i in range(2):
                    load_expert((at + 4 + i) % RAW, u0 + UPG - 2 + i, down(e, DFFE - COLS + i * 2 * P))

            with sp.Fori(0, EXPERTS) as g:
                expert(g, g)
            sp.wait_ge(plan_ready, 1)
            n_groups, spill = load_plan(sp)
            for s in range(SPILLS):
                with sp.If(n_groups > s):
                    expert(EXPERTS + s, spill[s])
                sp.end_ifs()
            for t in range(2):
                sp.wait_ge(normed_ready, 7 + t)
                sp.dma_start(out[0, t * P:(t + 1) * P, :], h_tok[:, t, :]).then_inc(stored, 16)
            sp.wait_ge(stored, 32)

        @block.gpsimd
        def _(pool):
            pool.wait_ge(x_landed, 48)
            pool.dma_start(tab[:, P:], consts[:, P:]).then_inc(small_landed, 16)
            for l in range(DEPTH):
                pool.dma_start(a2[:, l, :], w["gla_w_a2"][l]).then_inc(small_landed, 16)
            with nc.allow_non_contiguous_dma(reason="a few parameters, one per partition"):
                for l in range(DEPTH):
                    pool.dma_start(b_a[:, l, :], w["gla_b_a"][l].rearrange("(h p) -> p h", p=P)).then_inc(small_landed, 16)
                    pool.dma_start(gla_g[:, l, :], w["gla_norm_g"][l].rearrange("(k p) -> p k", p=P)).then_inc(small_landed, 16)
                    for s in range(2):
                        for i, name in (((0, "ln1"), (1, "ln2")) if l == 0 else ((2, "ln1"),)):
                            pool.dma_start(ln_gb[:, i, s, :], w[f"{name}_{'gb'[s]}"][l].rearrange("(k p) -> p k", p=P)).then_inc(small_landed, 16)
                        pool.dma_start(b_g[:, l, s, :], w["b_gate"][l, s].rearrange("(k p) -> p k", p=P)).then_inc(small_landed, 16)
                        pool.dma_start(ret_gb[:, l, s, :], w[("ret_norm_g", "ret_norm_b")[s]][l].rearrange("(k p) -> p k", p=P)).then_inc(small_landed, 16)

            loads = 0

            def load_rows(srcs):
                nonlocal loads
                if loads:
                    pool.wait_ge(rows_used, loads)
                for i, a in enumerate(srcs):
                    pool.dma_start(rows[:, i, 0:a.shape[0]], a.partition_broadcast(P)).then_inc(rows_landed, 16)
                loads += 1

            for l in range(DEPTH):
                pool.wait_ge(scores_out, l + 1)
                for tile, lo, hi in ((0, 0, CHUNK), (0, CHUNK, P), (1, 0, CHUNK), (1, CHUNK, P), (2, 0, META)):
                    n = hi - lo
                    a = sT[lo:hi, tile, 0:HEADS * n].rearrange("p (h i) -> p h i", h=HEADS)
                    pool.affine_select(out=a, in_=a, compare_op=ALU.is_ge, fill=0.0, base=0,
                                       pattern=[[0, HEADS], [1, n]], channel_multiplier=-1).then_inc(masked, 1)
                load_rows([w["ln1_g"][l], w["ln1_b"][l]])
                if l == 1:
                    full(pool, number[1, "wo1"])
                    pool.dma_start(wr[:, :, :], w["moe_w_router"][0].rearrange("(k p) e -> p k e", p=P)).then_inc(router_landed, 16)
                load_rows([w["ln2_g"][l], w["ln2_b"][l]])

        @block.tensor
        def _(pe):
            used = 0

            def mm3(dst, l_hi, l_lo, r_hi, r_lo, start, stop):
                nc.tensor.matmul(dst, l_lo, r_hi, start=start, stop=False)
                nc.tensor.matmul(dst, l_hi, r_lo, start=False, stop=False)
                return nc.tensor.matmul(dst, l_hi, r_hi, start=False, stop=stop)

            def begin(l, name):
                r = number[l, name]
                if r >= 2:
                    pe.wait_ge(act_done, r - 1)
                    pe.wait_ge(dve_done, r - 1)
                return bank(r)

            def after(l, name):
                r = number[l if (l, name) in number else 0, name]
                pe.wait_ge(act_done, r + 1)
                pe.wait_ge(dve_done, r + 1)

            def rowtile(x, k):
                return x[k // 4][:, k % 4, :] if type(x) is tuple else x[:, k, :]

            def next_unit():
                nonlocal used
                pe.wait_ge(lo_ready, used + 1)
                k, n = shape_of(used)
                s = used % HALVES
                used += 1
                return unit(w_hi, s, k, n), unit(w_lo, s, k, n), k, n

            def feature_major(l, name, x_hi_, x_lo_, cols, depth=KT, made_by=None, inside=None, bank_free=None):
                if bank_free:
                    pe.wait_ge(gated_ready, bank_free)
                    pt = bank(number[l, name])
                else:
                    pt = begin(l, name)
                for k0 in range(0, depth, 4):
                    if inside and inside[0] == k0:
                        inside[1]()
                    u_hi, u_lo, kn, n = next_unit()
                    if made_by:
                        after(l, made_by[k0 // 4])
                    for k in range(kn):
                        for m in range(n // P):
                            last = mm3(pt[:, m, cols], u_hi[:, k, m * P:(m + 1) * P], u_lo[:, k, m * P:(m + 1) * P],
                                       rowtile(x_hi_, k0 + k)[:, cols], rowtile(x_lo_, k0 + k)[:, cols],
                                       start=(k0 + k == 0), stop=(k0 + k == depth - 1))
                    last.then_inc(units_used, 1)

            def fill(last):
                last.then_inc(set_full, 1)

            def transposes(l, names, src, tiles, norm=None):
                for i, name in enumerate(names):
                    pt = begin(l, name)
                    if norm is not None:
                        pe.wait_ge(normed_ready, 2 * norm + i + 1)
                    for k in range(4):
                        for t in range(tiles):
                            c, n, f = TILE_COL[t], TILE_ROWS[t], (4 * i + k) * P
                            last = nc.tensor.transpose(pt[:, k, c:c + n], src[0:n, t, f:f + P], ident[0:n, 0:n])
                    fill(last)

            def back(l, names, sources, tiles):
                for (name, made_by), src in zip(names, sources):
                    after(l, made_by)
                    pt = begin(l, name)
                    for k in range(4):
                        for t in range(tiles):
                            c, n = TILE_COL[t], TILE_ROWS[t]
                            last = nc.tensor.transpose(pt[0:n, t, k * P:(k + 1) * P], src[:, k, c:c + n], ident)
                    fill(last)

            def key_tokens(l, name, made_by, keys):
                pt = begin(l, name)
                if made_by:
                    pe.wait_ge(made_by, 2 * (l + 1))
                else:
                    pe.wait_ge(gla_ready, l + 1)
                for t in range(3):
                    c, n = TILE_COL[t], TILE_ROWS[t]
                    for h in range(HEADS):
                        last = nc.tensor.transpose(pt[0:n, t, h * DK:(h + 1) * DK], keys(h)[:, c:c + n], ident)
                fill(last)

            def attention(l, b):
                pt = begin(l, f"{b}_sc")
                for tile, rws, cols in CHUNKS[b]:
                    n = rws.stop - rws.start
                    for h in range(HEADS):
                        last = nc.tensor.matmul(pt[rws, tile, h * n:(h + 1) * n], kT[:, h, cols], qT[:, h, cols], start=True, stop=True)
                fill(last)
                after(l, ("g_kt", "rvt1")[b == "r"])
                for c, (tile, rws, cols) in enumerate(CHUNKS[b]):
                    pt = begin(l, f"{b}_o{c}")
                    if c < len(CHUNKS[b]) - 1:
                        for h in range(HEADS):
                            last = nc.tensor.matmul(pt[:, h // 2, (h % 2) * DV:(h % 2 + 1) * DV], k_tok[rws, tile, h * DK:(h + 1) * DK],
                                                    v_tok[rws, tile, h * DV:(h + 1) * DV], start=True, stop=True)
                        last.then_inc(state_full, 1)
                    if c == 0:
                        if b == "g":
                            pe.wait_ge(masked, 5 * (l + 1))
                        else:
                            after(l, "r_sc")
                    out_of = [pt[rws, 2 + h // 2, (h % 2) * DV:(h % 2 + 1) * DV] for h in range(HEADS)]

                    def inside(h):
                        return nc.tensor.matmul(out_of[h], scores(b, tile, rws, h), v_tok[rws, tile, h * DV:(h + 1) * DV],
                                                start=True, stop=(c == 0))

                    def across(h):
                        return nc.tensor.matmul(out_of[h], qT[:, h, cols], state[:, c % 2, h * DV:(h + 1) * DV],
                                                start=False, stop=True)

                    if c:
                        inside(0)
                        inside(2)
                        pe.wait_ge(dve_done, number[l, f"{b}_o{c - 1}"] + 1)
                        across(0)
                        across(2)
                        inside(1)
                        across(1)
                        inside(3)
                        last = across(3)
                    elif l == 0:
                        for h in range(HEADS):
                            last = inside(h)
                    if c or l == 0:
                        fill(last)
                    else:
                        pe.wait_ge(state_full, state_n(l, b, c))
                        pe.sem_inc(set_full, 1)

            pe.wait_ge(ident_landed, 16)
            pe.wait_ge(x_landed, 48)
            transposes(0, ("ht0", "ht1"), h_tok, 3)
            for l in range(DEPTH):
                tiles = len(parts(l)) + 1
                cols = width(l)
                feature_major(l, "gk", hT_hi, hT_lo, slice(0, T), made_by=(("ht0", "ht1"), ("h2t0", "h2t1"))[l])
                feature_major(l, "gq", hT_hi, hT_lo, slice(0, T))
                feature_major(l, "ga", hT_hi, hT_lo, slice(0, T))
                after(l, "ga")
                pe.wait_ge(small_landed, SMALL)
                pt = begin(l, "z")
                for h in range(HEADS):
                    last = nc.tensor.matmul(pt[:, h, 0:T], a2[:, l, h * DK:(h + 1) * DK], gaT, start=True, stop=True)
                fill(last)
                feature_major(l, "gv0", hT_hi, hT_lo, slice(0, T))
                feature_major(l, "gv1", hT_hi, hT_lo, slice(0, T))
                back(l, (("gvt0", "gv0"),), (srT[:, 0:4, :],), 3)
                feature_major(l, "gta0", hT_hi, hT_lo, cols)
                back(l, (("gvt1", "gv1"),), (srT[:, 4:8, :],), 3)
                key_tokens(l, "g_kt", None, k_tail)
                attention(l, "g")
                for c in range(2):
                    feature_major(l, f"gr{c}", hT_hi, hT_lo, cols)
                feature_major(l, "gta1", hT_hi, hT_lo, cols)
                pe.wait_ge(o_ready, 2 * l + 1)
                transposes(l, ("g_t0", "g_t1"), o_tok, tiles)
                feature_major(l, "rq", hT_hi, hT_lo, cols, bank_free=8 * l + 2)
                feature_major(l, "rk", hT_hi, hT_lo, slice(0, T))
                for c in range(2):
                    feature_major(l, f"pa{c}", zT_hi, zT_lo, cols, made_by=("g_t0", "g_t1"))
                feature_major(l, "rv0", hT_hi, hT_lo, slice(0, T))
                key_tokens(l, "r_kt", rotated, lambda h: kT[:, h, :])
                feature_major(l, "rv1", hT_hi, hT_lo, slice(0, T))
                back(l, (("rvt0", "rv0"), ("rvt1", "rv1")), (srT[:, 0:4, :], srT[:, 4:8, :]), 3)
                attention(l, "r")
                for c in range(2):
                    feature_major(l, f"rg{c}", hT_hi, hT_lo, cols)
                feature_major(l, "gtb0", hT_hi, hT_lo, cols)
                pe.wait_ge(o_ready, 2 * l + 2)
                transposes(l, ("r_t0", "r_t1"), o_tok, tiles)
                feature_major(l, "gtb1", hT_hi, hT_lo, cols, bank_free=8 * l + 6)
                for c in range(2):
                    feature_major(l, f"pb{c}", zT_hi, zT_lo, cols, made_by=("r_t0", "r_t1"))
                feature_major(l, "wo0", m_hi, m_lo, cols, made_by=("pb0", "pb1"))
                feature_major(l, "wo1", m_hi, m_lo, cols, inside=(4, lambda: back(l, (("wot0", "wo0"),), (sgA[:, 0:4, :],), tiles)))
                back(l, (("wot1", "wo1"),), (sgA[:, 4:8, :],), tiles)
                transposes(l, ("h1t0", "h1t1"), h_tok, tiles, norm=2 * l)
                if l == 0:
                    for j in range(6):
                        feature_major(l, f"fg{j}", hT_hi, hT_lo, slice(0, T), made_by=None if j else ("h1t0", "h1t1"))
                        feature_major(l, f"fu{j}", hT_hi, hT_lo, slice(0, T))
                    feature_major(l, "fd0", aT_hi, aT_lo, slice(0, T), DFF // P, [f"fu{j}" for j in range(6)])
                    feature_major(l, "fd1", aT_hi, aT_lo, slice(0, T), DFF // P,
                                  inside=(16, lambda: back(l, (("fdt0", "fd0"),), (gT_s,), 3)))
                    back(l, (("fdt1", "fd1"),), (aT_f,), 3)
                    transposes(l, ("h2t0", "h2t1"), h_tok, 3, norm=1)

            pe.wait_ge(router_landed, 16)
            pt = begin(1, "route")
            for k in range(KT):
                if k % 4 == 0:
                    pe.wait_ge(dve_done, number[1, f"h1t{k // 4}"] + 1)
                for t in range(2):
                    c = TILE_COL[t]
                    last = nc.tensor.matmul(pt[:, t, 0:EXPERTS], ln_T[:, k, c:c + P], wr[:, k, :],
                                            start=(k == 0), stop=(k == KT - 1))
            fill(last)
            pt = begin(1, "rank")
            pe.wait_ge(sel_ready, 1)
            before, ones = table("before"), table("ones")
            nc.tensor.matmul(pt[:, 0, 0:EXPERTS], before, sel[:, 0, :], start=True, stop=True)
            nc.tensor.matmul(pt[:, 0, EXPERTS:2 * EXPERTS], before, sel[:, 1, :], start=True, stop=False)
            nc.tensor.matmul(pt[:, 0, EXPERTS:2 * EXPERTS], ones, sel[:, 0, :], start=False, stop=True)
            nc.tensor.matmul(pt[0:1, 1, 0:EXPERTS], ones[:, 0:1], sel[:, 0, :], start=True, stop=False)
            last = nc.tensor.matmul(pt[0:1, 1, 0:EXPERTS], ones[:, 0:1], sel[:, 1, :], start=False, stop=True)
            fill(last)
            pe.wait_ge(act_done, NSETS)
            pe.wait_ge(dve_done, NSETS)
            pe.wait_ge(x_lo_ready, 1)

            G_, U_ = ps[0][:, 0, :], ps[0][:, 1, :]
            TB, MISC = ps[0][:, 2, :], ps[0][:, 3, :]
            Y = ps[1][:, 0:2, :]
            X = ps[1][:, 2:4, :]

            def expert_unit(at, u):
                pe.wait_ge(lo_ready, u + 1)
                return w_hi[:, at % HALVES, :], w_lo[:, at % HALVES, :]

            def gate_or_up(dst, at, u):
                for i in range(2):
                    u_hi, u_lo = expert_unit(at + i, u + i)
                    for k in range(4):
                        last = mm3(dst, xg_hi[:, 4 * i + k, :], xg_lo[:, 4 * i + k, :],
                                   u_hi[:, k * COLS:(k + 1) * COLS], u_lo[:, k * COLS:(k + 1) * COLS],
                                   start=(i == 0 and k == 0), stop=(i == 1 and k == 3))
                    last.then_inc(units_used, 1)

            def turn(k):
                pe.wait_ge(hidden_ready, START + k + 1)
                pe.wait_ge(hidden_lo_ready, START + k)
                for i in range(4):
                    last = nc.tensor.transpose(TB[:, i * P:(i + 1) * P], a_sl[:, i * P:(i + 1) * P], ident)
                last.then_inc(hidden_turned, 1)

            def down(at, u, k, first, final):
                pe.wait_ge(hidden_lo_ready, START + k + 1)
                for i in range(2):
                    u_hi, u_lo = expert_unit(at + i, u + i)
                    for kk in range(2):
                        for q in range(2):
                            o = kk * D + q * COLS
                            last = nc.tensor.matmul(Y[:, q, :], ag_lo[:, 2 * i + kk, :], u_hi[:, o:o + COLS],
                                                    start=first and i == 0 and kk == 0, stop=False)
                            nc.tensor.matmul(Y[:, q, :], ag_hi[:, 2 * i + kk, :], u_lo[:, o:o + COLS], start=False, stop=False)
                            last = nc.tensor.matmul(Y[:, q, :], ag_hi[:, 2 * i + kk, :], u_hi[:, o:o + COLS],
                                                    start=False, stop=final and i == 1 and kk == 1)
                    last.then_inc(units_used, 1)

            def gather(n):
                pe.wait_ge(places_ready, START + n + 1)
                pe.wait_ge(scatter_added, START + 2 * n)
                for k in range(KT):
                    dst = X[:, k // 4, (k % 4) * P:(k % 4 + 1) * P]
                    for t in range(2):
                        nc.tensor.matmul(dst, x_lo[:, t, k * P:(k + 1) * P], S[:, t, :], start=(t == 0), stop=False)
                        last = nc.tensor.matmul(dst, x_hi[:, t, k * P:(k + 1) * P], S[:, t, :], start=False, stop=(t == 1))
                last.then_inc(gather_full, 1)

            def slots(g, e):
                pe.wait_ge(scatter_added, START + 2 * g + 2)
                for t in range(2):
                    nc.tensor.matmul(MISC[:, 0:1], S[:, t, :].bitcast(F32), comb[:, t, bass.ds(e, 1)], start=(t == 0), stop=(t == 1))
                for t in range(2):
                    last = nc.tensor.transpose(MISC[:, (t + 1) * P:(t + 2) * P], S[:, t, :].bitcast(F32), ident)
                last.then_inc(slots_full, 1)

            def scatter(n):
                pe.wait_ge(result_lo_ready, START + n + 1)
                pe.wait_ge(result_hi_ready, START + n + 1)
                pe.wait_ge(slots_ready, START + n)
                for t, dst in ((0, X), (1, ps[0][:, 2:4, :])):
                    for q in range(2):
                        nc.tensor.matmul(dst[:, q, :], ST[:, t, :], y_lo[:, q * COLS:(q + 1) * COLS], start=True, stop=False)
                        last = nc.tensor.matmul(dst[:, q, :], ST[:, t, :], y_hi[:, q * COLS:(q + 1) * COLS], start=False, stop=True)
                    last.then_inc(scatter_full, 1)

            def expert(g, e, overlapped, first_group=False):
                u0, k0, at = NS + g * UPG, g * JCH, NS
                n = g if overlapped else g + 1
                pe.wait_ge(gather_hi_ready, START + n + 1)
                pe.wait_ge(gather_lo_ready, START + n + 1)
                pe.wait_ge(silu_ready, START + k0)
                gate_or_up(G_, at, u0)
                if overlapped and not first_group:
                    scatter(g)
                pe.wait_ge(hidden_ready, START + k0)
                gate_or_up(U_, at + 2, u0 + 2)
                slots(g, e)

                def chunk(j, first):
                    uj, k = u0 + (j * UPJ - 2), k0 + j
                    pe.wait_ge(silu_ready, START + k)
                    gate_or_up(G_, at + 4, uj)
                    turn(k - 1)
                    gate_or_up(U_, at + 6, uj + 2)
                    if first:
                        pe.wait_ge(result_lo_ready, START + g + 1)
                    down(at + 8, uj + 4, k - 1, first, False)

                chunk(1, True)
                with pe.Fori(2, JCH) as j:
                    chunk(j, False)
                if overlapped:
                    gather(g + 1)
                turn(k0 + JCH - 1)
                down(at + 4, u0 + UPG - 2, k0 + JCH - 1, False, True)

            for first in (hidden_turned, gather_full, slots_full):
                pe.sem_inc(first, START)
            pe.sem_inc(scatter_full, START + 2)
            gather(0)
            expert(0, 0, True, first_group=True)
            with pe.Fori(1, EXPERTS) as g:
                expert(g, g, True)
            pe.wait_ge(plan_ready, 1)
            n_groups, spill = load_plan(pe)
            scatter(EXPERTS)
            for s in range(SPILLS):
                with pe.If(n_groups > s):
                    gather(EXPERTS + s + 1)
                    expert(EXPERTS + s, spill[s], False)
                    scatter(EXPERTS + s + 1)
                pe.end_ifs()

        @block.scalar
        def _(act):
            seq = 0

            def step(ins):
                nonlocal seq
                seq += 1
                ins.then_inc(act_seq, 1)

            def settle():
                act.wait_ge(act_seq, seq)

            def copy(dst, src, **kw):
                return nc.scalar.activation(dst, src, ACT.Copy, **kw)

            def hi_at(at, u, uses):
                act.wait_ge(raw_landed[at % RAW], uses * 16 + 16)
                act.wait_ge(units_used, u - HALVES + 1)
                copy(w_hi[:, at % HALVES, :], raw[:, at % RAW, :]).then_inc(hi_ready, 1)

            split = Splitter(act, hi_unit)

            def take(l, name, ahead=HALVES - 1):
                r = number[l, name]
                split.upto(ends[r] + ahead if ends[r] else r)
                full(act, r)
                return r, bank(r)

            def signed_off(r):
                if r:
                    act.wait_ge(act_done, r)
                act.sem_inc(act_done, 1)

            def skip(l, name):
                r, _ = take(l, name)
                signed_off(r)

            def to_transposed(l, names, dst):
                for i, name in enumerate(names):
                    r, pt = take(l, name)
                    copy(dst[:, 4 * i:4 * i + 4, width(l)], pt[:, :, width(l)]).then_inc(act_done, 1)

            def normed_to_transposed(l, names, norm):
                for c, name in enumerate(names):
                    r, pt = take(l, name)
                    for i in range(2):
                        k = 4 * c + 2 * i
                        act.wait_ge(norm_T, 4 * norm + 2 * c + i + 1)
                        copy(hT_hi[:, k:k + 2, width(l)], ln_T[:, k:k + 2, width(l)]).then_inc(norm_hi, 1)
                    signed_off(r)

            def std(count):
                act.wait_ge(var_ready, count)
                for rws, ts in parts_now:
                    ins = nc.scalar.activation(rstd[rws, ts, :], rstd[rws, ts, :], ACT.Sqrt)
                ins.then_inc(std_ready, 1)

            act.dma_start(ident, consts[:, 0:P]).then_inc(ident_landed, 16)
            stds = 0
            to_transposed(0, ("ht0", "ht1"), hT_hi)
            for l in range(DEPTH):
                parts_now = parts(l)
                r, pt = take(l, "gk")
                copy(kT[:, :, :], pt[:, :, 0:T]).then_inc(act_done, 1)
                r, pt = take(l, "gq")
                copy(qT[:, :, :], pt[:, :, 0:T], scale=DK ** -0.5).then_inc(act_done, 1)
                r, pt = take(l, "ga")
                copy(gaT, pt[0:RANK, 0, 0:T]).then_inc(act_done, 1)
                act.wait_ge(small_landed, SMALL)
                r, _ = take(l, "z")
                act.wait_ge(decay_input_ready, l + 1)
                step(nc.scalar.activation(fT[:, :, :], eT[:, :, :], ACT.Abs))
                settle()
                step(nc.scalar.activation(fT[:, :, :], fT[:, :, :], ACT.Exp, scale=-1.0))
                settle()
                nc.scalar.activation(fT[:, :, :], fT[:, :, :], ACT.Ln, bias=1.0).then_inc(softplus_ready, 1)
                signed_off(r)
                def value_features(name, c):
                    r, pt = take(l, name)
                    copy(srT[:, 4 * c:4 * c + 4, :], pt[:, :, 0:T]).then_inc(act_done, 1)

                def value_tokens(name, c):
                    r, pt = take(l, name)
                    for rws, ts in parts_all():
                        ins = copy(v_tok[rws, ts, c * COLS:(c + 1) * COLS], pt[rws, ts, :])
                    ins.then_inc(act_done, 1)

                value_features("gv0", 0)
                value_features("gv1", 1)
                value_tokens("gvt0", 0)
                act.wait_ge(log_decays_ready, l + 1)
                nc.scalar.activation(fT[:, :, :], bT[:, :, :], ACT.Exp, scale=1.0 / TAU)
                nc.scalar.activation(eT[:, :, :], bT[:, :, :], ACT.Exp, scale=-1.0 / TAU)
                for h in range(0, HEADS, 2):
                    nc.scalar.activation(o_tok[:, h // 2, 0:2 * T], o_tok[:, h // 2, 0:2 * T], ACT.Exp, scale=1.0 / TAU)
                nc.scalar.activation(decay[:, :, 0:1], bT[:, :, META - 1:META], ACT.Exp, scale=1.0 / TAU)
                nc.scalar.activation(decay[:, :, 1:], bT[:, :, META + CHUNK - 1:T:CHUNK], ACT.Exp, scale=1.0 / TAU).then_inc(decays_ready, 1)

                def merge_gate(q, c):
                    sg = (sgA, sgB)[q]
                    r, pt = take(l, f"gt{'ab'[q]}{c}")
                    for m in range(4):
                        ins = nc.scalar.activation(sg[:, 4 * c + m, width(l)], pt[:, m, width(l)], ACT.Sigmoid,
                                                   bias=b_g[:, l, q, 4 * c + m:4 * c + m + 1])
                    ins.then_inc(act_done, 1)

                merge_gate(0, 0)
                skip(l, "gvt1")
                for b, q in (("g", 0), ("r", 1)):
                    if b == "g":
                        r, pt = take(l, "g_kt")
                        for rws, ts in parts_all():
                            ins = copy(k_tok[rws, ts, :], pt[rws, ts, :])
                        ins.then_inc(act_done, 1)
                    else:
                        act.wait_ge(rotated, 2 * (l + 1))
                        value_features("rv0", 0)
                        skip(l, "r_kt")
                        value_features("rv1", 1)
                        value_tokens("rvt0", 0)
                        skip(l, "rvt1")
                    skip(l, f"{b}_sc")
                    for c, (tile, rws, _) in enumerate(CHUNKS[b]):
                        if c == 0 and l == 1:
                            skip(l, f"{b}_o{c}")
                            continue
                        r, pt = take(l, f"{b}_o{c}")
                        copy(o_tok[rws, tile, :].rearrange("p (b n) -> p b n", b=2), pt[rws, 2:4, :]).then_inc(act_done, 1)
                    stds += 1
                    split.upto(ends[number[l, f"{b}_o0"]] + HALVES)
                    std(stds)
                    for c in range(2):
                        r, pt = take(l, f"gr{c}" if b == "g" else f"rg{c}")
                        nc.scalar.activation(srT[:, 4 * c:4 * c + 4, width(l)], pt[:, :, width(l)], ACT.Silu).then_inc(act_done, 1)
                    merge_gate(q, 1 if b == "g" else 0)
                    for c in range(2):
                        r, pt = take(l, f"{b}_t{c}")
                        for i in range(2):
                            n = 4 * (2 * l + q) + 2 * c + i + 1
                            k = 4 * c + 2 * i
                            act.wait_ge(gated_ready, n)
                            copy(zT_hi[:, k:k + 2, width(l)], srT[:, k:k + 2, width(l)]).then_inc(gated_hi_ready, 1)
                        signed_off(r)
                    if b == "g":
                        dve_freed = number[l, "g_t1"] + 1
                        for i, name in enumerate(("rq", "rk")):
                            r, pt = take(l, name)
                            s = width(l) if i == 0 else slice(0, T)
                            hs = slice(4 * i, 4 * i + 4)
                            copy(raw_qk[:, hs, s], pt[:, :, s]).then_inc(act_done, 1)
                            act.wait_ge(act_done, r + 1)
                            act.wait_ge(dve_done, dve_freed)
                            for to, of in ((0, P // 2), (P // 2, 0)):
                                act.dma_start(srT[to:to + P // 2, hs, s], raw_qk[of:of + P // 2, hs, s]).then_inc(swap_landed[i], 16)
                        skip(l, "pa0")
                        skip(l, "pa1")
                    else:
                        merge_gate(1, 1)
                        for c in range(2):
                            r, _ = take(l, f"pb{c}")
                            act.wait_ge(merged_ready, 2 * l + c + 1)
                            copy(m_hi[c][:, :, width(l)], sgA[:, 4 * c:4 * c + 4, width(l)]).then_inc(act_done, 1)
                for c in range(2):
                    r, pt = take(l, f"wo{c}")
                    copy(sgA[:, 4 * c:4 * c + 4, width(l)], pt[:, :, width(l)]).then_inc(act_done, 1)
                skip(l, "wot0")
                skip(l, "wot1")
                stds += 1
                std(stds)
                if l == 1:
                    for i in range(HALVES):
                        hi_at(NS + i, NS + i, (NS + i) // RAW)
                    skip(l, "h1t0")
                    skip(l, "h1t1")
                else:
                    normed_to_transposed(l, ("h1t0", "h1t1"), 0)
                    for j in range(6):
                        n = 4 if j < 5 else 2
                        r, pt = take(l, f"fg{j}")
                        if j:
                            act.wait_ge(ffn_hidden_ready, j)
                        nc.scalar.activation(gT_s[:, 0:n, :], pt[:, 0:n, 0:T], ACT.Silu).then_inc(act_done, 1)
                        r, _ = take(l, f"fu{j}")
                        act.wait_ge(ffn_hidden_ready, j + 1)
                        copy(aT_hi[:, 4 * j:4 * j + n, :], aT_f[:, 0:n, :]).then_inc(ffn_hidden_hi_ready, 1)
                        signed_off(r)
                    for c, dst in enumerate((gT_s, aT_f)):
                        r, pt = take(l, f"fd{c}")
                        copy(dst[:, :, :], pt[:, :, 0:T]).then_inc(act_done, 1)
                    skip(l, "fdt0")
                    skip(l, "fdt1")
                    stds += 1
                    std(stds)
                    normed_to_transposed(0, ("h2t0", "h2t1"), 1)

            pt = bank(number[1, "route"])
            act.wait_ge(prob_ready, 1)
            for t in range(2):
                ins = nc.scalar.activation(prob[:, t, :], pt[:, t, 0:EXPERTS], ACT.Exp, bias=tiny[:, t, 0:1],
                                           accum_out=tiny[:, t, 1:2])
            ins.then_inc(act_done, 1)
            act.wait_ge(x_scaled, 1)
            copy(x_hi[:, :, :], h_tok[:, 0:2, :]).then_inc(x_hi_ready, 1)
            skip(1, "rank")

            def expert(g, e, overlapped, first_group=False):
                u0, k0 = NS + g * UPG, g * JCH
                base = g * (UPG // RAW)

                def hi(i, turns, u):
                    hi_at(NS + i, u, base + turns + (NS + i) // RAW)

                def turned(k, u):
                    act.wait_ge(hidden_turned, START + k + 1)
                    act.wait_ge(units_used, u)
                    copy(ag_hi[:, :, :], TB4).then_inc(hidden_hi_ready, 1)

                def silu(k, u):
                    act.wait_ge(units_used, u)
                    act.wait_ge(hidden_ready, START + k)
                    nc.scalar.activation(g_sl[:, :], ps[0][:, 0, :], ACT.Silu).then_inc(silu_ready, 1)

                def chunk(j, first):
                    uj, k, turns = u0 + (j * UPJ - 2), k0 + j, j - 1
                    for i in range(3):
                        hi(4 + i, turns, uj + i)
                    if first:
                        act.wait_ge(slots_full, START + g + 1)
                        act.wait_ge(result_lo_ready, START + g + 1)
                        copy(slot_w[:, :], ps[0][:, 3, 0:1])
                        copy(ST[:, :, :], ps[0][:, 3, P:3 * P].rearrange("p (t s) -> p t s", t=2)).then_inc(slots_ready, 1)
                    hi(7, turns, uj + 3)
                    turned(k - 1, uj)
                    silu(k, uj + 2)
                    for i in range(4, 6):
                        hi(4 + i, turns, uj + i)

                if not overlapped:
                    gathered(g + 1)
                if first_group:
                    hi(3, 0, u0 + 3)
                else:
                    for i in range(2):
                        hi(i, 0, u0 + i)
                    if overlapped:
                        result(g, u0)
                    for i in range(2, 4):
                        hi(i, 0, u0 + i)
                silu(k0, u0 + 2)
                chunk(1, True)
                with act.Fori(2, JCH) as j:
                    chunk(j, False)
                for i in range(2):
                    hi(4 + i, JCH - 1, u0 + UPG - 2 + i)
                turned(k0 + JCH - 1, u0 + UPG - 2)
                if overlapped:
                    gathered(g + 1)
                else:
                    result(g + 1, u0 + UPG)

            def gathered(n):
                act.wait_ge(gather_full, START + n + 1)
                copy(xg_hi[:, :, :], ps[1][:, 2:4, :].rearrange("p b (k s) -> p (b k) s", s=P)).then_inc(gather_hi_ready, 1)

            def result(n, u):
                act.wait_ge(units_used, u)
                act.wait_ge(slots_ready, START + n)
                act.wait_ge(scatter_full, START + 2 * n)
                nc.scalar.activation(y_hi[:, :].rearrange("p (b n) -> p b n", b=2), ps[1][:, 0:2, :], ACT.Copy,
                                     scale=slot_w[:, 0:1]).then_inc(result_hi_ready, 1)

            TB4 = ps[0][:, 2, :].rearrange("p (k s) -> p k s", s=P)
            for first in (silu_ready, gather_hi_ready, hidden_hi_ready, slots_ready):
                act.sem_inc(first, START)
            act.sem_inc(result_hi_ready, START + 1)
            gathered(0)
            expert(0, 0, True, first_group=True)
            with act.Fori(1, EXPERTS) as g:
                expert(g, g, True)
            act.wait_ge(plan_ready, 1)
            n_groups, spill = load_plan(act)
            result(EXPERTS, NS + EXPERTS * UPG)
            for s in range(SPILLS):
                with act.If(n_groups > s):
                    expert(EXPERTS + s, spill[s], False)
                act.end_ifs()
            act.wait_ge(var_ready, stds + 1)
            nc.scalar.activation(rstd[:, 0:2, :], rstd[:, 0:2, :], ACT.Sqrt).then_inc(std_ready, 1)

        @block.vector
        def _(dve):
            seq = 0

            def step(ins):
                nonlocal seq
                seq += 1
                ins.then_inc(dve_seq, 1)

            def settle():
                dve.wait_ge(dve_seq, seq)

            split = Splitter(dve, lo_unit)

            def take(l, name, ahead=HALVES - 1):
                r = number[l, name]
                split.upto(ends[r] + ahead if ends[r] else r)
                full(dve, r)
                return r, bank(r)

            def signed_off(r):
                if r:
                    dve.wait_ge(dve_done, r)
                dve.sem_inc(dve_done, 1)

            def skip(l, name, ahead=HALVES - 1):
                r, _ = take(l, name, ahead)
                signed_off(r)

            tt, ts_, stt = nc.vector.tensor_tensor, nc.vector.tensor_scalar, nc.vector.scalar_tensor_tensor

            def to_transposed(l, names, hi, lo):
                for i, name in enumerate(names):
                    r, pt = take(l, name)
                    dve.wait_ge(act_done, r + 1)
                    s = (slice(None), slice(4 * i, 4 * i + 4), width(l))
                    tt(lo[s], pt[:, :, width(l)], hi[s].bitcast(F32), ALU.subtract).then_inc(dve_done, 1)

            stds = 0

            def statistics(src, groups, size, where_parts, pieces=(0,), of=1):
                n = size // of
                for rws, ts in where_parts:
                    for t in range(ts.start, ts.stop):
                        for g in range(groups):
                            for q in pieces:
                                step(nc.vector.bn_stats(stats[rws, t, g + q, :], src[rws, t, g * size + q * n:g * size + (q + 1) * n]))

            def per_token(name, rws, ts):
                return table(name)[rws, :].unsqueeze(1).broadcast_to([rws.stop, ts.stop - ts.start, HEADS])

            def deviations(groups, pieces, eps, centred, where_parts, ahead=0, meanwhile=None, weight=False):
                nonlocal stds
                settle()
                for rws, ts in where_parts:
                    for t in range(ts.start, ts.stop):
                        for g in range(groups):
                            step(nc.vector.bn_aggr(mv[rws, t, g, :], stats[rws, t, g:g + pieces, :].rearrange("p a b -> p (a b)")))
                settle()
                for rws, ts in where_parts:
                    mean, var, r_ = mv[rws, ts, 0:groups, 0], mv[rws, ts, 0:groups, 1], rstd[rws, ts, 0:groups]
                    if not centred:
                        step(tt(r_, mean, mean, ALU.mult))
                        settle()
                        step(tt(r_, r_, var, ALU.add))
                        settle()
                        var = r_
                    if weight:
                        step(tt(r_, var, per_token("xi_squared", rws, ts), ALU.mult))
                        settle()
                        var = r_
                    step(ts_(r_, var, float(eps), None, ALU.add))
                settle()
                stds += 1
                for i, (rws, ts) in enumerate(where_parts):
                    ins = nc.vector.reciprocal(rstd[rws, ts, 0:groups], rstd[rws, ts, 0:groups])
                ins.then_inc(var_ready, 1)
                if ahead:
                    split.upto(ahead)
                if meanwhile:
                    meanwhile()
                dve.wait_ge(std_ready, stds)
                if weight:
                    for rws, ts in where_parts:
                        r_ = rstd[rws, ts, 0:groups]
                        step(tt(r_, r_, per_token("xi", rws, ts), ALU.mult))
                    settle()
                if centred and not meanwhile:
                    for rws, ts in where_parts:
                        step(stt(shift[rws, ts, 0:groups], mv[rws, ts, 0:groups, 0], -1.0, rstd[rws, ts, 0:groups], ALU.mult, ALU.mult))
                    settle()

            rows_n = 0

            def rows_ready():
                nonlocal rows_n
                rows_n += 1
                dve.wait_ge(rows_landed, 32 * rows_n)

            def layer_norm(where_parts, names):
                for c, name in enumerate(names):
                    r, pt = take(l, name, ahead=c)
                    for rws, ts in where_parts:
                        x_ = h_tok[rws, ts, c * COLS:(c + 1) * COLS]
                        ins = stt(x_, x_, float(ALPHA), pt[rws, ts, :], ALU.mult, ALU.add)
                    ins.then_inc(dve_done, 1)
                    dve.wait_ge(dve_done, r + 1)
                    statistics(h_tok, 1, D, where_parts, (c,), 2)
                deviations(1, 2, LN_EPS, True, where_parts)
                for c in range(2):
                    for rws, ts in where_parts:
                        for t in range(ts.start, ts.stop):
                            x_ = h_tok[rws, t, c * COLS:(c + 1) * COLS]
                            ins = ts_(x_, x_, rstd[rws, t, 0:1], shift[rws, t, 0:1], ALU.mult, ALU.add)
                    ins.then_inc(normed_ready, 1)

            def normed_to_transposed(l, names, norm):
                for c, name in enumerate(names):
                    r, pt = take(l, name, ahead=1)
                    for m in range(4):
                        k = 4 * c + m
                        ins = ts_(ln_T[:, k, width(l)], pt[:, m, width(l)], ln_gb[:, norm, 0, k:k + 1], ln_gb[:, norm, 1, k:k + 1],
                                  ALU.mult, ALU.add)
                        if m % 2:
                            ins.then_inc(norm_T, 1)
                    if l == 1:
                        dve.wait_ge(norm_T, 4 * norm + 2 * c + 2)
                        signed_off(r)
                        continue
                    for i in range(2):
                        dve.wait_ge(norm_T, 4 * norm + 2 * c + i + 1)
                        dve.wait_ge(norm_hi, 4 * norm + 2 * c + i + 1)
                        a = (slice(None), slice(4 * c + 2 * i, 4 * c + 2 * i + 2), width(l))
                        ins = tt(hT_lo[a], ln_T[a], hT_hi[a].bitcast(F32), ALU.subtract)
                    ins.then_inc(dve_done, 1)

            def gain_or_bias(i, where_parts):
                for rws, ts in where_parts:
                    for t in range(ts.start, ts.stop):
                        step(tt(h_tok[rws, t, :], h_tok[rws, t, :], rows[rws, i, :], (ALU.mult, ALU.add)[i]))

            def gain_and_bias(where_parts):
                rows_ready()
                for i in range(2):
                    gain_or_bias(i, where_parts)
                    settle()
                dve.sem_inc(rows_used, 1)

            def last_layer_norm():
                statistics(h_tok, 1, D, parts(1), (0, 1), 2)

                def centre():
                    for t in range(2):
                        step(ts_(shift[:, t, 0:1], mv[:, t, 0, 0:1], -1.0, None, ALU.mult))
                    settle()
                    rows_ready()
                    for t in range(2):
                        step(stt(h_tok[:, t, :], h_tok[:, t, :], shift[:, t, 0:1], rows[:, 0, :], ALU.add, ALU.mult))

                deviations(1, 2, LN_EPS, True, parts(1), meanwhile=centre)
                settle()
                for t in range(2):
                    stt(h_tok[:, t, :], h_tok[:, t, :], rstd[:, t, 0:1], rows[:, 1, :], ALU.mult, ALU.add).then_inc(normed_ready, 1)

            def value_tokens(l, name):
                r, pt = take(l, name)
                for rws, ts in parts_all():
                    ins = nc.vector.tensor_copy(v_tok[rws, ts, COLS:D], pt[rws, ts, :])
                ins.then_inc(dve_done, 1)

            def heads(a, n):
                return a.rearrange("p (h n) -> p h n", n=n)

            step(nc.vector.memset(rstd[:, :, :], 1.0))
            settle()
            to_transposed(0, ("ht0", "ht1"), hT_hi, hT_lo)
            for l in range(DEPTH):
                now = parts(l)
                skip(l, "gk")
                if l:
                    gain_and_bias(parts(0))
                skip(l, "gq")
                skip(l, "ga")
                r, pt = take(l, "z")
                dve.wait_ge(small_landed, SMALL)
                for h in range(HEADS):
                    ins = ts_(eT[:, h, :], pt[:, h, 0:T], b_a[:, l, h:h + 1], None, ALU.add)
                ins.then_inc(decay_input_ready, 1)
                signed_off(r)
                dve.wait_ge(decay_input_ready, l + 1)
                dve.wait_ge(softplus_ready, l + 1)
                step(stt(eT[:, :, :], eT[:, :, :], 0.0, fT[:, :, :], ALU.min, ALU.subtract))
                settle()
                for h in range(HEADS):
                    step(nc.vector.tensor_tensor_scan(bT[:, h, :], table("restart"), eT[:, h, :], 0.0, ALU.mult, ALU.add))
                settle()
                for h in range(0, HEADS, 2):
                    dst = o_tok[:, h // 2, 0:2 * T].rearrange("p (h t) -> p h t", h=2)
                    b2 = bT[:, h:h + 2, :]
                    step(tt(dst[:, :, 0:META], b2[:, :, META - 1:META].broadcast_to([P, 2, META]), b2[:, :, 0:META], ALU.subtract))
                    for hh in range(2):
                        d4 = dst[:, hh, META:].rearrange("p (c i) -> p c i", i=CHUNK)
                        s4 = b2[:, hh, META:].rearrange("p (c i) -> p c i", i=CHUNK)
                        ins = tt(d4, s4[:, :, CHUNK - 1:CHUNK].broadcast_to([P, NCHUNK - 1, CHUNK]), s4, ALU.subtract)
                        if h + hh < HEADS - 1:
                            step(ins)
                ins.then_inc(log_decays_ready, 1)
                skip(l, "gv0")
                skip(l, "gv1")
                skip(l, "gvt0")
                dve.wait_ge(decays_ready, l + 1)
                step(tt(qT[:, :, :], qT[:, :, :], fT[:, :, :], ALU.mult))
                for h in range(HEADS):
                    step(tt(k_tail(h), kT[:, h, :], k_tail(h), ALU.mult))
                settle()
                tt(kT[:, :, :], kT[:, :, :], eT[:, :, :], ALU.mult).then_inc(gla_ready, 1)
                skip(l, "gta0")
                value_tokens(l, "gvt1")
                skip(l, "g_kt")
                for b, q in (("g", 0), ("r", 1)):
                    if b == "r":
                        r, pt = take(l, "r_kt")
                        for t in range(3):
                            rws = slice(0, TILE_ROWS[t])
                            f = table("zeta")[rws, t * HEADS:(t + 1) * HEADS].unsqueeze(2).broadcast_to([rws.stop, HEADS, DK])
                            ins = tt(heads(k_tok[rws, t, :], DK), heads(pt[rws, t, :], DK), f, ALU.mult)
                        ins.then_inc(dve_done, 1)
                        skip(l, "rv1")
                        skip(l, "rvt0")
                        value_tokens(l, "rvt1")
                    r, pt = take(l, f"{b}_sc")
                    for tile, n in ((0, CHUNK), (1, CHUNK), (2, META)) if b == "g" else ((0, P), (1, P), (2, META)):
                        rws = slice(0, TILE_ROWS[tile])
                        if b == "g":
                            ins = nc.vector.tensor_copy(sT[rws, tile, 0:HEADS * n], pt[rws, tile, 0:HEADS * n])
                        else:
                            ins = tt(heads(scores(b, tile, rws), n), heads(pt[rws, tile, 0:HEADS * n], n),
                                     heads(table("mask"), P)[rws, :, 0:n], ALU.mult)
                    if b == "g":
                        ins.then_inc(scores_out, 1)
                        dve.wait_ge(scores_out, l + 1)
                        signed_off(r)
                    else:
                        ins.then_inc(dve_done, 1)
                    for c in range(len(CHUNKS[b])):
                        if c == len(CHUNKS[b]) - 1:
                            skip(l, f"{b}_o{c}")
                            continue
                        r = number[l, f"{b}_o{c}"]
                        pt = bank(r)
                        split.upto(ends[r] + HALVES - 1)
                        dve.wait_ge(state_full, state_n(l, b, c))
                        if c:
                            dve.wait_ge(dve_done, r)
                        for h in range(HEADS):
                            new = state[:, (c + 1) % 2, h * DV:(h + 1) * DV]
                            add = pt[:, h // 2, (h % 2) * DV:(h % 2 + 1) * DV]
                            if c == 0:
                                ins = nc.vector.tensor_copy(new, add)
                            else:
                                by = decay[:, h, c:c + 1] if b == "g" else float((1.0 - 2.0 ** (-5.0 - h)) ** P)
                                ins = stt(new, state[:, c % 2, h * DV:(h + 1) * DV], by, add, ALU.mult, ALU.add)
                        ins.then_inc(dve_done, 1)
                    dve.wait_ge(act_done, number[l, f"{b}_o{len(CHUNKS[b]) - 1}"] + 1)
                    statistics(o_tok, HEADS, DV, now)
                    deviations(HEADS, 1, LN_EPS if b == "g" else GN_EPS, b == "r", now,
                               ends[number[l, f"{b}_o0"]] + HALVES + 1, weight=(b == "r"))
                    for rws, ts in now:
                        for t in range(ts.start, ts.stop):
                            for h in range(HEADS):
                                o = o_tok[rws, t, h * DV:(h + 1) * DV]
                                if b == "g":
                                    step(ts_(o, o, rstd[rws, t, h:h + 1], None, ALU.mult))
                                else:
                                    step(ts_(o, o, rstd[rws, t, h:h + 1], shift[rws, t, h:h + 1], ALU.mult, ALU.add))
                    settle()
                    dve.sem_inc(o_ready, 1)
                    skip(l, f"{b[0]}r0" if b == "g" else "rg0")
                    skip(l, f"{b[0]}r1" if b == "g" else "rg1")
                    skip(l, "gta1" if b == "g" else "gtb0")
                    for c in range(2):
                        r, pt = take(l, f"{b}_t{c}")
                        dve.wait_ge(act_done, number[l, f"gr{c}" if b == "g" else f"rg{c}"] + 1)
                        z = srT[:, 4 * c:4 * c + 4, width(l)]
                        for m in range(4):
                            k = 4 * c + m
                            if b == "g":
                                ins = stt(z[:, m, :], pt[:, m, width(l)], gla_g[:, l, m % 2:m % 2 + 1], z[:, m, :], ALU.mult, ALU.mult)
                                if m % 2:
                                    ins.then_inc(gated_ready, 1)
                            else:
                                step(ts_(pt[:, m, width(l)], pt[:, m, width(l)], ret_gb[:, l, 0, k:k + 1], ret_gb[:, l, 1, k:k + 1],
                                         ALU.mult, ALU.add))
                        if b == "r":
                            settle()
                            for m in (0, 2):
                                tt(z[:, m:m + 2, :], pt[:, m:m + 2, width(l)], z[:, m:m + 2, :], ALU.mult).then_inc(gated_ready, 1)
                        for i in range(2):
                            n = 4 * (2 * l + q) + 2 * c + i + 1
                            dve.wait_ge(gated_ready, n)
                            dve.wait_ge(gated_hi_ready, n)
                            lo_s = (slice(None), slice(4 * c + 2 * i, 4 * c + 2 * i + 2), width(l))
                            ins = tt(zT_lo[lo_s], srT[lo_s], zT_hi[lo_s].bitcast(F32), ALU.subtract)
                        ins.then_inc(dve_done, 1)
                    if b == "g":
                        skip(l, "rq")
                        skip(l, "rk")
                        for i, (dst, s) in enumerate(((qT, width(l)), (kT, slice(0, T)))):
                            dve.wait_ge(swap_landed[i], 32 * (l + 1))
                            n = s.stop - s.start
                            a, x_ = raw_qk[:, 4 * i:4 * i + 4, s], srT[:, 4 * i:4 * i + 4, s]
                            step(tt(a, a, table("cos")[:, s].unsqueeze(1).broadcast_to([P, HEADS, n]), ALU.mult))
                            step(tt(x_, x_, table("sin")[:, s].unsqueeze(1).broadcast_to([P, HEADS, n]), ALU.mult))
                            r, pt = take(l, f"pa{i}")
                            m = (slice(None), slice(4 * i, 4 * i + 4), width(l))
                            tt(sgA[m], pt[:, :, width(l)], sgA[m], ALU.mult).then_inc(dve_done, 1)
                        settle()
                        for i, (dst, s) in enumerate(((qT, width(l)), (kT, slice(0, T)))):
                            tt(dst[:, :, s], raw_qk[:, 4 * i:4 * i + 4, s], srT[:, 4 * i:4 * i + 4, s], ALU.add).then_inc(rotated, 1)
                        dve.wait_ge(rotated, 2 * (l + 1))
                        skip(l, "rv0")
                    else:
                        skip(l, "gtb1")
                        for c in range(2):
                            r, pt = take(l, f"pb{c}")
                            s = (slice(None), slice(4 * c, 4 * c + 4), width(l))
                            dve.wait_ge(act_done, number[l, f"gtb{c}"] + 1)
                            step(tt(sgB[s], pt[:, :, width(l)], sgB[s], ALU.mult))
                            settle()
                            tt(sgA[s], sgA[s], sgB[s], ALU.add).then_inc(merged_ready, 1)
                            dve.wait_ge(merged_ready, 2 * l + c + 1)
                            dve.wait_ge(act_done, r + 1)
                            tt(m_lo[c][:, :, width(l)], sgA[s], m_hi[c][:, :, width(l)].bitcast(F32), ALU.subtract).then_inc(dve_done, 1)

                skip(l, "wo0")
                signed_off(number[l, "wo1"])
                layer_norm(now, ("wot0", "wot1"))
                normed_to_transposed(l, ("h1t0", "h1t1"), 2 * l)
                if l == 0:
                    for j in range(6):
                        n = 4 if j < 5 else 2
                        skip(l, f"fg{j}")
                        if j == 0:
                            gain_and_bias(now)
                        r, pt = take(l, f"fu{j}")
                        dve.wait_ge(act_done, r)
                        if j:
                            dve.wait_ge(ffn_hidden_hi_ready, j)
                        tt(aT_f[:, 0:n, :], pt[:, 0:n, 0:T], gT_s[:, 0:n, :], ALU.mult).then_inc(ffn_hidden_ready, 1)
                        dve.wait_ge(ffn_hidden_hi_ready, j + 1)
                        dve.wait_ge(ffn_hidden_ready, j + 1)
                        tt(aT_lo[:, 4 * j:4 * j + n, :], aT_f[:, 0:n, :], aT_hi[:, 4 * j:4 * j + n, :].bitcast(F32),
                           ALU.subtract).then_inc(dve_done, 1)
                    skip(l, "fd0")
                    signed_off(number[l, "fd1"])
                    layer_norm(now, ("fdt0", "fdt1"))
                    normed_to_transposed(0, ("h2t0", "h2t1"), 1)

            def lo(i, u):
                at = NS + i
                dve.wait_ge(hi_ready, u + 1)
                dve.wait_ge(units_used, u - HALVES + 1)
                tt(w_lo[:, at % HALVES, :], raw[:, at % RAW, :], w_hi[:, at % HALVES, :].bitcast(F32),
                   ALU.subtract).then_inc(lo_ready, 1)

            rows_ready()
            gain_or_bias(0, parts(1))
            lo(0, NS)
            r, pt = take(1, "route")
            for t in range(2):
                step(nc.vector.tensor_reduce(tiny[:, t, 0:1], pt[:, t, 0:EXPERTS], AX.X, ALU.max))
            settle()
            ts_(tiny[:, :, 0:1], tiny[:, :, 0:1], -1.0, None, ALU.mult).then_inc(prob_ready, 1)
            gain_or_bias(1, parts(1))
            settle()
            dve.sem_inc(x_scaled, 1)
            dve.sem_inc(rows_used, 1)
            dve.wait_ge(act_done, r + 1)
            step(nc.vector.reciprocal(tiny[:, :, 1:2], tiny[:, :, 1:2]))
            settle()
            for t in range(2):
                step(ts_(prob[:, t, :], prob[:, t, :], tiny[:, t, 1:2], None, ALU.mult))
            settle()
            for t in range(2):
                step(nc.vector.max(top[:, t, :], prob[:, t, :]))
            settle()
            for t in range(2):
                step(nc.vector.max_index(top_at[:, t, :], top[:, t, :], prob[:, t, :]))
            step(tt(tiny[:, :, 2:3], top[:, :, 0:1], top[:, :, 1:2], ALU.add))
            settle()
            step(nc.vector.tensor_copy(top_f[:, :, :], top_at[:, :, 0:2]))
            step(nc.vector.reciprocal(tiny[:, :, 2:3], tiny[:, :, 2:3]))
            settle()
            for t in range(2):
                for i in range(2):
                    step(ts_(hit[:, t, i, :], table("iota")[:, 0:EXPERTS], top_f[:, t, i:i + 1], None, ALU.is_equal))
                step(ts_(top[:, t, 0:2], top[:, t, 0:2], tiny[:, t, 2:3], None, ALU.mult))
            settle()
            step(tt(sel[:, :, :], hit[:, :, 0, :], hit[:, :, 1, :], ALU.add))
            for t in range(2):
                step(ts_(comb[:, t, :], hit[:, t, 0, :], top[:, t, 0:1], None, ALU.mult))
            settle()
            for t in range(2):
                step(stt(comb[:, t, :], hit[:, t, 1, :], top[:, t, 1:2], comb[:, t, :], ALU.mult, ALU.add))
            settle()
            dve.sem_inc(sel_ready, 1)
            dve.sem_inc(dve_done, 1)
            dve.wait_ge(x_hi_ready, 1)
            tt(x_lo[:, :, :], h_tok[:, 0:2, :], x_hi[:, :, :].bitcast(F32), ALU.subtract).then_inc(x_lo_ready, 1)
            r, pt = take(1, "rank")
            big = float(4 * P)
            step(nc.vector.memset(rank[:, :, EXPERTS:], big))
            step(ts_(rank[:, :, 0:EXPERTS], sel[:, :, :], -big, big, ALU.mult, ALU.add))
            settle()
            step(tt(rank[:, :, 0:EXPERTS], rank[:, :, 0:EXPERTS], pt[:, 0, 0:2 * EXPERTS].rearrange("p (t e) -> p t e", t=2), ALU.add))
            E = EXPERTS
            over, excl, num, hits = (plan_f[0:1, i * E:(i + 1) * E] for i in range(4))
            step(ts_(over, pt[0:1, 1, 0:E], float(P), None, ALU.is_gt))
            settle()
            dve.sem_inc(dve_done, 1)
            iota, ones = table("iota"), table("ones")

            def expert(g, e, overlapped, first_group=False):
                u0, k0 = NS + g * UPG, g * JCH

                def turned(k):
                    dve.wait_ge(hidden_hi_ready, START + k + 1)
                    tt(ag_lo[:, :, :], ps[0][:, 2, :].rearrange("p (k s) -> p k s", s=P), ag_hi[:, :, :].bitcast(F32),
                       ALU.subtract).then_inc(hidden_lo_ready, 1)

                def gated(k, u):
                    dve.wait_ge(units_used, u)
                    dve.wait_ge(silu_ready, START + k + 1)
                    dve.wait_ge(hidden_turned, START + k)
                    tt(a_sl[:, :], ps[0][:, 1, :], g_sl[:, :], ALU.mult).then_inc(hidden_ready, 1)

                def chunk(j, start):
                    uj, k = u0 + (j * UPJ - 2), k0 + j
                    for i in range(start, 4):
                        lo(4 + i, uj + i)
                    turned(k - 1)
                    for i in range(4, 6):
                        lo(4 + i, uj + i)
                    gated(k, uj + 4)

                if not overlapped:
                    places(g + 1, g, e, P)
                    gathered(g + 1)
                before = overlapped and not first_group
                if not first_group:
                    for i in range(2):
                        lo(i, u0 + i)
                    if before:
                        result(g)
                    lo(2, u0 + 2)
                lo(3, u0 + 3)
                if before:
                    add(g, 0)
                lo(4, u0 + 4)
                if before:
                    add(g, 1)
                lo(5, u0 + 5)
                gated(k0, u0 + 4)
                chunk(1, 2)
                with dve.Fori(2, JCH) as j:
                    chunk(j, 0)
                if overlapped:
                    places(g + 1, g + 1, e + 1, 0)
                for i in range(2):
                    lo(4 + i, u0 + UPG - 2 + i)
                turned(k0 + JCH - 1)
                if overlapped:
                    gathered(g + 1)
                else:
                    result(g + 1)
                    add(g + 1, 0)
                    add(g + 1, 1)

            def places(n, slots_read, e, first_slot):
                dve.wait_ge(gather_full, START + n)
                dve.wait_ge(slots_full, START + slots_read)
                for t in range(2):
                    ins = ts_(S[:, t, :], iota[:, first_slot:first_slot + P], rank[:, t, bass.ds(e, 1)], None, ALU.is_equal)
                ins.then_inc(places_ready, 1)

            def gathered(n):
                dve.wait_ge(gather_hi_ready, START + n + 1)
                tt(xg_lo[:, :, :], ps[1][:, 2:4, :].rearrange("p b (k s) -> p (b k) s", s=P), xg_hi[:, :, :].bitcast(F32),
                   ALU.subtract).then_inc(gather_lo_ready, 1)

            def result(n):
                dve.wait_ge(result_hi_ready, START + n + 1)
                stt(y_lo[:, :].rearrange("p (b n) -> p b n", b=2), ps[1][:, 0:2, :], slot_w[:, 0:1],
                    y_hi[:, :].bitcast(F32).rearrange("p (b n) -> p b n", b=2), ALU.mult, ALU.subtract).then_inc(result_lo_ready, 1)

            def add(n, t):
                dve.wait_ge(scatter_full, START + 2 * n + t + 1)
                dve.wait_ge(scatter_added, START + 2 * n + t)
                h = h_tok[:, t, :].rearrange("p (b n) -> p b n", b=2)
                src = (ps[1][:, 2:4, :], ps[0][:, 2:4, :])[t]
                tt(h, h, src, ALU.add).then_inc(scatter_added, 1)

            for first in (places_ready, gather_lo_ready, hidden_ready, hidden_lo_ready):
                dve.sem_inc(first, START)
            dve.sem_inc(result_lo_ready, START + 1)
            dve.sem_inc(scatter_added, START + 2)
            places(0, 0, 0, 0)
            step(nc.vector.tensor_tensor_scan(excl, ones[0:1, 0:E], over, 0.0, ALU.mult, ALU.add))
            step(tt(num, over, iota[0:1, 0:E], ALU.mult))
            settle()
            for s in range(SPILLS):
                step(stt(hits, excl, float(s + 1), num, ALU.is_equal, ALU.mult))
                settle()
                step(nc.vector.tensor_reduce(plan_f[0:1, 4 * E + 1 + s:4 * E + 2 + s], hits, AX.X, ALU.add))
                settle()
            step(nc.vector.tensor_reduce(plan_f[0:1, 4 * E:4 * E + 1], over, AX.X, ALU.add))
            settle()
            nc.vector.tensor_copy(plan[:, :], plan_f[0:1, 4 * E:4 * E + 4]).then_inc(plan_ready, 1)
            for i in range(1, HALVES):
                lo(i, NS + i)
            gathered(0)
            step(ts_(h_tok[:, 0:2, :], h_tok[:, 0:2, :], float(ALPHA), None, ALU.mult))
            settle()
            expert(0, 0, True, first_group=True)
            with dve.Fori(1, EXPERTS) as g:
                expert(g, g, True)

            n_groups, spill = load_plan(dve)
            result(EXPERTS)
            add(EXPERTS, 0)
            add(EXPERTS, 1)
            for s in range(SPILLS):
                with dve.If(n_groups > s):
                    expert(EXPERTS + s, spill[s], False)
                dve.end_ifs()
            dve.wait_ge(scatter_added, START + n_groups * 2 + 2 * EXPERTS + 2)
            last_layer_norm()


NAMES = ["x", "meta", "w_in", "b_gate", "gla_w_a2", "gla_b_a", "gla_norm_g", "ret_norm_g", "ret_norm_b", "w_pa", "w_pb",
         "w_o", "ln1_g", "ln1_b", "ffn_w_gate", "ffn_w_up", "ffn_w_down", "moe_w_router", "moe_w_gate", "moe_w_up",
         "moe_w_down", "ln2_g", "ln2_b"]


def kernel(**inputs):
    import numpy as _np
    import concourse.bacc as _bacc
    from concourse import mybir as _mybir
    from concourse.bass_utils import run_bass_kernel_spmd as _run

    nc = _bacc.Bacc("TRN2", target_bir_lowering=False, num_devices=1, dynamic_dma_scratch_size=4096)
    arrays, w = {}, {}
    for name in NAMES:
        a = _np.ascontiguousarray(inputs[name])
        arrays[f"in_{name}"] = a
        w[name] = nc.dram_tensor(f"in_{name}", a.shape, _mybir.dt.from_np(a.dtype), kind="ExternalInput").ap()
    tables, where = host_constants()
    arrays["in_tables"] = tables
    consts = nc.dram_tensor("in_tables", tables.shape, _mybir.dt.float32, kind="ExternalInput").ap()
    out = nc.dram_tensor("out", (1, SEQ, D), _mybir.dt.float32, kind="ExternalOutput").ap()
    trunk(nc, w, consts, where, out)
    r = _run(nc, [arrays], core_ids=[0])
    return r.results[0]["out"]
```
